# Optimizing a Trainium2 kernel written in Bass

```python
import math
import jax
import jax.numpy as jnp
from jax import lax
import numpy as np
import jax, jax.numpy as jnp

D_MODEL = 1024
BATCH = 1
SEQ = 512
DEPTH = 1

D_INNER = 2 * D_MODEL
D_ATTN = D_INNER // 2
D_SSM = D_INNER - D_ATTN
SB_HEAD_DIM = 64
SB_HEADS = D_ATTN // SB_HEAD_DIM
SSM_HEAD_DIM = 64
SSM_HEADS = D_SSM // SSM_HEAD_DIM
SSM_GROUPS = 2
SSM_STATE = 128
CONV_WIDTH = 4
SSD_CHUNK = 128
Q_BLOCK = 128
NORM_EPS = 1e-6
D_XBC = D_SSM + 2 * SSM_GROUPS * SSM_STATE
D_PROJ = 4 * D_ATTN + D_XBC + SSM_HEADS + D_SSM
DT_MIN = 1e-3
DT_MAX = 1e-1


def rms_norm(x, gain):
    xf = x.astype(jnp.float32)
    y = xf * lax.rsqrt(jnp.mean(xf * xf, axis=-1, keepdims=True) + NORM_EPS)
    return (y * gain.astype(jnp.float32)).astype(x.dtype)

def stick_breaking_attention(q, k, v):
    seq = q.shape[1]
    scale = q.shape[-1] ** -0.5
    outs = []
    for blk in range(seq // Q_BLOCK):
        start = blk * Q_BLOCK
        end = start + Q_BLOCK
        z = jnp.einsum("bqhd,bkhd->bhqk", q[:, start:end], k[:, :end]).astype(jnp.float32) * scale
        t_idx = start + jnp.arange(Q_BLOCK)[:, None]
        s_idx = jnp.arange(end)[None, :]
        mask = s_idx < t_idx
        log_beta = jax.nn.log_sigmoid(z)
        log_one_minus = jnp.where(mask, jax.nn.log_sigmoid(-z), 0.0)
        tail = lax.cumsum(log_one_minus, axis=3, reverse=True) - log_one_minus
        weights = jnp.exp(jnp.where(mask, log_beta + tail, -jnp.inf))
        outs.append(jnp.einsum("bhqk,bkhd->bqhd", weights.astype(v.dtype), v[:, :end]))
    return jnp.concatenate(outs, axis=1)

def causal_depthwise_conv(u, w, b):
    ch = u.shape[-1]
    y = lax.conv_general_dilated(
        u, w[:, None, :].astype(u.dtype), window_strides=(1,),
        padding=[(CONV_WIDTH - 1, 0)], dimension_numbers=("NWC", "WIO", "NWC"),
        feature_group_count=ch)
    return y + b.astype(u.dtype)

def ssd_scan(xs, dt, a, b_in, c_in, d_skip):
    bsz, seq, nh, hp = xs.shape
    ng, ns = b_in.shape[-2:]
    hpg = nh // ng
    nc = seq // SSD_CHUNK
    cl = SSD_CHUNK
    xf = xs.astype(jnp.float32)
    xdt = (xf * dt[..., None]).reshape(bsz, nc, cl, ng, hpg, hp)
    bc = b_in.astype(jnp.float32).reshape(bsz, nc, cl, ng, ns)
    cc = c_in.astype(jnp.float32).reshape(bsz, nc, cl, ng, ns)
    log_decay = (dt * a).reshape(bsz, nc, cl, ng, hpg).transpose(0, 1, 3, 4, 2)
    a_cum = jnp.cumsum(log_decay, axis=-1)
    causal = jnp.tril(jnp.ones((cl, cl), dtype=bool))
    seg = a_cum[..., :, None] - a_cum[..., None, :]
    decay = jnp.exp(jnp.where(causal, seg, -jnp.inf))
    cb = jnp.einsum("bclgn,bcsgn->bcgls", cc, bc)
    y_diag = jnp.einsum("bcgrls,bcsgrp->bclgrp", cb[:, :, :, None] * decay, xdt)
    decay_to_end = jnp.exp(a_cum[..., -1:] - a_cum)
    chunk_states = jnp.einsum("bclgn,bcgrl,bclgrp->bcgrpn", bc, decay_to_end, xdt)
    chunk_decay = jnp.exp(a_cum[..., -1])

    def step(h, inp):
        st, dec = inp
        return h * dec[..., None, None] + st, h

    h0 = jnp.zeros((bsz, ng, hpg, hp, ns), jnp.float32)
    _, prev = lax.scan(step, h0, (jnp.moveaxis(chunk_states, 1, 0), jnp.moveaxis(chunk_decay, 1, 0)))
    prev = jnp.moveaxis(prev, 0, 1)
    y_off = jnp.einsum("bclgn,bcgrpn,bcgrl->bclgrp", cc, prev, jnp.exp(a_cum))
    y = (y_diag + y_off).reshape(bsz, seq, nh, hp)
    return y + xf * d_skip.astype(jnp.float32)[:, None]

def first_inputs(seed: int = 0) -> dict:
    key = jax.random.key(seed)
    ks = jax.random.split(key, 16)
    f = jnp.float32
    nrm = jax.random.normal
    x = nrm(ks[0], (BATCH, SEQ, D_MODEL), f)
    c = nrm(ks[1], (BATCH, D_MODEL), f)
    w_ada = nrm(ks[2], (DEPTH, D_MODEL, 3 * D_MODEL), f) * D_MODEL ** -0.5
    b_ada = 0.02 * nrm(ks[3], (DEPTH, 3 * D_MODEL), f)
    norm_in_gain = 1.0 + 0.1 * nrm(ks[4], (DEPTH, D_MODEL), f)
    w_in = nrm(ks[5], (DEPTH, D_MODEL, D_PROJ), f) * D_MODEL ** -0.5
    conv_w = nrm(ks[6], (DEPTH, CONV_WIDTH, D_XBC), f) * CONV_WIDTH ** -0.5
    conv_b = 0.02 * nrm(ks[7], (DEPTH, D_XBC), f)
    dt0 = jnp.exp(jax.random.uniform(ks[8], (DEPTH, SSM_HEADS), f, math.log(DT_MIN), math.log(DT_MAX)))
    dt_bias = dt0 + jnp.log(-jnp.expm1(-dt0))
    a_log = jnp.log(jax.random.uniform(ks[9], (DEPTH, SSM_HEADS), f, 1.0, 16.0))
    d_skip = 1.0 + 0.1 * nrm(ks[10], (DEPTH, SSM_HEADS), f)
    sb_norm_gain = 1.0 + 0.1 * nrm(ks[11], (DEPTH, D_ATTN), f)
    ssm_norm_gain = 1.0 + 0.1 * nrm(ks[12], (DEPTH, D_SSM), f)
    w_out = nrm(ks[13], (DEPTH, D_INNER, D_MODEL), f) * D_INNER ** -0.5
    norm_f_gain = 1.0 + 0.1 * nrm(ks[14], (D_MODEL,), f)
    return {"x": x, "c": c, "w_ada": w_ada, "b_ada": b_ada, "norm_in_gain": norm_in_gain,
            "w_in": w_in, "conv_w": conv_w, "conv_b": conv_b, "dt_bias": dt_bias,
            "a_log": a_log, "d_skip": d_skip, "sb_norm_gain": sb_norm_gain,
            "ssm_norm_gain": ssm_norm_gain, "w_out": w_out, "norm_f_gain": norm_f_gain}

def first_block(x, c, w_ada, b_ada, norm_in_gain, w_in, conv_w, conv_b, dt_bias, a_log,
              d_skip, sb_norm_gain, ssm_norm_gain, w_out, norm_f_gain):
    bsz, seq, _ = x.shape
    splits = [D_ATTN, 2 * D_ATTN, 3 * D_ATTN, 4 * D_ATTN, 4 * D_ATTN + D_XBC,
              4 * D_ATTN + D_XBC + SSM_HEADS]
    c_act = jax.nn.silu(c)
    for layer in range(DEPTH):
        mod = c_act @ w_ada[layer] + b_ada[layer]
        shift, scale, gate = jnp.split(mod, 3, axis=-1)
        h = rms_norm(x, norm_in_gain[layer]) * (1.0 + scale[:, None, :]) + shift[:, None, :]

        proj = h @ w_in[layer]
        q, k, v, z_attn, xbc, dt_raw, z_ssm = jnp.split(proj, splits, axis=-1)

        o = stick_breaking_attention(
            q.reshape(bsz, seq, SB_HEADS, SB_HEAD_DIM),
            k.reshape(bsz, seq, SB_HEADS, SB_HEAD_DIM),
            v.reshape(bsz, seq, SB_HEADS, SB_HEAD_DIM)).reshape(bsz, seq, D_ATTN)
        y_attn = rms_norm(o, sb_norm_gain[layer]) * jax.nn.silu(z_attn)

        xbc = jax.nn.silu(causal_depthwise_conv(xbc, conv_w[layer], conv_b[layer]))
        xs, b_ssm, c_ssm = jnp.split(xbc, [D_SSM, D_SSM + SSM_GROUPS * SSM_STATE], axis=-1)
        dt = jax.nn.softplus((dt_raw + dt_bias[layer]).astype(jnp.float32))
        a = -jnp.exp(a_log[layer].astype(jnp.float32))
        y = ssd_scan(xs.reshape(bsz, seq, SSM_HEADS, SSM_HEAD_DIM), dt, a,
                     b_ssm.reshape(bsz, seq, SSM_GROUPS, SSM_STATE),
                     c_ssm.reshape(bsz, seq, SSM_GROUPS, SSM_STATE), d_skip[layer])
        y = y.reshape(bsz, seq, D_SSM).astype(x.dtype)
        y_ssm = rms_norm(y * jax.nn.silu(z_ssm), ssm_norm_gain[layer])

        mixed = jnp.concatenate([y_attn, y_ssm], axis=-1) @ w_out[layer]
        x = x + gate[:, None, :] * mixed
    return rms_norm(x, norm_f_gain)


DEPTH_2 = 2

N_MIXERS = 2
RWKV_HEAD = 64
RWKV_HEADS = D_MODEL // RWKV_HEAD
DECAY_LORA = 64
AAA_LORA = 64
MV_LORA = 32
GATE_LORA = 160
GN_EPS = 64e-5
N_RWKV_BRANCHES = 6
ATT_HEADS = 16
QK_HEAD = 64
V_HEAD = 64
Q_LORA = 256
KV_LORA = 128
IDX_HEADS = 8
IDX_DIM = 64
TOPK_MAX = 256
DSA_IN = Q_LORA + KV_LORA + IDX_DIM + IDX_HEADS
REL_BUCKETS = 32
REL_MAX_DIST = 128
D_FF = 2816
CONV_W = 3
DN_ALPHA = (2 * DEPTH_2) ** 0.25
DN_BETA = (8 * DEPTH_2) ** -0.25
LN_EPS = 1e-5


def layer_norm(x, g, b, eps=LN_EPS):
    xf = x.astype(jnp.float32)
    mu = xf.mean(-1, keepdims=True)
    var = jnp.square(xf - mu).mean(-1, keepdims=True)
    return ((xf - mu) * lax.rsqrt(var + eps) * g + b).astype(x.dtype)

def rms_norm_2(x, g, eps=1e-6):
    xf = x.astype(jnp.float32)
    return (xf * lax.rsqrt(jnp.square(xf).mean(-1, keepdims=True) + eps) * g).astype(x.dtype)

def token_shift(x):
    return jnp.pad(x, ((0, 0), (1, 0), (0, 0)))[:, :-1]

def t5_bucket(dist):
    n = jnp.maximum(dist, 0)
    max_exact = REL_BUCKETS // 2
    nf = jnp.maximum(n, 1).astype(jnp.float32)
    large = max_exact + (jnp.log(nf / max_exact) / math.log(REL_MAX_DIST / max_exact)
                         * (REL_BUCKETS - max_exact)).astype(jnp.int32)
    large = jnp.minimum(large, REL_BUCKETS - 1)
    return jnp.where(n < max_exact, n, large)

def _wkv7_step(state, inp):
    r_t, w_t, k_t, v_t, a_t, b_t = inp
    sa = jnp.einsum('bhvk,bhk->bhv', state, a_t)
    state = (state * w_t[:, :, None, :] + sa[..., None] * b_t[:, :, None, :]
             + v_t[..., None] * k_t[:, :, None, :])
    y = jnp.einsum('bhvk,bhk->bhv', state, r_t)
    return state, y

def rwkv7_time_mix(x, v_first, vres, mix, w_rkv, w0, w1, w2, a0, a1, a2, g1, g2,
                   k_k, k_a, r_k, lnx_g, lnx_b, w_o):
    B, S, D = x.shape
    H, N = RWKV_HEADS, RWKV_HEAD
    f32 = jnp.float32
    xx = token_shift(x) - x
    xm = x[None] + xx[None] * mix[:, None, None, :]
    r, k, v = jnp.einsum('nbsd,nde->nbse', xm[:3], w_rkv)
    xv, xw, xa, xg = xm[2], xm[3], xm[4], xm[5]
    w_log = -jax.nn.softplus(-(w0 + jnp.tanh(xw @ w1) @ w2)) - 0.5
    decay = jnp.exp(-jnp.exp(w_log.astype(f32)))
    if vres is None:
        v_first = v
    else:
        v0, v1, v2 = vres
        v = v + (v_first - v) * jax.nn.sigmoid(v0 + (xv @ v1) @ v2)
    a = jax.nn.sigmoid(a0 + (xa @ a1) @ a2)
    g = jax.nn.sigmoid(xg @ g1) @ g2
    heads = lambda t: t.reshape(B, S, H, N)
    kk = heads(k * k_k).astype(f32)
    kk = kk / jnp.maximum(jnp.sqrt(jnp.sum(kk * kk, -1, keepdims=True)), 1e-12)
    k = k * (1 + (a - 1) * k_a)
    rh, kh, vh, ah = heads(r), heads(k), heads(v), heads(a)
    tm = lambda t: jnp.moveaxis(t.astype(f32), 1, 0)
    xs = (tm(rh), tm(heads(decay)), tm(kh), tm(vh), tm(-kk), tm(kk * ah.astype(f32)))
    state0 = jnp.zeros((B, H, N, N), f32)
    _, y = lax.scan(_wkv7_step, state0, xs)
    y = jnp.moveaxis(y, 0, 1)
    mu = y.mean(-1, keepdims=True)
    var = jnp.square(y - mu).mean(-1, keepdims=True)
    y = ((y - mu) * lax.rsqrt(var + GN_EPS)).reshape(B, S, D) * lnx_g + lnx_b
    bonus = jnp.sum(rh * kh * r_k, -1, keepdims=True) * vh
    y = (y.astype(x.dtype) + bonus.reshape(B, S, D)) * g
    return y @ w_o, v_first

def dsa_attention(x, w_in, q_norm_g, kv_norm_g, w_uq, w_uk, w_uv, w_qidx, kidx_g, kidx_b,
                  rel_bias, w_o):
    B, S, D = x.shape
    H = ATT_HEADS
    topk = min(TOPK_MAX, S // 4)
    h = x @ w_in
    c_q, c_kv, k_idx, w_idx = jnp.split(
        h, [Q_LORA, Q_LORA + KV_LORA, Q_LORA + KV_LORA + IDX_DIM], axis=-1)
    c_q = rms_norm_2(c_q, q_norm_g)
    c_kv = rms_norm_2(c_kv, kv_norm_g)
    q = (c_q @ w_uq).reshape(B, S, H, QK_HEAD)
    q_idx = (c_q @ w_qidx).reshape(B, S, IDX_HEADS, IDX_DIM)
    k_idx = layer_norm(k_idx, kidx_g, kidx_b)
    w_idx = w_idx * (IDX_HEADS ** -0.5 * IDX_DIM ** -0.5)
    nb = S // Q_BLOCK
    blk = lambda t: jnp.swapaxes(t.reshape((B, nb, Q_BLOCK) + t.shape[2:]), 0, 1)
    starts = jnp.arange(nb, dtype=jnp.int32) * Q_BLOCK
    key_pos = jnp.arange(S, dtype=jnp.int32)
    qk_scale = QK_HEAD ** -0.5

    def block(args):
        q_b, qi_b, wi_b, t0 = args
        t_pos = t0 + jnp.arange(Q_BLOCK, dtype=jnp.int32)
        s_idx = jnp.einsum('bthd,bsd->bths', qi_b, k_idx)
        score = jnp.einsum('bths,bth->bts', jax.nn.relu(s_idx), wi_b).astype(jnp.float32)
        causal = key_pos[None, :] <= t_pos[:, None]
        score = jnp.where(causal[None], score, -jnp.inf)
        _, sel = lax.top_k(score, topk)
        kv_sel = jax.vmap(lambda c, i: c[i])(c_kv, sel)
        q_abs = jnp.einsum('bthd,hdc->bthc', q_b, w_uk)
        logits = jnp.einsum('bthc,btkc->bhtk', q_abs, kv_sel).astype(jnp.float32) * qk_scale
        dist = t_pos[None, :, None] - sel
        bias = rel_bias[t5_bucket(dist)].astype(jnp.float32)
        logits = logits + jnp.moveaxis(bias, -1, 1)
        logits = jnp.where((dist >= 0)[:, None], logits, -jnp.inf)
        p = jax.nn.softmax(logits, axis=-1).astype(x.dtype)
        o_lat = jnp.einsum('bhtk,btkc->bthc', p, kv_sel)
        o = jnp.einsum('bthc,hcv->bthv', o_lat, w_uv)
        return o.reshape(B, Q_BLOCK, H * V_HEAD)

    o = lax.map(block, (blk(q), blk(q_idx), blk(w_idx), starts))
    o = jnp.swapaxes(o, 0, 1).reshape(B, S, H * V_HEAD)
    return o @ w_o

def conv_ffn(x, w_up, conv_w, conv_b, w_down):
    S = x.shape[1]
    u = x @ w_up
    up = jnp.pad(u, ((0, 0), (CONV_W - 1, 0), (0, 0)))
    u = sum(up[:, j:j + S] * conv_w[j] for j in range(CONV_W)) + conv_b
    gate, val = jnp.split(u, 2, axis=-1)
    return (jax.nn.silu(gate) * val) @ w_down

def second_inputs(seed: int = 0) -> dict:
    key = jax.random.key(seed)
    ks = iter(jax.random.split(key, 64))
    f32 = jnp.float32
    n = lambda shape, scale: scale * jax.random.normal(next(ks), shape, f32)
    D, H, N = D_MODEL, RWKV_HEADS, RWKV_HEAD
    n_rwkv = (DEPTH_2 + 1) // 2
    n_dsa = DEPTH_2 // 2
    n_vres = max(n_rwkv - 1, 0)
    return {
        "x": n((BATCH, SEQ, D), 1.0),
        "ln_g": 1.0 + n((DEPTH_2, 2, D), 0.02),
        "ln_b": n((DEPTH_2, 2, D), 0.02),
        "rwkv_mix": jax.random.uniform(next(ks), (n_rwkv, N_RWKV_BRANCHES, D), f32),
        "rwkv_w_rkv": n((n_rwkv, 3, D, D), D ** -0.5),
        "rwkv_w0": -1.5 + n((n_rwkv, D), 1.0),
        "rwkv_w1": n((n_rwkv, D, DECAY_LORA), D ** -0.5),
        "rwkv_w2": n((n_rwkv, DECAY_LORA, D), 0.5 * DECAY_LORA ** -0.5),
        "rwkv_a0": n((n_rwkv, D), 0.1),
        "rwkv_a1": n((n_rwkv, D, AAA_LORA), D ** -0.5),
        "rwkv_a2": n((n_rwkv, AAA_LORA, D), 0.5 * AAA_LORA ** -0.5),
        "rwkv_v0": n((n_vres, D), 0.1),
        "rwkv_v1": n((n_vres, D, MV_LORA), D ** -0.5),
        "rwkv_v2": n((n_vres, MV_LORA, D), 0.5 * MV_LORA ** -0.5),
        "rwkv_g1": n((n_rwkv, D, GATE_LORA), D ** -0.5),
        "rwkv_g2": n((n_rwkv, GATE_LORA, D), GATE_LORA ** -0.5),
        "rwkv_k_k": 0.85 + n((n_rwkv, D), 0.05),
        "rwkv_k_a": 1.0 + n((n_rwkv, D), 0.05),
        "rwkv_r_k": n((n_rwkv, H, N), 0.1),
        "rwkv_lnx_g": 1.0 + n((n_rwkv, D), 0.02),
        "rwkv_lnx_b": n((n_rwkv, D), 0.02),
        "rwkv_w_o": n((n_rwkv, D, D), DN_BETA * D ** -0.5),
        "dsa_w_in": n((n_dsa, D, DSA_IN), D ** -0.5),
        "dsa_q_norm_g": 1.0 + n((n_dsa, Q_LORA), 0.02),
        "dsa_kv_norm_g": 1.0 + n((n_dsa, KV_LORA), 0.02),
        "dsa_w_uq": n((n_dsa, Q_LORA, ATT_HEADS * QK_HEAD), Q_LORA ** -0.5),
        "dsa_w_uk": n((n_dsa, ATT_HEADS, QK_HEAD, KV_LORA), KV_LORA ** -0.5),
        "dsa_w_uv": n((n_dsa, ATT_HEADS, KV_LORA, V_HEAD), KV_LORA ** -0.5),
        "dsa_w_qidx": n((n_dsa, Q_LORA, IDX_HEADS * IDX_DIM), Q_LORA ** -0.5),
        "dsa_kidx_g": 1.0 + n((n_dsa, IDX_DIM), 0.02),
        "dsa_kidx_b": n((n_dsa, IDX_DIM), 0.02),
        "dsa_w_o": n((n_dsa, ATT_HEADS * V_HEAD, D), DN_BETA * (ATT_HEADS * V_HEAD) ** -0.5),
        "rel_bias": n((REL_BUCKETS, ATT_HEADS), 0.5),
        "ffn_w_up": n((DEPTH_2, D, 2 * D_FF), D ** -0.5),
        "ffn_conv_w": n((DEPTH_2, CONV_W, 2 * D_FF), CONV_W ** -0.5),
        "ffn_conv_b": n((DEPTH_2, 2 * D_FF), 0.02),
        "ffn_w_down": n((DEPTH_2, D_FF, D), DN_BETA * D_FF ** -0.5),
    }

def second_block(x, ln_g, ln_b, rwkv_mix, rwkv_w_rkv, rwkv_w0, rwkv_w1, rwkv_w2, rwkv_a0, rwkv_a1,
              rwkv_a2, rwkv_v0, rwkv_v1, rwkv_v2, rwkv_g1, rwkv_g2, rwkv_k_k, rwkv_k_a, rwkv_r_k,
              rwkv_lnx_g, rwkv_lnx_b, rwkv_w_o, dsa_w_in, dsa_q_norm_g, dsa_kv_norm_g, dsa_w_uq,
              dsa_w_uk, dsa_w_uv, dsa_w_qidx, dsa_kidx_g, dsa_kidx_b, dsa_w_o, rel_bias,
              ffn_w_up, ffn_conv_w, ffn_conv_b, ffn_w_down):
    v_first = None
    for i in range(DEPTH_2):
        j = i // N_MIXERS
        if i % N_MIXERS == 0:
            vres = None if j == 0 else (rwkv_v0[j - 1], rwkv_v1[j - 1], rwkv_v2[j - 1])
            h, v_first = rwkv7_time_mix(
                x, v_first, vres, rwkv_mix[j], rwkv_w_rkv[j], rwkv_w0[j], rwkv_w1[j], rwkv_w2[j],
                rwkv_a0[j], rwkv_a1[j], rwkv_a2[j], rwkv_g1[j], rwkv_g2[j], rwkv_k_k[j],
                rwkv_k_a[j], rwkv_r_k[j], rwkv_lnx_g[j], rwkv_lnx_b[j], rwkv_w_o[j])
        else:
            h = dsa_attention(
                x, dsa_w_in[j], dsa_q_norm_g[j], dsa_kv_norm_g[j], dsa_w_uq[j], dsa_w_uk[j],
                dsa_w_uv[j], dsa_w_qidx[j], dsa_kidx_g[j], dsa_kidx_b[j], rel_bias, dsa_w_o[j])
        x = layer_norm(DN_ALPHA * x + h, ln_g[i, 0], ln_b[i, 0])
        f = conv_ffn(x, ffn_w_up[i], ffn_conv_w[i], ffn_conv_b[i], ffn_w_down[i])
        x = layer_norm(DN_ALPHA * x + f, ln_g[i, 1], ln_b[i, 1])
    return x


def setup_inputs(seed=0):
    out = dict(first_inputs(seed))
    for name, value in second_inputs(seed + 1).items():
        if name != "x":
            out[name + "_2"] = value
    return out


def reference(
    x, c, w_ada, b_ada, norm_in_gain, w_in, conv_w, conv_b, dt_bias, a_log, d_skip,
    sb_norm_gain, ssm_norm_gain, w_out, norm_f_gain, ln_g_2, ln_b_2, rwkv_mix_2, rwkv_w_rkv_2,
    rwkv_w0_2, rwkv_w1_2, rwkv_w2_2, rwkv_a0_2, rwkv_a1_2, rwkv_a2_2, rwkv_v0_2, rwkv_v1_2,
    rwkv_v2_2, rwkv_g1_2, rwkv_g2_2, rwkv_k_k_2, rwkv_k_a_2, rwkv_r_k_2, rwkv_lnx_g_2,
    rwkv_lnx_b_2, rwkv_w_o_2, dsa_w_in_2, dsa_q_norm_g_2, dsa_kv_norm_g_2, dsa_w_uq_2,
    dsa_w_uk_2, dsa_w_uv_2, dsa_w_qidx_2, dsa_kidx_g_2, dsa_kidx_b_2, dsa_w_o_2, rel_bias_2,
    ffn_w_up_2, ffn_conv_w_2, ffn_conv_b_2, ffn_w_down_2,
):
    x = first_block(
        x, c, w_ada, b_ada, norm_in_gain, w_in, conv_w, conv_b, dt_bias, a_log, d_skip,
        sb_norm_gain, ssm_norm_gain, w_out, norm_f_gain,
    )
    return second_block(
        x, ln_g_2, ln_b_2, rwkv_mix_2, rwkv_w_rkv_2, rwkv_w0_2, rwkv_w1_2, rwkv_w2_2, rwkv_a0_2,
        rwkv_a1_2, rwkv_a2_2, rwkv_v0_2, rwkv_v1_2, rwkv_v2_2, rwkv_g1_2, rwkv_g2_2, rwkv_k_k_2,
        rwkv_k_a_2, rwkv_r_k_2, rwkv_lnx_g_2, rwkv_lnx_b_2, rwkv_w_o_2, dsa_w_in_2,
        dsa_q_norm_g_2, dsa_kv_norm_g_2, dsa_w_uq_2, dsa_w_uk_2, dsa_w_uv_2, dsa_w_qidx_2,
        dsa_kidx_g_2, dsa_kidx_b_2, dsa_w_o_2, rel_bias_2, ffn_w_up_2, ffn_conv_w_2,
        ffn_conv_b_2, ffn_w_down_2,
    )


_drawn_inputs = setup_inputs


def setup_inputs(seed=0):
    import zlib

    import numpy as np

    out = dict(_drawn_inputs(seed))
    spreads = {}
    factors = {'conv_b': 6.389,
     'd_skip': 3.56,
     'rwkv_w1_2': 4.648,
     'rwkv_w2_2': 4.692,
     'rwkv_a0_2': 5.624,
     'rwkv_k_k_2': 8.0,
     'rwkv_k_a_2': 4.902,
     'rwkv_lnx_g_2': 8.0,
     'rwkv_lnx_b_2': 8.0,
     'dsa_q_norm_g_2': 8.0,
     'dsa_kv_norm_g_2': 8.0,
     'dsa_kidx_g_2': 8.0,
     'dsa_kidx_b_2': 8.0,
     'ffn_conv_b_2': 6.081}
    for name, (base, spread) in spreads.items():
        noise = np.random.default_rng([zlib.crc32(name.encode()), seed]).standard_normal(out[name].shape)
        drawn = base * np.exp(spread * noise) if base else spread * noise
        out[name] = jnp.asarray(drawn.astype(out[name].dtype))
    for name, factor in factors.items():
        out[name] = (out[name] * factor).astype(out[name].dtype)
    return out
```

```python
import numpy as np
import concourse.bass as bass
from concourse import mybir
from contextlib import ExitStack

P = 128
T = 512
D = 1024
KT = D // P
NB = T // P
HD = 64
H = D // HD
D_SSM = 1024
XBC_T = 12
D_FF = 2816
FT = D_FF // P
BUCKETS = 32
TOPK = min(256, T // 4)
RING = 6
CHUNK = 8 * P
ALPHA = 4 ** 0.25
NEG = -1e30
C0 = float(np.exp(-0.5))
BAND = T + P
TAKEN = -3e38

SB_W = [T - P * i for i in range(NB)]
SB_AT = [0, 512, 1024, 896]
SB_N = 1280

COLS = [("c", 8), ("b_ada", 24), ("norm_in_gain", 8), ("conv_w", 48), ("conv_b", 12), ("d_skip", 8),
        ("sb_norm_gain", 8), ("ssm_norm_gain", 8), ("norm_f_gain", 8), ("dt_bias", 16), ("a_log", 16),
        ("ln_g", 32), ("ln_b", 32), ("mix", 48), ("w0", 8), ("a0", 8), ("k_k", 8), ("k_a", 8),
        ("r_k", 8), ("lnx_g", 8), ("lnx_b", 8), ("q_norm_g", 2), ("kv_norm_g", 1), ("kidx_g", 1),
        ("kidx_b", 1), ("ffn_conv_w", 2 * 3 * 2 * FT), ("ffn_conv_b", 2 * 2 * FT)]
COL_AT = {}
_n = 0
for _name, _w in COLS:
    COL_AT[_name] = _n
    _n += _w
N_COLS = _n

MATS = ["ident", "ones", "head_ones", "lt", "le", "gt", "neg_ge", "neg_ones", "flip", "neg_after"] + [f"pair{i}" for i in range(7)] + ["pair0_t"]
MAT_AT = {m: i for i, m in enumerate(MATS)}


def square_constants():
    p, f = np.arange(P)[:, None], np.arange(P)[None, :]
    out = {"ident": p == f, "ones": p >= 0 * f, "head_ones": p // HD == f // HD, "lt": p < f, "le": p <= f,
           "gt": p > f, "neg_ge": -1.0 * (p >= f), "neg_ones": -1.0 * (p >= 0 * f),
           "flip": p + f == P - 1, "neg_after": np.where(f > p, NEG, 0)}
    for i in range(7):
        out[f"pair{i}"] = (p >> (i + 1) == f >> (i + 1)) & (((p >> i) & 1) == 1) & (((f >> i) & 1) == 0)
    out["pair0_t"] = out["pair0"].T
    return np.concatenate([np.asarray(out[m], np.float32) for m in MATS], axis=1)


def late_constant():
    out = np.zeros((P, SB_N), np.float32)
    p, f = np.arange(P)[:, None], np.arange(P)[None, :]
    for i in range(NB):
        out[:, SB_AT[i]:SB_AT[i] + P] = np.where(p >= f, NEG, 0)
    return out


def bucket_constant():
    n = np.maximum(T - 1 - np.arange(BAND), 0)
    nf = np.maximum(n, 1).astype(np.float32)
    large = 16 + (np.log(nf / 16) / np.log(128 / 16) * 16).astype(np.int32)
    b = np.where(n < 16, n, np.minimum(large, BUCKETS - 1))
    return (np.arange(BUCKETS)[:, None] == b[None, :]).astype(np.float32)


ORDER = ["xT", "cols", "squares", "late", "bucket1h", "w_ada", "w_in", "w_dt", "w_out", "w_rkv", "w_w1", "w_a1",
         "w_g1", "w_w2", "w_a2", "w_g2", "w_o", "d_in", "d_uq", "d_widx", "d_uk", "d_uv", "d_qidx", "d_wo", "rel_bias",
         "up0", "up1", "down0", "down1"]


def program(nc, A, out, stop=None, dump=None):
    f32 = mybir.dt.float32
    ALU = mybir.AluOpType
    ACT = mybir.ActivationFunctionType
    AX = mybir.AxisListType.X
    ctx = ExitStack()
    assert TOPK == P

    def sb(name, shape):
        return ctx.enter_context(nc.sbuf_tensor(name, shape, f32))

    section = []

    def sem(name):
        section.append(nc.alloc_semaphore(name))
        return section[-1]

    def end_section():
        nc.clear_and_free_semaphores(section)
        section.clear()
        nc.all_engine_barrier()

    with ctx:
        F = [sb(f"act{i}", [P, KT, T]) for i in range(9)]
        ring = sb("weight_ring", [P, RING, CHUNK])
        cols = sb("cols", [P, N_COLS])
        squares = sb("squares", [P, len(MATS) * P])
        small = sb("small", [P, 256])
        mod = sb("mod", [P, 24])
        stat = sb("stat", [P, 2, T])
        PS = ctx.enter_context(nc.psum_tensor("banks", [P, 8, T], f32))
        late = sb("late", [P, SB_N])
        aux = sb("aux", [P, 3584])

        def col(name, i):
            return cols[:, COL_AT[name] + i:COL_AT[name] + i + 1]

        def mat(name):
            return squares[:, MAT_AT[name] * P:MAT_AT[name] * P + P]

        def mat4(name):
            return mat(name).unsqueeze(1).to_broadcast([P, 4, P])

        plan = []

        def planned(array, n_tiles, k_tiles, n_cols=P):
            for n in n_tiles:
                for k in range(0, k_tiles, 8):
                    w = min(8, k_tiles - k)
                    plan.append((array[n, :, k * n_cols:(k + w) * n_cols], w * n_cols))

        planned(A["w_ada"], range(24), 8)
        planned(A["w_in"], range(32), 8)
        planned(A["w_in"], range(32, 44), 8)
        planned(A["w_dt"], range(1), 8, 16)
        planned(A["w_in"], range(44, 52), 8)
        planned(A["w_out"], range(8), 16)
        planned(A["w_rkv"], range(24), 8)
        planned(A["w_w1"], range(1), 8, 64)
        planned(A["w_a1"], range(1), 8, 64)
        planned(A["w_g1"], range(2), 8, 80)
        planned(A["w_o"], range(8), 8)
        planned(A["up0"], [i + j * FT for i in range(FT) for j in range(2)], 8)
        planned(A["down0"], range(8), FT)
        planned(A["d_in"], range(4), 8)
        planned(A["d_widx"], range(1), 8, 8)
        planned(A["d_uq"], range(8), 2)
        planned(A["d_qidx"], range(4), 2)
        planned(A["d_wo"], range(8), 8)
        planned(A["up1"], [i + j * FT for i in range(FT) for j in range(2)], 8)
        planned(A["down1"], range(8), FT)
        weight_loaded = [nc.alloc_semaphore(f"weight_loaded{i}") for i in range(RING)]
        weight_used = nc.alloc_semaphore("weight_used")
        stored = nc.alloc_semaphore("out_stored")
        at = {"issued": 0, "used": 0}

        def next_chunk(pe):
            i = at["used"]
            pe.wait_ge(weight_loaded[i % RING], 16 * (i // RING + 1))
            at["used"] += 1
            return ring[:, i % RING, :]

        def col_k(name, i):
            return cols[:, COL_AT[name] + i:COL_AT[name] + i + 1]

        def gemm(name, n_tiles, k_tiles, rhs, evac, n_cols=P, prepare=None):
            per = -(-k_tiles // 8)
            first = at["used"]
            names = list(evac)
            taken = {e: sem(name + "_taken_by_" + e) for e in names}
            who = lambda n: names[n % len(names)]
            nth = lambda n: n // len(names) + 1
            prepared = sem(name + "_prepared") if prepare else None
            with nc.Block() as block:
                @block.tensor
                def _(pe):
                    for n in range(n_tiles):
                        if n >= 4:
                            pe.wait_ge(taken[who(n - 4)], nth(n - 4))
                        for k in range(k_tiles):
                            if k % 8 == 0:
                                w = next_chunk(pe)
                            if prepare and n == 0:
                                pe.wait_ge(prepared, k + 1)
                            mm = nc.tensor.matmul(PS[0:n_cols, n % 4, :], w[:, k % 8 * n_cols:(k % 8 + 1) * n_cols],
                                                  rhs(k), start=k == 0, stop=k == k_tiles - 1)
                            if k % 8 == 7 or k == k_tiles - 1:
                                mm.then_inc(weight_used, 1)

                def run(e, eng):
                    for n in range(n_tiles):
                        if who(n) == e:
                            eng.wait_ge(weight_used, first + per * (n + 1))
                            evac[e](eng, n, PS[0:n_cols, n % 4, :]).then_inc(taken[e], 1)

                if "act" in evac:
                    @block.scalar
                    def _(act):
                        run("act", act)
                if "dve" in evac or prepare:
                    @block.vector
                    def _(dve):
                        if prepare:
                            for k in range(k_tiles):
                                prepare(k).then_inc(prepared, 1)
                        run("dve", dve)

                @block.sync
                def _(sp):
                    stream(sp)

        def stream(sp):
            while at["issued"] < min(len(plan), at["used"] + RING):
                i = at["issued"]
                src, w = plan[i]
                if i >= RING:
                    sp.wait_ge(weight_used, i - RING + 1)
                sp.dma_start(ring[:, i % RING, 0:w], src).then_inc(weight_loaded[i % RING], 16)
                at["issued"] += 1

        def norm(name, x, n_tiles, n_channels, eps, gain, write, centered=False, bias=None, scratch=None, stage_cols=P,
                 ones="ones", width=T, prescale=None):
            summed, squared = sem(name + "_summed"), sem(name + "_squared")
            step, root = sem(name + "_step"), sem(name + "_root")
            sq = scratch
            with nc.Block() as block:
                @block.tensor
                def _(pe):
                    if centered:
                        for i in range(n_tiles):
                            mm = nc.tensor.matmul(PS[:, 4, :], mat(ones), x(i), start=i == 0, stop=i == n_tiles - 1)
                        mm.then_inc(summed, 1)
                    for i in range(n_tiles):
                        pe.wait_ge(squared, i + 1)
                        mm = nc.tensor.matmul(PS[:, 5, :], mat(ones), sq(i), start=i == 0, stop=i == n_tiles - 1)
                    mm.then_inc(summed, 1)

                @block.scalar
                def _(act):
                    for i in range(n_tiles):
                        if centered:
                            act.wait_ge(step, i + 1)
                        nc.scalar.activation(sq(i), x(i), ACT.Square).then_inc(squared, 1)
                    act.wait_ge(summed, 2 if centered else 1)
                    act.wait_ge(step, (n_tiles if centered else 0) + 1)
                    nc.scalar.activation(stat[:, 0, :], PS[:, 5, :], ACT.Sqrt, scale=1.0 / n_channels,
                                         bias=small[:, 250:251]).then_inc(root, 1)
                    if bias is not None:
                        for i in range(n_tiles):
                            act.wait_ge(step, (n_tiles if centered else 0) + 3 + i)
                            nc.scalar.activation(write(i), write(i), ACT.Identity, bias=bias(i)).then_inc(root, 1)

                @block.vector
                def _(dve):
                    done = 0
                    if centered:
                        dve.wait_ge(summed, 1)
                        for i in range(n_tiles):
                            nc.vector.scalar_tensor_tensor(out=x(i), in0=PS[:, 4, :], scalar=-1.0 / n_channels, in1=x(i),
                                                           op0=ALU.mult, op1=ALU.add).then_inc(step, 1)
                        done = n_tiles
                    nc.vector.memset(small[:, 250:251], eps).then_inc(step, 1)
                    dve.wait_ge(root, 1)
                    nc.vector.reciprocal(stat[:, 1, :], stat[:, 0, :]).then_inc(step, 1)
                    dve.wait_ge(step, done + 2)
                    for i in range(n_tiles):
                        nc.vector.scalar_tensor_tensor(out=write(i), in0=x(i), scalar=gain(i), in1=stat[:, 1, :],
                                                       op0=ALU.mult, op1=ALU.mult).then_inc(step, 1)

        def loads(name, pairs):
            loaded = sem(name)
            with nc.Block() as block:
                @block.scalar
                def _(act):
                    for dst, src in pairs:
                        act.dma_start(dst, src).then_inc(loaded, 16)
                    act.wait_ge(loaded, 16 * len(pairs))

                @block.sync
                def _(sp):
                    stream(sp)

        def copy_act(dst):
            return lambda eng, n, bank: nc.scalar.copy(dst(n), bank)

        def copy_dve(dst):
            return lambda eng, n, bank: nc.vector.tensor_copy(dst(n), bank)

        class Stop(Exception):
            pass

        def checkpoint(name, ap=None):
            if stop == name:
                w = sem("dumped")
                with nc.Block() as block:
                    @block.sync
                    def _(sp):
                        sp.dma_start(dump, ap).then_inc(w, 16)
                        for i in range(RING):
                            sp.wait_ge(weight_loaded[i], 16 * len(range(i, at["issued"], RING)))
                        sp.wait_ge(w, 16)
                raise Stop

        def rows(t):
            return lambda i: t[:, i, :]

        x, h = F[0], F[1]
        loads("inputs_loaded", [(cols[:, :], A["cols"]), (squares[:, :], A["squares"]), (x[:, :, :], A["xT"]),
                                (late[:, :], A["late"])])

        c_ready, mod_taken = sem("c_ready"), sem("mod_taken")
        first = at["used"]
        with nc.Block() as block:
            @block.scalar
            def _(act):
                nc.scalar.activation(small[:, 0:8], cols[:, COL_AT["c"]:COL_AT["c"] + 8], ACT.Silu).then_inc(c_ready, 1)

            @block.tensor
            def _(pe):
                pe.wait_ge(c_ready, 1)
                for n in range(24):
                    w = next_chunk(pe)
                    for k in range(8):
                        mm = nc.tensor.matmul(PS[:, 0, n:n + 1], w[:, k * P:(k + 1) * P], small[:, k:k + 1], start=k == 0, stop=k == 7)
                    mm.then_inc(weight_used, 1)

            @block.vector
            def _(dve):
                dve.wait_ge(weight_used, first + 24)
                nc.vector.tensor_tensor(mod[:, :], PS[:, 0, 0:24], cols[:, COL_AT["b_ada"]:COL_AT["b_ada"] + 24], ALU.add).then_inc(mod_taken, 1)
                dve.wait_ge(mod_taken, 1)
                nc.vector.scalar_tensor_tensor(out=small[:, 8:16], in0=mod[:, 8:16], scalar=1.0,
                                               in1=cols[:, COL_AT["norm_in_gain"]:COL_AT["norm_in_gain"] + 8],
                                               op0=ALU.add, op1=ALU.mult).then_inc(mod_taken, 1)

            @block.sync
            def _(sp):
                stream(sp)
        norm("norm_in", rows(x), 8, D, 1e-6, lambda i: small[:, 8 + i:9 + i], rows(h), bias=lambda i: mod[:, i:i + 1],
             scratch=rows(F[2]))
        checkpoint("h", h[:, :, :])

        q, k_, v = F[2], F[3], F[4]
        gemm("q", 8, 8, rows(h), {"act": lambda e, n, b: nc.scalar.mul(q[:, n, :], b, HD ** -0.5),
                                  "dve": lambda e, n, b: nc.vector.tensor_scalar(q[:, n, :], b, HD ** -0.5, None, ALU.mult)})
        gemm("k", 8, 8, rows(h), {"act": copy_act(rows(k_)), "dve": copy_dve(rows(k_))})

        def gemm_tokens(name, n_tiles, rhs_tokens, dst):
            first = at["used"]
            taken = sem(name + "_taken")
            with nc.Block() as block:
                @block.tensor
                def _(pe):
                    for n in range(n_tiles):
                        if n >= 4:
                            pe.wait_ge(taken, n - 3)
                        w = next_chunk(pe)
                        for b in range(NB):
                            for k in range(8):
                                mm = nc.tensor.matmul(PS[:, n % 4, b * P:(b + 1) * P], rhs_tokens(k, b), w[:, k * P:(k + 1) * P],
                                                      start=k == 0, stop=k == 7)
                        mm.then_inc(weight_used, 1)

                @block.scalar
                def _(act):
                    for n in range(n_tiles):
                        act.wait_ge(weight_used, first + n + 1)
                        nc.scalar.copy(dst(n), PS[:, n % 4, :].rearrange("p (b c) -> p b c", b=NB)).then_inc(taken, 1)

                @block.sync
                def _(sp):
                    stream(sp)

        v_tok = v[:, :, :].rearrange("p a b -> p (a b)").rearrange("p (b c) -> p b c", b=NB)
        gemm_tokens("v", 8, lambda k, b: h[:, k, b * P:(b + 1) * P], lambda n: v_tok[:, :, n * P:(n + 1) * P])
        checkpoint("v", v[:, :, :])

        o = F[5]
        work = F[6][:, :, :].rearrange("p a b -> p (a b)")
        clamped = [work[:, 0:SB_N], work[:, SB_N:2 * SB_N]]
        sp_m = [F[7][:, :, :].rearrange("p a b -> p (a b)")[:, i * SB_N:(i + 1) * SB_N] for i in range(2)]
        wts = F[8][:, :, :].rearrange("p a b -> p (a b)")[:, 0:SB_N]
        zb = PS[:, 0:3, :].rearrange("p a b -> p (a b)")
        wb = PS[:, 3:6, :].rearrange("p a b -> p (a b)")
        z_ready, z_taken, sp_step = sem("z_ready"), sem("z_taken"), sem("softplus_step")
        clamp_ready, log_ready, sp_ready = sem("clamp_ready"), sem("log_ready"), sem("sp_ready")
        w_ready, w_clamped, wts_ready = sem("w_ready"), sem("w_clamped"), sem("wts_ready")
        o_ready, o_taken, exp_done, late_masked = sem("o_ready"), sem("o_taken"), sem("sb_exp_done"), sem("sp_masked")
        with nc.Block() as block:
            def head(t, hh, a, b):
                return t[hh % 2 * HD:(hh % 2 + 1) * HD, hh // 2, a:b]

            @block.tensor
            def _(pe):
                def scores(hh, dst, stop):
                    for i in range(NB):
                        mm = nc.tensor.matmul(dst[:, SB_AT[i]:SB_AT[i] + SB_W[i]], head(k_, hh, i * P, (i + 1) * P),
                                              head(q, hh, i * P, T), start=True, stop=stop)
                    return mm

                def products(hh):
                    pe.wait_ge(wts_ready, hh + 1)
                    if hh >= 4 and hh % 2 == 0:
                        pe.wait_ge(o_taken, (hh - 4) // 2 + 1)
                    for i in range(NB):
                        mm = nc.tensor.matmul(PS[hh % 2 * HD:(hh % 2 + 1) * HD, 6 + hh // 2 % 2, i * P:T],
                                              v_tok[:, i, hh * HD:(hh + 1) * HD], wts[:, SB_AT[i]:SB_AT[i] + SB_W[i]],
                                              start=i == 0, stop=i == NB - 1)
                    mm.then_inc(o_ready, 1)

                scores(0, zb, True).then_inc(z_ready, 1)
                for hh in range(H):
                    if hh + 1 < H:
                        pe.wait_ge(sp_ready, hh + 1)
                        scores(hh + 1, zb, True).then_inc(z_ready, 1)
                    pe.wait_ge(late_masked, hh + 1)
                    if hh >= 1:
                        pe.wait_ge(w_clamped, hh)
                    for i in range(NB):
                        nc.tensor.matmul(wb[:, SB_AT[i]:SB_AT[i] + SB_W[i]], head(k_, hh, i * P, (i + 1) * P),
                                         head(q, hh, i * P, T), start=True, stop=False)
                        for j in range(i, NB):
                            mm = nc.tensor.matmul(wb[:, SB_AT[i] + (j - i) * P:SB_AT[i] + SB_W[i]],
                                                  mat("neg_ge" if i == j else "neg_ones"),
                                                  sp_m[hh % 2][:, SB_AT[j]:SB_AT[j] + SB_W[j]], start=False, stop=j == NB - 1)
                    mm.then_inc(w_ready, 1)
                    if hh >= 1:
                        products(hh - 1)
                products(H - 1)

            @block.vector
            def _(dve):
                def clamp(hh):
                    dve.wait_ge(z_ready, hh + 1)
                    if hh >= 2:
                        dve.wait_ge(log_ready, hh - 1)
                    nc.vector.tensor_scalar(clamped[hh % 2], zb[:, 0:SB_N], 80.0, None, ALU.min).then_inc(clamp_ready, 1)
                for hh in range(H):
                    clamp(hh)
                    dve.wait_ge(log_ready, hh + 1)
                    if hh >= 2:
                        dve.wait_ge(w_ready, hh - 1)
                    nc.vector.tensor_tensor(sp_m[hh % 2], clamped[hh % 2], zb[:, 0:SB_N], ALU.max).then_inc(sp_ready, 1)
                    dve.wait_ge(w_ready, hh + 1)
                    if hh >= 1:
                        dve.wait_ge(o_ready, hh)
                    nc.vector.scalar_tensor_tensor(out=wts, in0=wb[:, 0:SB_N], scalar=0.0, in1=late[:, :],
                                                   op0=ALU.min, op1=ALU.add).then_inc(w_clamped, 1)

            @block.scalar
            def _(act):
                def out_pair(p):
                    act.wait_ge(o_ready, 2 * p + 2)
                    nc.scalar.copy(o[:, p, :], PS[:, 6 + p % 2, :]).then_inc(o_taken, 1)
                for hh in range(H):
                    act.wait_ge(clamp_ready, hh + 1)
                    nc.scalar.activation(clamped[hh % 2], clamped[hh % 2], ACT.Exp).then_inc(exp_done, 1)
                    act.wait_ge(exp_done, hh + 1)
                    nc.scalar.activation(clamped[hh % 2], clamped[hh % 2], ACT.Ln, bias=1.0).then_inc(log_ready, 1)
                    act.wait_ge(w_clamped, hh + 1)
                    nc.scalar.activation(wts, wts, ACT.Exp).then_inc(wts_ready, 1)
                    if hh % 2 == 0 and hh >= 2:
                        out_pair(hh // 2 - 1)
                out_pair(H // 2 - 1)

            @block.gpsimd
            def _(pool):
                for hh in range(H):
                    pool.wait_ge(sp_ready, hh + 1)
                    for a, n in ((0, 1), (512, 1), (896, 2)):
                        part = sp_m[hh % 2][:, a:a + n * P].rearrange("p (n c) -> p n c", c=P)
                        last = nc.gpsimd.tensor_tensor(part, part, mat("lt").unsqueeze(1).to_broadcast([P, n, P]), ALU.mult)
                    last.then_inc(late_masked, 1)
        checkpoint("o", o[:, :, :])

        def conv_gemm(name, n_tiles, rhs, taps, w_col, b_col, dst, pair_out=None):
            first = at["used"]
            step, silu_done = sem(name + "_step"), sem(name + "_silu")
            per_pair = 2 * taps + 1

            def steps(n):
                return n // 2 * per_pair + taps * (n % 2 + 1) if pair_out else taps * (n + 1)

            with nc.Block() as block:
                @block.tensor
                def _(pe):
                    for n in range(n_tiles):
                        if n >= 4:
                            pe.wait_ge(step, steps(n - 4))
                        w = next_chunk(pe)
                        for k in range(8):
                            mm = nc.tensor.matmul(PS[:, n % 4, :], w[:, k * P:(k + 1) * P], rhs(k), start=k == 0, stop=k == 7)
                        mm.then_inc(weight_used, 1)

                @block.vector
                def _(dve):
                    for n in range(n_tiles):
                        dve.wait_ge(weight_used, first + n + 1)
                        if pair_out and n >= 4 and n % 2 == 0:
                            pass
                        nc.vector.tensor_scalar(dst(n), PS[:, n % 4, :], w_col(n, taps - 1), b_col(n), ALU.mult, ALU.add).then_inc(step, 1)
                        for j in range(1, taps):
                            dve.wait_ge(step, steps(n) - taps + j)
                            nc.vector.scalar_tensor_tensor(out=dst(n)[:, j:], in0=PS[:, n % 4, 0:T - j], scalar=w_col(n, taps - 1 - j),
                                                           in1=dst(n)[:, j:], op0=ALU.mult, op1=ALU.add).then_inc(step, 1)
                        if pair_out and n % 2 == 1:
                            dve.wait_ge(silu_done, n // 2 + 1)
                            dve.wait_ge(step, steps(n))
                            nc.vector.tensor_tensor(pair_out(n // 2), dst(n - 1), dst(n), ALU.mult).then_inc(step, 1)

                @block.scalar
                def _(act):
                    for n in range(n_tiles):
                        if pair_out and n % 2 == 1:
                            continue
                        act.wait_ge(step, steps(n))
                        nc.scalar.activation(dst(n), dst(n), ACT.Silu).then_inc(silu_done, 1)

                @block.sync
                def _(sp):
                    stream(sp)

        def multiply(name, dst, a, b):
            with nc.Block() as block:
                @block.vector
                def _(dve):
                    nc.vector.tensor_tensor(dst, a, b, ALU.mult)

                @block.sync
                def _(sp):
                    stream(sp)

        y_attn = F[2]
        norm("norm_sb", rows(o), 8, D, 1e-6, lambda i: col("sb_norm_gain", i), rows(y_attn), scratch=rows(F[3]))
        gemm("z_attn", 8, 8, rows(h), {"act": lambda e, n, b: nc.scalar.activation(F[3][:, n, :], b, ACT.Silu)})
        multiply("gate_attn", y_attn[:, :, :], y_attn[:, :, :], F[3][:, :, :])
        checkpoint("ya", y_attn[:, :, :])
        xs, bc = F[3], F[4]
        conv_gemm("xbc", 12, rows(h), 4, lambda n, j: col("conv_w", j * 12 + n), lambda n: col("conv_b", n),
                  lambda n: xs[:, n, :] if n < 8 else bc[:, n - 8, :])
        checkpoint("xbc", xs[:, :, :])

        flat = lambda t: t[:, :, :].rearrange("p a b -> p (a b)")
        sdt = flat(F[7])
        slot = lambda i: sdt[:, i * 64:(i + 1) * 64]
        by_block = lambda ap: ap.rearrange("p (b h) -> p b h", b=NB)
        over_blocks = lambda name: cols[:, COL_AT[name]:COL_AT[name] + H].unsqueeze(1).to_broadcast([P, NB, H])
        z_, m_, dt_, ea_, da_ = (slot(i) for i in range(5))
        dt_step, dt_act = sem("dt_step"), sem("dt_act")
        first = at["used"]
        with nc.Block() as block:
            @block.tensor
            def _(pe):
                w = next_chunk(pe)
                for b in range(NB):
                    for k in range(8):
                        mm = nc.tensor.matmul(PS[:, 0, b * H:(b + 1) * H], h[:, k, b * P:(b + 1) * P], w[:, k * H:(k + 1) * H], start=k == 0, stop=k == 7)
                mm.then_inc(weight_used, 1)

            @block.scalar
            def _(act):
                nc.scalar.activation(by_block(ea_), over_blocks("a_log"), ACT.Exp).then_inc(dt_act, 1)
                act.wait_ge(dt_step, 2)
                nc.scalar.activation(m_, m_, ACT.Exp).then_inc(dt_act, 1)
                act.wait_ge(dt_act, 2)
                nc.scalar.activation(m_, m_, ACT.Ln, bias=1.0).then_inc(dt_act, 1)

            @block.vector
            def _(dve):
                dve.wait_ge(weight_used, first + 1)
                nc.vector.tensor_tensor(by_block(z_), by_block(PS[:, 0, 0:64]), over_blocks("dt_bias"), ALU.add).then_inc(dt_step, 1)
                dve.wait_ge(dt_step, 1)
                nc.vector.tensor_scalar(m_, z_, 80.0, None, ALU.min).then_inc(dt_step, 1)
                dve.wait_ge(dt_act, 3)
                nc.vector.tensor_tensor(dt_, m_, z_, ALU.max).then_inc(dt_step, 1)
                dve.wait_ge(dt_step, 3)
                nc.vector.scalar_tensor_tensor(out=da_, in0=dt_, scalar=-1.0, in1=ea_, op0=ALU.mult, op1=ALU.mult).then_inc(dt_step, 1)

            @block.sync
            def _(sp):
                stream(sp)

        y = F[5]
        state = sdt[:, 512:1536]
        acum, total, cend, etot = sdt[:, 320:336], sdt[:, 336:352], sdt[:, 352:368], sdt[:, 368:384]
        b_tok = sdt[:, 1536:1792]
        cb = sdt[:, 1792:2048]
        x_dt, x_end = sdt[:, 2048:3072], sdt[:, 3072:4096]
        seg, c_exp = flat(F[6])[:, 0:2048], flat(F[6])[:, 2048:4096]
        per_head = lambda ap, w: ap.unsqueeze(2).to_broadcast([P, ap.shape[1], w])
        zeroed = sem("state_zeroed")
        with nc.Block() as block:
            @block.vector
            def _(dve):
                nc.vector.memset(state, 0.0).then_inc(zeroed, 1)
        for c in range(NB):
            t0, t1 = c * P, (c + 1) * P
            da_c, dt_c = da_[:, c * H:(c + 1) * H], dt_[:, c * H:(c + 1) * H]
            cums, moved, cbs, broad = (sem(f"scan{c}_{n}") for n in ("cums", "moved", "cb", "broadcast"))
            vec, sca, outs, states = (sem(f"scan{c}_{n}") for n in ("vec", "act", "y_ready", "state_ready"))
            with nc.Block() as block:
                @block.tensor
                def _(pe):
                    nc.tensor.matmul(PS[:, 0, 0:16], mat("le"), da_c, start=True, stop=True)
                    nc.tensor.matmul(PS[:, 0, 16:32], mat("ones"), da_c, start=True, stop=True).then_inc(cums, 1)
                    for i in range(8):
                        mm = nc.tensor.transpose(PS[:, 1 + i // 4, i % 4 * P:(i % 4 + 1) * P], xs[:, i, t0:t1], mat("ident"))
                        if i == 7:
                            mm.then_inc(moved, 1)
                    for g in range(2):
                        nc.tensor.transpose(PS[:, 3, g * P:(g + 1) * P], bc[:, g, t0:t1], mat("ident"))
                    for g in range(2):
                        mm = nc.tensor.matmul(PS[:, 3, (2 + g) * P:(3 + g) * P], bc[:, g, t0:t1], bc[:, 2 + g, t0:t1], start=True, stop=True)
                    mm.then_inc(cbs, 1)
                    for hh in range(H):
                        mm = nc.tensor.matmul(PS[:, 4 + hh // 4, hh % 4 * P:(hh % 4 + 1) * P],
                                              da_c[:, hh:hh + 1].to_broadcast([P, P]), mat("le"), start=True, stop=True)
                        if hh % 4 == 3:
                            mm.then_inc(broad, 1)

                @block.vector
                def _(dve):
                    dve.wait_ge(cums, 1)
                    nc.vector.tensor_copy(sdt[:, 320:352], PS[:, 0, 0:32]).then_inc(vec, 1)
                    dve.wait_ge(vec, 1)
                    nc.vector.tensor_tensor(cend, total, acum, ALU.subtract).then_inc(vec, 1)
                    dve.wait_ge(moved, 1)
                    nc.vector.tensor_tensor(x_dt.rearrange("p (h c) -> p h c", h=H),
                                            PS[:, 1:3, :].rearrange("p a (h c) -> p (a h) c", c=HD), per_head(dt_c, HD), ALU.mult).then_inc(vec, 1)
                    dve.wait_ge(cbs, 1)
                    nc.vector.tensor_tensor(cb.rearrange("p (g l) -> p g l", g=2), PS[:, 3, 2 * P:4 * P].rearrange("p (g l) -> p g l", g=2),
                                            mat("le").unsqueeze(1).to_broadcast([P, 2, P]), ALU.mult).then_inc(vec, 1)
                    dve.wait_ge(sca, 2)
                    dve.wait_ge(vec, 4)
                    nc.vector.tensor_tensor(x_end.rearrange("p (h c) -> p h c", h=H), x_dt.rearrange("p (h c) -> p h c", h=H),
                                            per_head(cend, HD), ALU.mult).then_inc(vec, 1)
                    for q4 in range(4):
                        dve.wait_ge(broad, q4 + 1)
                        part = seg[:, q4 * T:(q4 + 1) * T]
                        nc.vector.tensor_tensor(part.rearrange("p (h l) -> p h l", h=4), PS[:, 4 + q4, :].rearrange("p (h l) -> p h l", h=4),
                                                per_head(acum[:, q4 * 4:q4 * 4 + 4], P), ALU.subtract).then_inc(vec, 1)
                        dve.wait_ge(vec, 6 + 2 * q4)
                        nc.vector.tensor_scalar(part, part, 0.0, None, ALU.min).then_inc(vec, 1)
                    for q4 in range(4):
                        dve.wait_ge(sca, 5 + 2 * q4)
                        for t, m in ((seg, cb[:, q4 // 2 * P:(q4 // 2 + 1) * P]), (c_exp, bc[:, 2 + q4 // 2, t0:t1])):
                            part = t[:, q4 * T:(q4 + 1) * T].rearrange("p (h l) -> p h l", h=4)
                            nc.vector.tensor_tensor(part, part, m.unsqueeze(1).to_broadcast([P, 4, P]), ALU.mult).then_inc(vec, 1)
                    for i in range(8):
                        if i % 4 == 0:
                            dve.wait_ge(outs, i // 4 + 1)
                        nc.vector.scalar_tensor_tensor(out=y[:, i, t0:t1], in0=xs[:, i, t0:t1], scalar=col("d_skip", i),
                                                       in1=PS[:, 1 + i // 4, i % 4 * P:(i % 4 + 1) * P], op0=ALU.mult, op1=ALU.add).then_inc(vec, 1)
                    dve.wait_ge(outs, 2)
                    sv = state.rearrange("p (h c) -> p h c", h=H)
                    nc.vector.tensor_tensor(sv, sv, per_head(etot, HD), ALU.mult).then_inc(vec, 1)
                    dve.wait_ge(states, 1)
                    dve.wait_ge(vec, 30)
                    for g in range(2):
                        nc.vector.tensor_tensor(state[:, g * T:(g + 1) * T], state[:, g * T:(g + 1) * T], PS[:, 6 + g, :], ALU.add).then_inc(vec, 1)

                @block.scalar
                def _(act):
                    act.wait_ge(vec, 1)
                    nc.scalar.activation(etot, total, ACT.Exp).then_inc(sca, 1)
                    act.wait_ge(vec, 2)
                    nc.scalar.activation(cend, cend, ACT.Exp).then_inc(sca, 1)
                    act.wait_ge(vec, 4)
                    nc.scalar.copy(b_tok, PS[:, 3, 0:2 * P]).then_inc(sca, 1)
                    for q4 in range(4):
                        act.wait_ge(vec, 6 + 2 * q4)
                        nc.scalar.activation(c_exp[:, q4 * T:(q4 + 1) * T], PS[:, 4 + q4, :], ACT.Exp).then_inc(sca, 1)
                        act.wait_ge(vec, 7 + 2 * q4)
                        part = seg[:, q4 * T:(q4 + 1) * T]
                        nc.scalar.activation(part, part, ACT.Exp).then_inc(sca, 1)

                @block.tensor
                def _(pe):
                    for hh in range(H):
                        if hh % 4 == 0:
                            pe.wait_ge(vec, 15 + 2 * (hh // 4))
                        dst = PS[hh % 2 * HD:(hh % 2 + 1) * HD, 1 + hh // 8, hh // 2 % 4 * P:(hh // 2 % 4 + 1) * P]
                        nc.tensor.matmul(dst, x_dt[:, hh * HD:(hh + 1) * HD], seg[:, hh * P:(hh + 1) * P], start=True, stop=False)
                        mm = nc.tensor.matmul(dst, state[:, hh * HD:(hh + 1) * HD], c_exp[:, hh * P:(hh + 1) * P], start=False, stop=True)
                        if hh % 8 == 7:
                            mm.then_inc(outs, 1)
                    pe.wait_ge(sca, 11)
                    for g in range(2):
                        mm = nc.tensor.matmul(PS[:, 6 + g, :], b_tok[:, g * P:(g + 1) * P], x_end[:, g * T:(g + 1) * T], start=True, stop=True)
                    mm.then_inc(states, 1)
        checkpoint("yssd", y[:, :, :])

        gemm("z_ssm", 8, 8, rows(h), {"act": lambda e, n, b: nc.scalar.activation(F[3][:, n, :], b, ACT.Silu)})
        multiply("gate_ssm", F[3][:, :, :], F[3][:, :, :], y[:, :, :])
        y_ssm = F[4]
        norm("norm_ssm", rows(F[3]), 8, D, 1e-6, lambda i: col("ssm_norm_gain", i), rows(y_ssm), scratch=rows(F[6]))
        checkpoint("ys", y_ssm[:, :, :])
        gemm("w_out", 8, 16, lambda k: y_attn[:, k, :] if k < 8 else y_ssm[:, k - 8, :],
             {"dve": lambda e, n, b: nc.vector.scalar_tensor_tensor(out=x[:, n, :], in0=b, scalar=mod[:, 16 + n:17 + n], in1=x[:, n, :],
                                                                    op0=ALU.mult, op1=ALU.add)})
        norm("norm_f", rows(x), 8, D, 1e-6, lambda i: col("norm_f_gain", i), rows(x), scratch=rows(F[6]))
        checkpoint("x1", x[:, :, :])
        end_section()

        r, kx, v, sig, a_, xx, xm, tmp = F[1:9]
        ALL = lambda t: t[:, :, :]

        def differences(dst):
            with nc.Block() as block:
                @block.vector
                def _(dve):
                    nc.vector.tensor_tensor(dst[:, :, 1:T], x[:, :, 0:T - 1], x[:, :, 1:T], ALU.subtract)
                    nc.vector.tensor_scalar(dst[:, :, 0:1], x[:, :, 0:1], -1.0, None, ALU.mult)

                @block.sync
                def _(sp):
                    stream(sp)

        def mixed(dst, diff, branch):
            return lambda k: nc.vector.scalar_tensor_tensor(out=dst[:, k, :], in0=diff[:, k, :], scalar=col("mix", branch * 8 + k),
                                                            in1=x[:, k, :], op0=ALU.mult, op1=ALU.add)

        def lora_out(name, parts, evac):
            ready, taken = sem(name + "_ready"), sem(name + "_taken")
            with nc.Block() as block:
                @block.tensor
                def _(pe):
                    for n in range(8):
                        if n >= 4:
                            pe.wait_ge(taken, n - 3)
                        for j, (w, hid) in enumerate(parts):
                            mm = nc.tensor.matmul(PS[:, n % 4, :], w[:, n * P:(n + 1) * P], hid, start=j == 0, stop=j == len(parts) - 1)
                        mm.then_inc(ready, 1)

                def run(eng):
                    for n in range(8):
                        eng.wait_ge(ready, n + 1)
                        evac["act" if "act" in evac else "dve"](eng, n, PS[:, n % 4, :]).then_inc(taken, 1)

                if "act" in evac:
                    @block.scalar
                    def _(act):
                        run(act)
                else:
                    @block.vector
                    def _(dve):
                        run(dve)

        differences(xx)
        for b, (name, dst) in enumerate((("r", r), ("k7", kx), ("v7", v))):
            gemm(name, 8, 8, rows(xm), {"act": copy_act(rows(dst))}, prepare=mixed(xm, xx, b))
        lw = flat(tmp)
        w2_, a2_, hid_w, hid_a = lw[0:64, 0:D], lw[0:64, D:2 * D], lw[0:64, 2 * D:2 * D + T], lw[0:64, 2 * D + T:3 * D]
        loads("lora_loaded", [(w2_, A["w_w2"]), (a2_, A["w_a2"])])
        gemm("lora_w", 1, 8, rows(xm), {"act": lambda e, n, b: nc.scalar.activation(hid_w, b, ACT.Tanh)}, n_cols=64, prepare=mixed(xm, xx, 3))
        lora_out("decay", [(w2_, hid_w)], {"act": lambda e, n, b: nc.scalar.activation(sig[:, n, :], b, ACT.Sigmoid, bias=col("w0", n))})
        gemm("lora_a", 1, 8, rows(xm), {"act": copy_act(lambda n: hid_a)}, n_cols=64, prepare=mixed(xm, xx, 4))
        lora_out("rate", [(a2_, hid_a)], {"act": lambda e, n, b: nc.scalar.activation(a_[:, n, :], b, ACT.Sigmoid, bias=col("a0", n))})

        kk, bonus = xm, xx
        e1, e2, e3 = sem("kk_vec"), sem("kk_act"), sem("kk_sums")
        with nc.Block() as block:
            @block.vector
            def _(dve):
                for i in range(8):
                    nc.vector.tensor_scalar(kk[:, i, :], kx[:, i, :], col("k_k", i), None, ALU.mult).then_inc(e1, 1)
                dve.wait_ge(e2, 9)
                nc.vector.tensor_scalar(ALL(tmp), ALL(tmp), 1e-12, None, ALU.max).then_inc(e1, 1)
                dve.wait_ge(e1, 9)
                nc.vector.reciprocal(ALL(tmp), ALL(tmp)).then_inc(e1, 1)
                dve.wait_ge(e1, 10)
                nc.vector.tensor_tensor(ALL(kk), ALL(kk), ALL(tmp), ALU.mult).then_inc(e1, 1)
                dve.wait_ge(e1, 11)
                for i in range(8):
                    nc.vector.tensor_scalar(tmp[:, i, :], a_[:, i, :], 1.0, col("k_a", i), ALU.subtract, ALU.mult).then_inc(e1, 1)
                dve.wait_ge(e1, 19)
                nc.vector.scalar_tensor_tensor(out=ALL(kx), in0=ALL(tmp), scalar=1.0, in1=ALL(kx), op0=ALU.add, op1=ALU.mult).then_inc(e1, 1)
                dve.wait_ge(e1, 20)
                for i in range(8):
                    nc.vector.scalar_tensor_tensor(out=tmp[:, i, :], in0=r[:, i, :], scalar=col("r_k", i), in1=kx[:, i, :],
                                                   op0=ALU.mult, op1=ALU.mult).then_inc(e1, 1)
                dve.wait_ge(e3, 2)
                nc.vector.tensor_tensor(ALL(bonus), PS[:, :, :], ALL(v), ALU.mult).then_inc(e1, 1)

            @block.scalar
            def _(act):
                for i in range(8):
                    act.wait_ge(e1, i + 1)
                    nc.scalar.activation(tmp[:, i, :], kk[:, i, :], ACT.Square).then_inc(e2, 1)
                act.wait_ge(e3, 1)
                nc.scalar.activation(ALL(tmp), PS[:, :, :], ACT.Sqrt).then_inc(e2, 1)

            @block.tensor
            def _(pe):
                for i in range(8):
                    pe.wait_ge(e2, i + 1)
                    mm = nc.tensor.matmul(PS[:, i, :], mat("head_ones"), tmp[:, i, :], start=True, stop=True)
                mm.then_inc(e3, 1)
                pe.wait_ge(e2, 9)
                for i in range(8):
                    pe.wait_ge(e1, 21 + i)
                    mm = nc.tensor.matmul(PS[:, i, :], mat("head_ones"), tmp[:, i, :], start=True, stop=True)
                mm.then_inc(e3, 1)

        ch = lambda t: t[:, :, :].rearrange("p a (c l) -> p (a c) l", c=NB)
        mid, e_mid, e_end, fac = (small[:, 16 + 32 * i:48 + 32 * i] for i in range(4))
        s1, s2 = sem("decay_vec"), sem("decay_act")
        with nc.Block() as block:
            @block.vector
            def _(dve):
                for i in range(8):
                    for c in range(NB):
                        part = slice(c * P, (c + 1) * P)
                        nc.vector.tensor_tensor_scan(tmp[:, i, part], mat("ones"), sig[:, i, part], 0.0, ALU.mult, ALU.add).then_inc(s1, 1)
                dve.wait_ge(s1, 32)
                nc.vector.tensor_copy(mid.unsqueeze(2), ch(tmp)[:, :, 63:64]).then_inc(s1, 1)
                dve.wait_ge(s1, 33)
                nc.vector.tensor_tensor(ch(tmp), ch(tmp), mid.unsqueeze(2).to_broadcast([P, 32, P]), ALU.subtract).then_inc(s1, 1)
                dve.wait_ge(s1, 34)
                nc.vector.tensor_tensor(ALL(sig), ALL(tmp), ALL(sig), ALU.subtract).then_inc(s1, 1)
                nc.vector.tensor_tensor(ALL(a_), ALL(a_), ALL(kk), ALU.mult).then_inc(s1, 1)
                dve.wait_ge(s1, 36)
                dve.wait_ge(s2, 1)
                nc.vector.scalar_tensor_tensor(out=ALL(kk), in0=ALL(sig), scalar=-1.0, in1=ALL(kk), op0=ALU.mult, op1=ALU.mult).then_inc(s1, 1)
                dve.wait_ge(s2, 2)
                nc.vector.tensor_tensor(ALL(a_), ALL(a_), ALL(sig), ALU.mult).then_inc(s1, 1)
                nc.vector.tensor_tensor(ALL(kx), ALL(kx), ALL(sig), ALU.mult).then_inc(s1, 1)
                dve.wait_ge(s2, 3)
                nc.vector.tensor_tensor(ALL(r), ALL(r), ALL(tmp), ALU.mult).then_inc(s1, 1)
                nc.vector.tensor_copy(e_end.unsqueeze(2), ch(tmp)[:, :, P - 1:P]).then_inc(s1, 1)
                dve.wait_ge(s1, 41)
                dve.wait_ge(s2, 4)
                by_c = lambda t: t.rearrange("p (a c) -> p a c", c=NB)
                nc.vector.tensor_tensor(by_c(fac)[:, :, 0:NB - 1], by_c(e_end)[:, :, 0:NB - 1], by_c(e_mid)[:, :, 1:NB], ALU.mult).then_inc(s1, 1)

            @block.scalar
            def _(act):
                act.wait_ge(s1, 35)
                nc.scalar.activation(ALL(sig), ALL(sig), ACT.Exp, scale=-C0).then_inc(s2, 1)
                act.wait_ge(s1, 37)
                nc.scalar.activation(ALL(sig), ALL(tmp), ACT.Exp, scale=C0).then_inc(s2, 1)
                act.wait_ge(s2, 2)
                nc.scalar.activation(ALL(tmp), ALL(tmp), ACT.Exp, scale=-C0).then_inc(s2, 1)
                nc.scalar.activation(e_mid, mid, ACT.Exp, scale=-C0).then_inc(s2, 1)

        rt, kt, at_, bt = r, kx, kk, a_
        held = flat(sig)
        G, Rb, Rk, Ak = (held[:, i * 1024:(i + 1) * 1024] for i in range(4))
        work = flat(tmp)
        N_, GT, Q = (work[:, i * 1024:(i + 1) * 1024] for i in range(3))
        k_tok, b_tok, v_tok = (aux[:, i * T:(i + 1) * T] for i in range(3))
        W_, U_ = aux[:, 3 * T:4 * T], aux[:, 4 * T:5 * T]
        S_ = [aux[:, 2560 + i * 256:2560 + (i + 1) * 256] for i in range(2)]
        LEVELS = 7
        names = ["grams", "gram_moved", "start_made", "q_made", "q_moved", "g_made", "g_moved", "gt_moved",
                 "turned", "turned_moved", "w_made", "w_moved", "u_made", "u_moved", "y_made", "y_moved", "s_made", "s_moved"]
        (grams, gram_moved, start_made, q_made, q_moved, g_made, g_moved, gt_moved, turned, turned_moved, w_made, w_moved,
         u_made, u_moved, y_made, y_moved, s_made, s_moved) = (sem("wkv_" + n) for n in names)
        s_zero = sem("wkv_state_zeroed")
        with nc.Block() as block:
            @block.vector
            def _(dve):
                nc.vector.memset(aux[:, 2560:3072], 0.0).then_inc(s_zero, 1)
        four = lambda t, g: t[:, g * T:(g + 1) * T].rearrange("p (h l) -> p h l", h=4)
        bank4 = lambda b: PS[:, b, :].rearrange("p (h l) -> p h l", h=4)
        at_group = lambda j: j % 2 * 4 + j // 2
        for u in range(2 * NB):
            c, half = u // 2, u % 2
            t0, t1 = c * P, (c + 1) * P
            S = S_[half]

            def hd_(t, j):
                return t[j % 2 * HD:(j % 2 + 1) * HD, half * 4 + j // 2, t0:t1]

            with nc.Block() as block:
                @block.tensor
                def _(pe):
                    for g in range(2):
                        for bank, l_, r_ in ((g, bt, at_), (2 + g, at_, bt), (4 + g, kt, at_), (6 + g, bt, rt)):
                            for j in range(4):
                                mm = nc.tensor.matmul(PS[:, bank, j * P:(j + 1) * P], hd_(l_, 2 * j + g), hd_(r_, 2 * j + g), start=True, stop=True)
                            mm.then_inc(grams, 1)
                    for g in range(2):
                        pe.wait_ge(gram_moved, 10 * u + 4 * g + 4)
                        for j in range(4):
                            mm = nc.tensor.matmul(PS[:, 6 + g, j * P:(j + 1) * P], hd_(kt, 2 * j + g), hd_(rt, 2 * j + g), start=True, stop=True)
                        mm.then_inc(grams, 1)
                    for l in range(1, LEVELS):
                        n = 2 * ((LEVELS - 1) * u + l - 1)
                        nt = 2 * ((LEVELS - 2) * u + l - 1)
                        for g in range(2):
                            if l == 1:
                                pe.wait_ge(start_made, 6 * u + 3 * g + 3)
                            else:
                                pe.wait_ge(gt_moved, nt - 2 + g + 1)
                            for j in range(4):
                                mm = nc.tensor.matmul(PS[:, g, j * P:(j + 1) * P], four(N_, g)[:, j, :], four(GT, g)[:, j, :], start=True, stop=True)
                            mm.then_inc(q_made, 1)
                        for g in range(2):
                            pe.wait_ge(q_moved, n + g + 1)
                            if l > 1:
                                pe.wait_ge(g_moved, n - 2 + g + 1)
                            for j in range(4):
                                mm = nc.tensor.matmul(PS[:, 2 + g, j * P:(j + 1) * P], four(Q, g)[:, j, :], four(G, g)[:, j, :], start=True, stop=True)
                            if l < LEVELS - 1:
                                for j in range(4):
                                    dst = PS[:, 4 + g, j * P:(j + 1) * P]
                                    nc.tensor.matmul(dst, mat("ident"), four(GT, g)[:, j, :], start=True, stop=False)
                                    mm = nc.tensor.matmul(dst, four(G, g)[:, j, :], four(Q, g)[:, j, :], start=False, stop=True)
                            mm.then_inc(g_made, 1)

                @block.vector
                def _(dve):
                    for g in range(2):
                        for n, (dst, bank, m) in enumerate(((N_, g, "lt"), (GT, 2 + g, "pair0"), (Ak, 4 + g, "lt"), (Rb, 6 + g, "le"))):
                            dve.wait_ge(grams, 10 * u + 4 * g + n + 1)
                            nc.vector.tensor_tensor(four(dst, g), bank4(bank), mat4(m), ALU.mult).then_inc(gram_moved, 1)
                    for g in range(2):
                        dve.wait_ge(grams, 10 * u + 9 + g)
                        nc.vector.tensor_tensor(four(Rk, g), bank4(6 + g), mat4("le"), ALU.mult).then_inc(gram_moved, 1)
                    for l in range(1, LEVELS):
                        n = 2 * ((LEVELS - 1) * u + l - 1)
                        for g in range(2):
                            dve.wait_ge(q_made, n + g + 1)
                            if l > 1:
                                dve.wait_ge(g_made, n - 2 + g + 1)
                            nc.vector.tensor_tensor(four(Q, g), bank4(g), mat4(f"pair{l}"), ALU.mult).then_inc(q_moved, 1)
                        for g in range(2):
                            dve.wait_ge(g_made, n + g + 1)
                            if l > 1:
                                dve.wait_ge(g_moved, n - 2 + g + 1)
                            nc.vector.tensor_tensor(four(G, g), bank4(2 + g), four(G, g), ALU.add).then_inc(g_moved, 1)

                @block.gpsimd
                def _(pool):
                    for g in range(2):
                        pool.wait_ge(gram_moved, 10 * u + 4 * g + 2)
                        nc.gpsimd.tensor_tensor(four(G, g), four(N_, g), mat4("pair0_t"), ALU.mult).then_inc(start_made, 1)
                        nc.gpsimd.tensor_tensor(four(GT, g), four(GT, g), mat4("ident"), ALU.add).then_inc(start_made, 1)
                        pool.wait_ge(start_made, 6 * u + 3 * g + 2)
                        nc.gpsimd.tensor_tensor(four(G, g), four(G, g), mat4("ident"), ALU.add).then_inc(start_made, 1)

                @block.scalar
                def _(act):
                    for l in range(1, LEVELS - 1):
                        n = 2 * ((LEVELS - 1) * u + l - 1)
                        for g in range(2):
                            act.wait_ge(g_made, n + g + 1)
                            if l == 1:
                                act.wait_ge(start_made, 6 * u + 3 * g + 3)
                            nc.scalar.copy(four(GT, g), bank4(4 + g)).then_inc(gt_moved, 1)

            with nc.Block() as block:
                @block.tensor
                def _(pe):
                    for n, t in enumerate((v, kt, bt)):
                        for i in range(4):
                            mm = nc.tensor.transpose(PS[:, n, i * P:(i + 1) * P], t[:, half * 4 + i, t0:t1], mat("ident"))
                        mm.then_inc(turned, 1)
                    pe.wait_ge(turned_moved, 3 * u + 1)
                    for j in range(8):
                        dst = PS[:, 3 + 4 * (j % 2), j // 2 * HD:(j // 2 + 1) * HD]
                        sl = S[j % 2 * HD:(j % 2 + 1) * HD, j // 2 * HD:(j // 2 + 1) * HD]
                        nc.tensor.matmul(dst, hd_(at_, j), sl, start=True, stop=False)
                        mm = nc.tensor.matmul(dst, Ak[:, at_group(j) * P:(at_group(j) + 1) * P], v_tok[:, j * HD:(j + 1) * HD], start=False, stop=True)
                    mm.then_inc(w_made, 1)
                    pe.wait_ge(w_moved, u + 1)
                    for j in range(8):
                        mm = nc.tensor.matmul(PS[:, 4, j * HD:(j + 1) * HD], G[:, j * P:(j + 1) * P], W_[:, j * HD:(j + 1) * HD], start=True, stop=True)
                    mm.then_inc(u_made, 1)
                    pe.wait_ge(u_moved, u + 1)
                    for j in range(8):
                        half_p = slice(j % 2 * HD, (j % 2 + 1) * HD)
                        dst = PS[half_p, 5, j // 2 * P:(j // 2 + 1) * P]
                        hs = slice(j * HD, (j + 1) * HD)
                        gs = slice(at_group(j) * HD, (at_group(j) + 1) * HD)
                        nc.tensor.matmul(dst, S[half_p, j // 2 * HD:(j // 2 + 1) * HD], hd_(rt, j), start=True, stop=False)
                        nc.tensor.matmul(dst, v_tok[:, hs], Rk[:, at_group(j) * P:(at_group(j) + 1) * P], start=False, stop=False)
                        mm = nc.tensor.matmul(dst, U_[:, gs], Rb[:, at_group(j) * P:(at_group(j) + 1) * P], start=False, stop=True)
                    mm.then_inc(y_made, 1)
                    if c < NB - 1:
                        pe.wait_ge(turned_moved, 3 * u + 3)
                        for j in range(8):
                            half_p = slice(j % 2 * HD, (j % 2 + 1) * HD)
                            dst = PS[half_p, 6, j // 2 * HD:(j // 2 + 1) * HD]
                            hs = slice(j * HD, (j + 1) * HD)
                            gs = slice(at_group(j) * HD, (at_group(j) + 1) * HD)
                            nc.tensor.matmul(dst, b_tok[:, hs], U_[:, gs], start=True, stop=False)
                            mm = nc.tensor.matmul(dst, k_tok[:, hs], v_tok[:, hs], start=False, stop=True)
                        mm.then_inc(s_made, 1)

                @block.scalar
                def _(act):
                    for n, dst in enumerate((v_tok, k_tok, b_tok)):
                        act.wait_ge(turned, 3 * u + n + 1)
                        nc.scalar.copy(dst, PS[:, n, :]).then_inc(turned_moved, 1)
                    act.wait_ge(y_made, u + 1)
                    nc.scalar.copy(rt[:, half * 4:half * 4 + 4, t0:t1], bank4(5)).then_inc(y_moved, 1)

                @block.vector
                def _(dve):
                    dve.wait_ge(w_made, u + 1)
                    nc.vector.tensor_copy(W_.rearrange("p (g w) -> p g w", g=2), PS[:, 3:8:4, 0:256]).then_inc(w_moved, 1)
                    dve.wait_ge(u_made, u + 1)
                    nc.vector.tensor_copy(U_, PS[:, 4, :]).then_inc(u_moved, 1)
                    if c < NB - 1:
                        dve.wait_ge(s_made, u + 1)
                        nc.vector.tensor_tensor(S, S, PS[:, 6, 0:256], ALU.add).then_inc(s_moved, 1)
                        dve.wait_ge(s_moved, 2 * u + 1)
                        fv = fac.rearrange("p (a c) -> p a c", c=NB)[:, half * 4:half * 4 + 4, c:c + 1].to_broadcast([P, 4, HD])
                        sv = S.rearrange("p (a v) -> p a v", a=4)
                        nc.vector.tensor_tensor(sv, sv, fv, ALU.mult).then_inc(s_moved, 1)
        checkpoint("wkv", ALL(r))

        yy, sq = r, tmp
        n1, n2, n3 = sem("gn_vec"), sem("gn_act"), sem("gn_sums")
        with nc.Block() as block:
            @block.tensor
            def _(pe):
                for i in range(8):
                    mm = nc.tensor.matmul(PS[:, i, :], mat("head_ones"), yy[:, i, :], start=True, stop=True)
                mm.then_inc(n3, 1)
                pe.wait_ge(n2, 1)
                for i in range(8):
                    mm = nc.tensor.matmul(PS[:, i, :], mat("head_ones"), sq[:, i, :], start=True, stop=True)
                mm.then_inc(n3, 1)

            @block.vector
            def _(dve):
                nc.vector.memset(small[:, 250:251], 64e-5).then_inc(n1, 1)
                dve.wait_ge(n3, 1)
                nc.vector.scalar_tensor_tensor(out=ALL(yy), in0=PS[:, :, :], scalar=-1.0 / HD, in1=ALL(yy), op0=ALU.mult, op1=ALU.add).then_inc(n1, 1)
                dve.wait_ge(n2, 2)
                nc.vector.reciprocal(ALL(sig), ALL(sig)).then_inc(n1, 1)
                dve.wait_ge(n1, 3)
                nc.vector.tensor_tensor(ALL(yy), ALL(yy), ALL(sig), ALU.mult).then_inc(n1, 1)
                dve.wait_ge(n1, 4)
                for i in range(8):
                    nc.vector.tensor_scalar(yy[:, i, :], yy[:, i, :], col("lnx_g", i), col("lnx_b", i), ALU.mult, ALU.add).then_inc(n1, 1)
                dve.wait_ge(n1, 12)
                nc.vector.tensor_tensor(ALL(yy), ALL(yy), ALL(bonus), ALU.add).then_inc(n1, 1)

            @block.scalar
            def _(act):
                act.wait_ge(n1, 2)
                nc.scalar.activation(ALL(sq), ALL(yy), ACT.Square).then_inc(n2, 1)
                act.wait_ge(n3, 2)
                nc.scalar.activation(ALL(sig), PS[:, :, :], ACT.Sqrt, scale=1.0 / HD, bias=small[:, 250:251]).then_inc(n2, 1)

        differences(F[2])
        g2_ = [flat(F[4])[0:80, i * D:(i + 1) * D] for i in range(2)]
        hid_g = [flat(F[4])[0:80, 2 * D + i * T:2 * D + (i + 1) * T] for i in range(2)]
        loads("g2_loaded", [(g2_[0], A["w_g2"][0:80, :]), (g2_[1], A["w_g2"][80:160, :])])
        gemm("lora_g", 2, 8, rows(F[3]), {"act": lambda e, n, b: nc.scalar.activation(hid_g[n], b, ACT.Sigmoid)}, n_cols=80,
             prepare=mixed(F[3], F[2], 5))
        lora_out("gate7", [(g2_[0], hid_g[0]), (g2_[1], hid_g[1])],
                 {"dve": lambda e, n, b: nc.vector.tensor_tensor(yy[:, n, :], yy[:, n, :], b, ALU.mult)})

        def add_to_x(e, n, b):
            return nc.vector.scalar_tensor_tensor(out=x[:, n, :], in0=x[:, n, :], scalar=ALPHA, in1=b, op0=ALU.mult, op1=ALU.add)

        def layer_norm(layer, which):
            i0 = (2 * layer + which) * 8
            norm(f"ln{layer}{which}", rows(x), 8, D, 1e-5, lambda i: col("ln_g", i0 + i), rows(x), centered=True,
                 bias=lambda i: col("ln_b", i0 + i), scratch=rows(F[8]))

        def ffn(layer):
            hid = lambda i: F[1 + i // 8][:, i % 8, :]
            tile_of = lambda n: n // 2 + n % 2 * FT
            conv_gemm(f"up{layer}", 2 * FT, rows(x), 3,
                      lambda n, j: col("ffn_conv_w", (layer * 3 + j) * 2 * FT + tile_of(n)),
                      lambda n: col("ffn_conv_b", layer * 2 * FT + tile_of(n)),
                      lambda n: F[8][:, n // 2 % 2, :] if n % 2 else hid(n // 2), pair_out=hid)
            gemm(f"down{layer}", 8, FT, hid, {"dve": add_to_x})
            layer_norm(layer, 1)

        gemm("w_o", 8, 8, rows(yy), {"dve": add_to_x})
        layer_norm(0, 0)
        checkpoint("x2", ALL(x))
        ffn(0)
        checkpoint("x3", ALL(x))
        end_section()

        low = F[1]
        c_q, c_kv, k_idx = rows(low), low[:, 2, :], low[:, 3, :]
        gemm("d_in", 4, 8, rows(x), {"act": copy_act(rows(low))})
        w_idx = small[:, 144:176]
        w_idx_taken = sem("w_idx_taken")
        first = at["used"]
        with nc.Block() as block:
            @block.tensor
            def _(pe):
                w = next_chunk(pe)
                for b in range(NB):
                    for k in range(8):
                        mm = nc.tensor.matmul(PS[:, 0, b * 8:(b + 1) * 8], x[:, k, b * P:(b + 1) * P], w[:, k * 8:(k + 1) * 8], start=k == 0, stop=k == 7)
                mm.then_inc(weight_used, 1)

            @block.vector
            def _(dve):
                dve.wait_ge(weight_used, first + 1)
                nc.vector.tensor_scalar(w_idx, PS[:, 0, 0:32], 8 ** -0.5 * 64 ** -0.5, None, ALU.mult).then_inc(w_idx_taken, 1)

            @block.sync
            def _(sp):
                stream(sp)
        norm("norm_cq", c_q, 2, 256, 1e-6, lambda i: col("q_norm_g", i), c_q, scratch=rows(F[8]))
        norm("norm_ckv", lambda i: c_kv, 1, P, 1e-6, lambda i: col("kv_norm_g", 0), lambda i: c_kv, scratch=rows(F[8]))
        norm("norm_kidx", lambda i: k_idx, 1, HD, 1e-5, lambda i: col("kidx_g", 0), lambda i: k_idx, centered=True,
             bias=lambda i: col("kidx_b", 0), scratch=rows(F[8]), ones="head_ones")
        qd, qi = F[2], F[3]
        gemm("d_uq", 8, 2, c_q, {"act": lambda e, n, b: nc.scalar.mul(qd[:, n, :], b, HD ** -0.5)})
        gemm("d_qidx", 4, 2, c_q, {"dve": copy_dve(rows(qi))})

        f8 = flat(F[8])
        uk, uv = f8[:, 0:1024], f8[:, 1024:2048]
        qabs = [f8[:, 2048 + i * T:2048 + (i + 1) * T] for i in range(2)]
        lg = [flat(F[3])[:, 1280 + i * SB_N:1280 + (i + 1) * SB_N] for i in range(2)]
        rb, oneh, band = flat(F[7])[0:32, 0:16], flat(F[7])[0:32, 512:512 + BAND], flat(F[7])[0:16, 2048:2048 + BAND]
        loads("dsa_loaded", [(rb, A["rel_bias"]), (oneh, A["bucket1h"]), (uk, A["d_uk"]), (uv, A["d_uv"])])
        band_dram = nc.dram_tensor("band", (H, BAND), f32, kind="Internal")
        toep = [F[5], F[6]]
        band_made, band_taken, band_stored, toep_loaded = sem("band_made"), sem("band_taken"), sem("band_stored"), sem("toeplitz_loaded")
        ckv_tok = aux[:, 0:T]
        tok_made, tok_taken = sem("ckv_tok_made"), sem("ckv_tok_taken")
        with nc.Block() as block:
            @block.tensor
            def _(pe):
                nc.tensor.matmul(PS[0:16, 0, :], rb, oneh[:, 0:T], start=True, stop=True)
                nc.tensor.matmul(PS[0:16, 1, 0:P], rb, oneh[:, T:BAND], start=True, stop=True).then_inc(band_made, 1)
                for b in range(NB):
                    mm = nc.tensor.transpose(PS[:, 2, b * P:(b + 1) * P], low[:, 2, b * P:(b + 1) * P], mat("ident"))
                mm.then_inc(tok_made, 1)

            @block.scalar
            def _(act):
                act.wait_ge(band_made, 1)
                nc.scalar.copy(band, PS[0:16, 0:2, :].rearrange("p a b -> p (a b)")[:, 0:BAND]).then_inc(band_taken, 1)
                act.wait_ge(tok_made, 1)
                nc.scalar.copy(ckv_tok, PS[:, 2, :]).then_inc(tok_taken, 1)

            @block.sync
            def _(sp):
                sp.wait_ge(band_taken, 1)
                sp.dma_start(band_dram.ap(), band).then_inc(band_stored, 16)
                sp.wait_ge(band_stored, 16)
                for i in range(2):
                    src = bass.AP(band_dram, i * 8 * BAND, [[1, P], [BAND, 8], [1, T]])
                    sp.dma_start(toep[i][:, :, :], src).then_inc(toep_loaded, 16)
                stream(sp)

        mask, left = F[4], lambda b: F[4][:, 4 + b, :]
        best = small[:, 176:208]
        rel = [F[7][:, i, :] for i in range(8)]
        sc_made, sc_relu, sc_added, select = sem("index_scores_made"), sem("index_relu"), sem("index_added"), sem("selected")
        with nc.Block() as block:
            @block.tensor
            def _(pe):
                for b in range(1, NB):
                    n = (b + 1) * P
                    for i in range(8):
                        half_p = slice(i % 2 * HD, (i % 2 + 1) * HD)
                        if b > 1:
                            pe.wait_ge(sc_relu, 8 * (b - 2) + i + 1)
                        nc.tensor.matmul(PS[:, i, 0:n], qi[half_p, i // 2, b * P:(b + 1) * P], low[half_p, 3, 0:n], start=True, stop=True).then_inc(sc_made, 1)

            @block.scalar
            def _(act):
                for b in range(1, NB):
                    n = (b + 1) * P
                    for i in range(8):
                        act.wait_ge(sc_made, 8 * (b - 1) + i + 1)
                        if b > 1:
                            act.wait_ge(sc_added, 9 * (b - 2) + i + 1)
                        nc.scalar.activation(rel[i][:, 0:n], PS[:, i, 0:n], ACT.Relu).then_inc(sc_relu, 1)

            @block.vector
            def _(dve):
                for b in range(1, NB):
                    n = (b + 1) * P
                    for i in range(8):
                        dve.wait_ge(sc_relu, 8 * (b - 1) + i + 1)
                        wcol = w_idx[:, b * 8 + i:b * 8 + i + 1]
                        if i == 0:
                            nc.vector.tensor_scalar(left(b)[:, 0:n], rel[i][:, 0:n], wcol, None, ALU.mult).then_inc(sc_added, 1)
                        else:
                            dve.wait_ge(sc_added, 9 * (b - 1) + i)
                            nc.vector.scalar_tensor_tensor(out=left(b)[:, 0:n], in0=rel[i][:, 0:n], scalar=wcol, in1=left(b)[:, 0:n],
                                                           op0=ALU.mult, op1=ALU.add).then_inc(sc_added, 1)
                    dve.wait_ge(sc_added, 9 * (b - 1) + 8)
                    nc.vector.tensor_tensor(left(b)[:, b * P:n], left(b)[:, b * P:n], mat("neg_after"), ALU.add).then_inc(sc_added, 1)
                dve.wait_ge(sc_added, 27)
                for k in range(TOPK // 8):
                    for b in range(1, NB):
                        if k:
                            dve.wait_ge(select, 6 * k - 3 + b)
                        nc.vector.max(out=best[:, 8 * b:8 * b + 8], in_=left(b)[:, 0:(b + 1) * P]).then_inc(select, 1)
                    for b in range(1, NB):
                        dve.wait_ge(select, 6 * k + b)
                        nc.vector.match_replace(out=left(b)[:, 0:(b + 1) * P], in_to_replace=best[:, 8 * b:8 * b + 8],
                                                in_values=left(b)[:, 0:(b + 1) * P], imm_value=TAKEN).then_inc(select, 1)
                dve.wait_ge(select, 6 * (TOPK // 8))
                for b in range(1, NB):
                    n = (b + 1) * P
                    nc.vector.tensor_scalar(mask[:, b, 0:n], left(b)[:, 0:n], TAKEN / 2, NEG, ALU.is_ge, ALU.mult).then_inc(select, 1)
                nc.vector.tensor_copy(mask[:, 0, 0:P], mat("neg_after")).then_inc(select, 1)

            @block.sync
            def _(sp):
                sp.wait_ge(toep_loaded, 32)

        LG_BANK = [(2, 0), (3, 0), (2, P), (4, 0)]
        L_AT = [0, P, 3 * P, 6 * P]
        att = F[7]
        pt_ = aux[:, T:T + SB_N]
        olat = aux[:, 1792:2304]
        mx, sm = small[:, 208:216], small[:, 216:224]
        nmx, rs = small[:, 224:232], small[:, 232:240]
        names = ["qabs_made", "qabs_moved", "logits_made", "masked", "negated", "exped", "inverted", "scaled", "turned",
                 "turned_moved", "olat_made", "olat_moved", "o_made", "o_moved"]
        (qa_made, qa_moved, lg_made, lg_masked, negated, exped, inverted, scaled, pt_made, pt_moved, ol_made, ol_moved,
         oo_made, oo_moved) = (sem("dsa_" + n) for n in names)
        with nc.Block() as block:
            @block.tensor
            def _(pe):
                def absorb(hh):
                    half_p = slice(hh % 2 * HD, (hh % 2 + 1) * HD)
                    if hh:
                        pe.wait_ge(qa_moved, hh)
                    if hh >= 2:
                        pe.wait_ge(oo_moved, hh - 1)
                    nc.tensor.matmul(PS[:, 0, :], uk[half_p, hh // 2 * P:(hh // 2 + 1) * P], qd[half_p, hh // 2, :], start=True, stop=True).then_inc(qa_made, 1)

                def logits(hh):
                    pe.wait_ge(qa_moved, hh + 1)
                    if hh:
                        pe.wait_ge(lg_masked, 4 * hh)
                    for b in range(NB):
                        n = (b + 1) * P
                        bank, at0 = LG_BANK[b]
                        dst = PS[:, bank, at0:at0 + n]
                        nc.tensor.matmul(dst, qabs[hh % 2][:, b * P:(b + 1) * P], low[:, 2, 0:n], start=True, stop=False)
                        mm = nc.tensor.matmul(dst, mat("flip"), toep[hh // 8][:, hh % 8, T - n:T], start=False, stop=True)
                    mm.then_inc(lg_made, 1)

                absorb(0)
                logits(0)
                for hh in range(H):
                    if hh + 1 < H:
                        absorb(hh + 1)
                        logits(hh + 1)
                    pe.wait_ge(scaled, 4 * hh + 4)
                    if hh:
                        pe.wait_ge(pt_moved, 2 * hh)
                    for i in range(NB):
                        for b in range(i, NB):
                            at0 = SB_AT[i] + (b - i) * P
                            mm = nc.tensor.transpose(PS[:, 5 + at0 // T, at0 % T:at0 % T + P], lg[hh % 2][:, L_AT[b] + i * P:L_AT[b] + (i + 1) * P], mat("ident"))
                    mm.then_inc(pt_made, 1)
                    pe.wait_ge(pt_moved, 2 * hh + 2)
                    if hh:
                        pe.wait_ge(ol_moved, hh)
                    for i in range(NB):
                        mm = nc.tensor.matmul(PS[:, 1, i * P:T], ckv_tok[:, i * P:(i + 1) * P], pt_[:, SB_AT[i]:SB_AT[i] + SB_W[i]],
                                              start=i == 0, stop=i == NB - 1)
                    mm.then_inc(ol_made, 1)
                    pe.wait_ge(ol_moved, hh + 1)
                    if hh + 1 < H:
                        pe.wait_ge(qa_moved, hh + 2)
                    half_p = slice(hh % 2 * HD, (hh % 2 + 1) * HD)
                    nc.tensor.matmul(PS[half_p, 0, :], uv[:, hh * HD:(hh + 1) * HD], olat, start=True, stop=True).then_inc(oo_made, 1)

            @block.vector
            def _(dve):
                for hh in range(H):
                    p = hh % 2
                    dve.wait_ge(lg_made, hh + 1)
                    if hh >= 2:
                        dve.wait_ge(pt_made, hh - 1)
                    for b in range(NB):
                        n = (b + 1) * P
                        bank, at0 = LG_BANK[b]
                        nc.vector.tensor_tensor_reduce(out=lg[p][:, L_AT[b]:L_AT[b] + n], in0=PS[:, bank, at0:at0 + n], in1=mask[:, b, 0:n],
                                                       scale=1.0, scalar=-3e38, op0=ALU.add, op1=ALU.max,
                                                       accum_out=mx[:, 4 * p + b:4 * p + b + 1]).then_inc(lg_masked, 1)
                    dve.wait_ge(lg_masked, 4 * hh + 4)
                    nc.vector.tensor_scalar(nmx[:, 4 * p:4 * p + 4], mx[:, 4 * p:4 * p + 4], -1.0, None, ALU.mult).then_inc(negated, 1)
                    dve.wait_ge(exped, 4 * hh + 4)
                    nc.vector.reciprocal(rs[:, 4 * p:4 * p + 4], sm[:, 4 * p:4 * p + 4]).then_inc(inverted, 1)
                    dve.wait_ge(inverted, hh + 1)
                    for b in range(NB):
                        part = lg[p][:, L_AT[b]:L_AT[b] + (b + 1) * P]
                        nc.vector.tensor_scalar(part, part, rs[:, 4 * p + b:4 * p + b + 1], None, ALU.mult).then_inc(scaled, 1)
                    dve.wait_ge(pt_made, hh + 1)
                    if hh:
                        dve.wait_ge(ol_made, hh)
                    nc.vector.tensor_copy(pt_[:, 0:2 * T], PS[:, 5:7, :].rearrange("p a b -> p (a b)")).then_inc(pt_moved, 1)
                    nc.vector.tensor_copy(pt_[:, 2 * T:SB_N], PS[:, 7, 0:SB_N - 2 * T]).then_inc(pt_moved, 1)

            @block.scalar
            def _(act):
                def absorbed(hh):
                    act.wait_ge(qa_made, hh + 1)
                    if hh >= 2:
                        act.wait_ge(lg_made, hh - 1)
                    nc.scalar.copy(qabs[hh % 2], PS[:, 0, :]).then_inc(qa_moved, 1)
                absorbed(0)
                for hh in range(H):
                    p = hh % 2
                    if hh + 1 < H:
                        absorbed(hh + 1)
                    act.wait_ge(negated, hh + 1)
                    if hh >= 2:
                        act.wait_ge(inverted, hh - 1)
                    for b in range(NB):
                        part = lg[p][:, L_AT[b]:L_AT[b] + (b + 1) * P]
                        nc.scalar.activation(part, part, ACT.Exp, bias=nmx[:, 4 * p + b:4 * p + b + 1],
                                             accum_out=sm[:, 4 * p + b:4 * p + b + 1]).then_inc(exped, 1)
                    act.wait_ge(ol_made, hh + 1)
                    if hh:
                        act.wait_ge(oo_made, hh)
                    nc.scalar.copy(olat, PS[:, 1, :]).then_inc(ol_moved, 1)
                    act.wait_ge(oo_made, hh + 1)
                    half_p = slice(hh % 2 * HD, (hh % 2 + 1) * HD)
                    nc.scalar.copy(att[half_p, hh // 2, :], PS[half_p, 0, :]).then_inc(oo_moved, 1)

        gemm("d_wo", 8, 8, rows(att), {"dve": add_to_x})
        layer_norm(1, 0)
        checkpoint("x4", ALL(x))
        ffn(1)

        with nc.Block() as block:
            @block.sync
            def _(sp):
                sp.dma_start(out, ALL(x)).then_inc(stored, 16)
                sp.wait_ge(stored, 16)


def weight_tiles(w, n_cols=P):
    k, n = w.shape
    return np.ascontiguousarray(w.reshape(k // P, P, n // n_cols, n_cols).transpose(2, 1, 0, 3).reshape(n // n_cols, P, -1))


def columns(v):
    return np.ascontiguousarray(v).reshape(-1, P).T


def lay_out(i):
    row = lambda v: np.broadcast_to(v.reshape(1, -1), (P, v.size))
    c = {"c": columns(i["c"]), "b_ada": columns(i["b_ada"]), "norm_in_gain": columns(i["norm_in_gain"]),
         "conv_w": columns(i["conv_w"][0]), "conv_b": columns(i["conv_b"]), "d_skip": columns(np.repeat(i["d_skip"], HD)),
         "sb_norm_gain": columns(i["sb_norm_gain"]), "ssm_norm_gain": columns(i["ssm_norm_gain"]),
         "norm_f_gain": columns(i["norm_f_gain"]), "dt_bias": row(i["dt_bias"]), "a_log": row(i["a_log"]),
         "ln_g": columns(i["ln_g_2"]), "ln_b": columns(i["ln_b_2"]), "mix": columns(i["rwkv_mix_2"]),
         "w0": columns(i["rwkv_w0_2"]), "a0": columns(i["rwkv_a0_2"]), "k_k": columns(i["rwkv_k_k_2"]),
         "k_a": columns(i["rwkv_k_a_2"]), "r_k": columns(i["rwkv_r_k_2"]), "lnx_g": columns(i["rwkv_lnx_g_2"]),
         "lnx_b": columns(i["rwkv_lnx_b_2"]), "q_norm_g": columns(i["dsa_q_norm_g_2"]),
         "kv_norm_g": columns(i["dsa_kv_norm_g_2"]), "kidx_g": columns(np.tile(i["dsa_kidx_g_2"][0], 2)),
         "kidx_b": columns(np.tile(i["dsa_kidx_b_2"][0], 2)),
         "ffn_conv_w": columns(i["ffn_conv_w_2"]), "ffn_conv_b": columns(i["ffn_conv_b_2"])}
    w_in = i["w_in"][0]
    d_in = i["dsa_w_in_2"][0]
    at = D_XBC0 = 4096 + 1536
    a = {"xT": np.ascontiguousarray(i["x"][0].T.reshape(KT, P, T).transpose(1, 0, 2)),
         "cols": np.ascontiguousarray(np.concatenate([c[n] for n, _ in COLS], axis=1)),
         "squares": square_constants(), "late": late_constant(), "bucket1h": bucket_constant(),
         "w_ada": weight_tiles(i["w_ada"][0]),
         "w_in": weight_tiles(np.concatenate([w_in[:, :at], w_in[:, at + 16:]], axis=1)),
         "w_dt": weight_tiles(w_in[:, at:at + 16], 16), "w_out": weight_tiles(i["w_out"][0]),
         "w_rkv": np.concatenate([weight_tiles(w) for w in i["rwkv_w_rkv_2"][0]]),
         "w_w1": weight_tiles(i["rwkv_w1_2"][0], 64), "w_a1": weight_tiles(i["rwkv_a1_2"][0], 64),
         "w_g1": weight_tiles(i["rwkv_g1_2"][0], 80), "w_w2": i["rwkv_w2_2"][0], "w_a2": i["rwkv_a2_2"][0],
         "w_g2": i["rwkv_g2_2"][0], "w_o": weight_tiles(i["rwkv_w_o_2"][0]),
         "d_in": weight_tiles(np.concatenate([d_in[:, :384], d_in[:, 384:448], d_in[:, 384:448]], axis=1)),
         "d_widx": weight_tiles(d_in[:, 448:456], 8),
         "d_uq": weight_tiles(i["dsa_w_uq_2"][0]), "d_uk": i["dsa_w_uk_2"][0].reshape(H // 2, P, P).transpose(1, 0, 2).reshape(P, -1),
         "d_uv": i["dsa_w_uv_2"][0].transpose(1, 0, 2).reshape(P, -1), "d_qidx": weight_tiles(i["dsa_w_qidx_2"][0]),
         "d_wo": weight_tiles(i["dsa_w_o_2"][0]), "rel_bias": i["rel_bias_2"]}
    for l in range(2):
        a[f"up{l}"] = weight_tiles(i["ffn_w_up_2"][l])
        a[f"down{l}"] = weight_tiles(i["ffn_w_down_2"][l])
    return {n: np.ascontiguousarray(v) for n, v in a.items()}


def kernel(**inputs):
    import concourse.bacc as bacc
    from concourse.bass_utils import run_bass_kernel_spmd

    arrays = lay_out({n: np.asarray(v) for n, v in inputs.items()})
    nc = bacc.Bacc("TRN2", target_bir_lowering=False, num_devices=1)
    dram = {n: nc.dram_tensor("in_" + n, a.shape, mybir.dt.float32, kind="ExternalInput").ap() for n, a in arrays.items()}
    out = nc.dram_tensor("out", (P, KT, T), mybir.dt.float32, kind="ExternalOutput").ap()
    program(nc, dram, out)
    r = run_bass_kernel_spmd(nc, [{"in_" + n: a for n, a in arrays.items()}], core_ids=[0])
    got = r.results[0]["out"]
    return np.ascontiguousarray(got.transpose(1, 0, 2).reshape(D, T).T).reshape(1, T, D)
```

```python
import numpy as np
import concourse.bass as bass
from concourse import mybir
from contextlib import ExitStack

P = 128
T = 512
D = 1024
KT = D // P
NB = T // P
HD = 64
H = D // HD
D_SSM = 1024
XBC_T = 12
D_FF = 2816
FT = D_FF // P
BUCKETS = 32
TOPK = min(256, T // 4)
RING = 6
CHUNK = 8 * P
ALPHA = 4 ** 0.25
NEG = -1e30
C0 = float(np.exp(-0.5))
BAND = T + P
TAKEN = -3e38

SB_W = [T - P * i for i in range(NB)]
SB_AT = [0, 512, 1024, 896]
SB_N = 1280

COLS = [("c", 8), ("b_ada", 24), ("norm_in_gain", 8), ("conv_w", 48), ("conv_b", 12), ("d_skip", 8),
        ("sb_norm_gain", 8), ("ssm_norm_gain", 8), ("norm_f_gain", 8), ("dt_bias", 16), ("a_log", 16),
        ("ln_g", 32), ("ln_b", 32), ("mix", 48), ("w0", 8), ("a0", 8), ("k_k", 8), ("k_a", 8),
        ("r_k", 8), ("lnx_g", 8), ("lnx_b", 8), ("q_norm_g", 2), ("kv_norm_g", 1), ("kidx_g", 1),
        ("kidx_b", 1), ("ffn_conv_w", 2 * 3 * 2 * FT), ("ffn_conv_b", 2 * 2 * FT)]
COL_AT = {}
_n = 0
for _name, _w in COLS:
    COL_AT[_name] = _n
    _n += _w
N_COLS = _n

MATS = ["ident", "ones", "head_ones", "lt", "le", "gt", "neg_ge", "neg_ones", "flip", "neg_after"] + [f"pair{i}" for i in range(7)] + ["pair0_t"]
MAT_AT = {m: i for i, m in enumerate(MATS)}


def square_constants():
    p, f = np.arange(P)[:, None], np.arange(P)[None, :]
    out = {"ident": p == f, "ones": p >= 0 * f, "head_ones": p // HD == f // HD, "lt": p < f, "le": p <= f,
           "gt": p > f, "neg_ge": -1.0 * (p >= f), "neg_ones": -1.0 * (p >= 0 * f),
           "flip": p + f == P - 1, "neg_after": np.where(f > p, NEG, 0)}
    for i in range(7):
        out[f"pair{i}"] = (p >> (i + 1) == f >> (i + 1)) & (((p >> i) & 1) == 1) & (((f >> i) & 1) == 0)
    out["pair0_t"] = out["pair0"].T
    return np.concatenate([np.asarray(out[m], np.float32) for m in MATS], axis=1)


def late_constant():
    out = np.zeros((P, SB_N), np.float32)
    p, f = np.arange(P)[:, None], np.arange(P)[None, :]
    for i in range(NB):
        out[:, SB_AT[i]:SB_AT[i] + P] = np.where(p >= f, NEG, 0)
    return out


def bucket_constant():
    n = np.maximum(T - 1 - np.arange(BAND), 0)
    nf = np.maximum(n, 1).astype(np.float32)
    large = 16 + (np.log(nf / 16) / np.log(128 / 16) * 16).astype(np.int32)
    b = np.where(n < 16, n, np.minimum(large, BUCKETS - 1))
    return (np.arange(BUCKETS)[:, None] == b[None, :]).astype(np.float32)


def head_selectors():
    channel, head = np.arange(D)[:, None] // HD, np.arange(H)[None, :]
    one = (channel == head).astype(np.float32)
    return one.reshape(KT, P, H).transpose(1, 0, 2).reshape(P, KT * H), one.T


ORDER = ["xT", "cols", "squares", "late", "bucket1h", "w_ada", "w_in", "w_dt", "w_out", "w_rkv", "w_w1", "w_a1",
         "w_g1", "w_w2", "w_a2", "w_g2", "w_o", "d_in", "d_uq", "d_widx", "d_uk", "d_uv", "d_qidx", "d_wo", "rel_bias",
         "up0", "up1", "down0", "down1"]


def program(nc, A, out, stop=None, dump=None):
    f32 = mybir.dt.float32
    ALU = mybir.AluOpType
    ACT = mybir.ActivationFunctionType
    AX = mybir.AxisListType.X
    ctx = ExitStack()
    assert TOPK == P

    def sb(name, shape):
        return ctx.enter_context(nc.sbuf_tensor(name, shape, f32))

    section = []

    def sem(name):
        section.append(nc.alloc_semaphore(name))
        return section[-1]

    def end_section():
        nc.clear_and_free_semaphores(section)
        section.clear()
        nc.all_engine_barrier()

    with ctx:
        F = [sb(f"act{i}", [P, KT, T]) for i in range(9)]
        ring = sb("weight_ring", [P, RING, CHUNK])
        cols = sb("cols", [P, N_COLS])
        squares = sb("squares", [P, len(MATS) * P])
        small = sb("small", [P, 256])
        mod = sb("mod", [P, 24])
        stat = sb("stat", [P, 2, T])
        stat_t = stat
        PS = ctx.enter_context(nc.psum_tensor("banks", [P, 8, T], f32))
        late = sb("late", [P, SB_N])
        aux = sb("aux", [P, 3584])

        def col(name, i):
            return cols[:, COL_AT[name] + i:COL_AT[name] + i + 1]

        def mat(name):
            return squares[:, MAT_AT[name] * P:MAT_AT[name] * P + P]

        def mat4(name):
            return mat(name).unsqueeze(1).to_broadcast([P, 4, P])

        plan = []

        def planned(array, n_tiles, k_tiles, n_cols=P):
            for n in n_tiles:
                for k in range(0, k_tiles, 8):
                    w = min(8, k_tiles - k)
                    plan.append((array[n, :, k * n_cols:(k + w) * n_cols], w * n_cols))

        planned(A["w_ada"], range(24), 8)
        planned(A["w_in"], range(32), 8)
        planned(A["w_in"], range(32, 44), 8)
        planned(A["w_dt"], range(1), 8, 16)
        planned(A["w_in"], range(44, 52), 8)
        planned(A["w_out"], range(8), 16)
        planned(A["w_rkv"], range(24), 8)
        planned(A["w_w1"], range(1), 8, 64)
        planned(A["w_a1"], range(1), 8, 64)
        planned(A["w_g1"], range(2), 8, 80)
        planned(A["w_o"], range(8), 8)
        planned(A["up0"], [i + j * FT for i in range(FT) for j in range(2)], 8)
        planned(A["down0"], range(8), FT)
        planned(A["d_in"], range(4), 8)
        planned(A["d_widx"], range(1), 8, 8)
        planned(A["d_uq"], range(8), 2)
        planned(A["d_qidx"], range(4), 2)
        planned(A["d_wo"], range(8), 8)
        planned(A["up1"], [i + j * FT for i in range(FT) for j in range(2)], 8)
        planned(A["down1"], range(8), FT)
        weight_loaded = [nc.alloc_semaphore(f"weight_loaded{i}") for i in range(RING)]
        weight_used = nc.alloc_semaphore("weight_used")
        stored = nc.alloc_semaphore("out_stored")
        at = {"issued": 0, "used": 0}

        def next_chunk(pe):
            i = at["used"]
            pe.wait_ge(weight_loaded[i % RING], 16 * (i // RING + 1))
            at["used"] += 1
            return ring[:, i % RING, :]

        def col_k(name, i):
            return cols[:, COL_AT[name] + i:COL_AT[name] + i + 1]

        def gemm(name, n_tiles, k_tiles, rhs, evac, n_cols=P, prepare=None):
            per = -(-k_tiles // 8)
            first = at["used"]
            names = list(evac)
            taken = {e: sem(name + "_taken_by_" + e) for e in names}
            who = lambda n: names[n % len(names)]
            nth = lambda n: n // len(names) + 1
            prepared = sem(name + "_prepared") if prepare else None
            with nc.Block() as block:
                @block.tensor
                def _(pe):
                    for n in range(n_tiles):
                        if n >= 4:
                            pe.wait_ge(taken[who(n - 4)], nth(n - 4))
                        for k in range(k_tiles):
                            if k % 8 == 0:
                                w = next_chunk(pe)
                            if prepare and n == 0:
                                pe.wait_ge(prepared, k + 1)
                            mm = nc.tensor.matmul(PS[0:n_cols, n % 4, :], w[:, k % 8 * n_cols:(k % 8 + 1) * n_cols],
                                                  rhs(k), start=k == 0, stop=k == k_tiles - 1)
                            if k % 8 == 7 or k == k_tiles - 1:
                                mm.then_inc(weight_used, 1)

                def run(e, eng):
                    for n in range(n_tiles):
                        if who(n) == e:
                            eng.wait_ge(weight_used, first + per * (n + 1))
                            evac[e](eng, n, PS[0:n_cols, n % 4, :]).then_inc(taken[e], 1)

                if "act" in evac:
                    @block.scalar
                    def _(act):
                        run("act", act)
                if "dve" in evac or prepare:
                    @block.vector
                    def _(dve):
                        if prepare:
                            for k in range(k_tiles):
                                prepare(k).then_inc(prepared, 1)
                        run("dve", dve)

                @block.sync
                def _(sp):
                    stream(sp)

        def stream(sp):
            while at["issued"] < min(len(plan), at["used"] + RING):
                i = at["issued"]
                src, w = plan[i]
                if i >= RING:
                    sp.wait_ge(weight_used, i - RING + 1)
                sp.dma_start(ring[:, i % RING, 0:w], src).then_inc(weight_loaded[i % RING], 16)
                at["issued"] += 1

        def norm(name, x, n_tiles, n_channels, eps, gain, write, centered=False, bias=None, scratch=None):
            summed, squared = sem(name + "_summed"), sem(name + "_squared")
            step, shifted, rooted = sem(name + "_step"), sem(name + "_shifted"), sem(name + "_rooted")
            sq = scratch
            sums = 1 if centered else 0
            before = n_tiles if centered else 0
            with nc.Block() as block:
                @block.tensor
                def _(pe):
                    if centered:
                        for i in range(n_tiles):
                            mm = nc.tensor.matmul(PS[:, 4, :], mat("ones"), x(i), start=i == 0, stop=i == n_tiles - 1)
                        mm.then_inc(summed, 1)
                    for b in range(NB):
                        for i in range(n_tiles):
                            if b == 0:
                                pe.wait_ge(squared, i + 1)
                            mm = nc.tensor.matmul(PS[:, 5, b:b + 1], sq(i)[:, b * P:(b + 1) * P], mat("ones")[:, 0:1],
                                                  start=i == 0, stop=i == n_tiles - 1)
                    mm.then_inc(summed, 1)
                    pe.wait_ge(step, before + 3)
                    nc.tensor.matmul(PS[:, 5, :], mat("ones"), stat[:, 0, :], start=True, stop=True).then_inc(summed, 1)

                @block.scalar
                def _(act):
                    for i in range(n_tiles):
                        if centered:
                            act.wait_ge(step, i + 1)
                        nc.scalar.activation(sq(i), x(i), ACT.Square, scale=n_channels ** -0.5).then_inc(squared, 1)
                    act.wait_ge(summed, sums + 1)
                    act.wait_ge(step, before + 1)
                    nc.scalar.activation(small[:, 240:244], PS[:, 5, 0:4], ACT.Sqrt, bias=small[:, 250:251]).then_inc(rooted, 1)
                    if bias is not None:
                        for i in range(n_tiles):
                            act.wait_ge(step, before + 4 + i)
                            nc.scalar.activation(write(i), write(i), ACT.Identity, bias=bias(i)).then_inc(shifted, 1)

                @block.vector
                def _(dve):
                    if centered:
                        dve.wait_ge(summed, 1)
                        for i in range(n_tiles):
                            nc.vector.scalar_tensor_tensor(out=x(i), in0=PS[:, 4, :], scalar=-1.0 / n_channels, in1=x(i),
                                                           op0=ALU.mult, op1=ALU.add).then_inc(step, 1)
                    nc.vector.memset(small[:, 250:251], eps).then_inc(step, 1)
                    dve.wait_ge(rooted, 1)
                    nc.vector.reciprocal(small[:, 244:248], small[:, 240:244]).then_inc(step, 1)
                    dve.wait_ge(step, before + 2)
                    nc.vector.tensor_tensor(stat[:, 0, :].rearrange("p (b t) -> p b t", b=NB), mat4("ident"),
                                            small[:, 244:248].unsqueeze(2).to_broadcast([P, NB, P]), ALU.mult).then_inc(step, 1)
                    dve.wait_ge(summed, sums + 2)
                    for i in range(n_tiles):
                        nc.vector.scalar_tensor_tensor(out=write(i), in0=x(i), scalar=gain(i), in1=PS[:, 5, :],
                                                       op0=ALU.mult, op1=ALU.mult).then_inc(step, 1)

        def loads(name, pairs):
            loaded = sem(name)
            with nc.Block() as block:
                @block.scalar
                def _(act):
                    for dst, src in pairs:
                        act.dma_start(dst, src).then_inc(loaded, 16)
                    act.wait_ge(loaded, 16 * len(pairs))

                @block.sync
                def _(sp):
                    stream(sp)

        def copy_act(dst):
            return lambda eng, n, bank: nc.scalar.copy(dst(n), bank)

        def copy_dve(dst):
            return lambda eng, n, bank: nc.vector.tensor_copy(dst(n), bank)

        class Stop(Exception):
            pass

        def checkpoint(name, ap=None):
            if stop == name:
                w = sem("dumped")
                with nc.Block() as block:
                    @block.sync
                    def _(sp):
                        sp.dma_start(dump, ap).then_inc(w, 16)
                        for i in range(RING):
                            sp.wait_ge(weight_loaded[i], 16 * len(range(i, at["issued"], RING)))
                        sp.wait_ge(w, 16)
                raise Stop

        def rows(t):
            return lambda i: t[:, i, :]

        x, h = F[0], F[1]
        loads("inputs_loaded", [(cols[:, :], A["cols"]), (squares[:, :], A["squares"]), (x[:, :, :], A["xT"]),
                                (late[:, :], A["late"])])

        c_ready, mod_taken = sem("c_ready"), sem("mod_taken")
        first = at["used"]
        with nc.Block() as block:
            @block.scalar
            def _(act):
                nc.scalar.activation(small[:, 0:8], cols[:, COL_AT["c"]:COL_AT["c"] + 8], ACT.Silu).then_inc(c_ready, 1)

            @block.tensor
            def _(pe):
                pe.wait_ge(c_ready, 1)
                for n in range(24):
                    w = next_chunk(pe)
                    for k in range(8):
                        mm = nc.tensor.matmul(PS[:, 0, n:n + 1], w[:, k * P:(k + 1) * P], small[:, k:k + 1], start=k == 0, stop=k == 7)
                    mm.then_inc(weight_used, 1)

            @block.vector
            def _(dve):
                dve.wait_ge(weight_used, first + 24)
                nc.vector.tensor_tensor(mod[:, :], PS[:, 0, 0:24], cols[:, COL_AT["b_ada"]:COL_AT["b_ada"] + 24], ALU.add).then_inc(mod_taken, 1)
                dve.wait_ge(mod_taken, 1)
                nc.vector.scalar_tensor_tensor(out=small[:, 8:16], in0=mod[:, 8:16], scalar=1.0,
                                               in1=cols[:, COL_AT["norm_in_gain"]:COL_AT["norm_in_gain"] + 8],
                                               op0=ALU.add, op1=ALU.mult).then_inc(mod_taken, 1)

            @block.sync
            def _(sp):
                stream(sp)
        norm("norm_in", rows(x), 8, D, 1e-6, lambda i: small[:, 8 + i:9 + i], rows(h), bias=lambda i: mod[:, i:i + 1],
             scratch=rows(F[2]))
        checkpoint("h", h[:, :, :])

        q, k_, v = F[2], F[3], F[4]
        gemm("q", 8, 8, rows(h), {"act": lambda e, n, b: nc.scalar.mul(q[:, n, :], b, HD ** -0.5),
                                  "dve": lambda e, n, b: nc.vector.tensor_scalar(q[:, n, :], b, HD ** -0.5, None, ALU.mult)})
        gemm("k", 8, 8, rows(h), {"act": copy_act(rows(k_)), "dve": copy_dve(rows(k_))})

        def gemm_tokens(name, n_tiles, rhs_tokens, dst):
            first = at["used"]
            taken = sem(name + "_taken")
            with nc.Block() as block:
                @block.tensor
                def _(pe):
                    for n in range(n_tiles):
                        if n >= 4:
                            pe.wait_ge(taken, n - 3)
                        w = next_chunk(pe)
                        for b in range(NB):
                            for k in range(8):
                                mm = nc.tensor.matmul(PS[:, n % 4, b * P:(b + 1) * P], rhs_tokens(k, b), w[:, k * P:(k + 1) * P],
                                                      start=k == 0, stop=k == 7)
                        mm.then_inc(weight_used, 1)

                @block.scalar
                def _(act):
                    for n in range(n_tiles):
                        act.wait_ge(weight_used, first + n + 1)
                        nc.scalar.copy(dst(n), PS[:, n % 4, :].rearrange("p (b c) -> p b c", b=NB)).then_inc(taken, 1)

                @block.sync
                def _(sp):
                    stream(sp)

        v_tok = v[:, :, :].rearrange("p a b -> p (a b)").rearrange("p (b c) -> p b c", b=NB)
        gemm_tokens("v", 8, lambda k, b: h[:, k, b * P:(b + 1) * P], lambda n: v_tok[:, :, n * P:(n + 1) * P])
        checkpoint("v", v[:, :, :])

        o = F[5]
        work = F[6][:, :, :].rearrange("p a b -> p (a b)")
        clamped = [work[:, 0:SB_N], work[:, SB_N:2 * SB_N]]
        sp_m = [F[7][:, :, :].rearrange("p a b -> p (a b)")[:, i * SB_N:(i + 1) * SB_N] for i in range(2)]
        wts = [F[8][:, :, :].rearrange("p a b -> p (a b)")[:, i * SB_N:(i + 1) * SB_N] for i in range(2)]
        zb = PS[:, 0:3, :].rearrange("p a b -> p (a b)")
        wb = PS[:, 3:6, :].rearrange("p a b -> p (a b)")
        z_ready, z_taken, sp_step = sem("z_ready"), sem("z_taken"), sem("softplus_step")
        clamp_ready, log_ready, sp_ready = sem("clamp_ready"), sem("log_ready"), sem("sp_ready")
        w_ready, w_clamped, wts_ready = sem("w_ready"), sem("w_clamped"), sem("wts_ready")
        o_ready, o_taken, exp_done, late_masked = sem("o_ready"), sem("o_taken"), sem("sb_exp_done"), sem("sp_masked")
        with nc.Block() as block:
            def head(t, hh, a, b):
                return t[hh % 2 * HD:(hh % 2 + 1) * HD, hh // 2, a:b]

            @block.tensor
            def _(pe):
                def scores(hh, dst, stop):
                    for i in range(NB):
                        mm = nc.tensor.matmul(dst[:, SB_AT[i]:SB_AT[i] + SB_W[i]], head(k_, hh, i * P, (i + 1) * P),
                                              head(q, hh, i * P, T), start=True, stop=stop)
                    return mm

                def products(hh):
                    pe.wait_ge(wts_ready, hh + 1)
                    if hh >= 4 and hh % 2 == 0:
                        pe.wait_ge(o_taken, (hh - 4) // 2 + 1)
                    for i in range(NB):
                        mm = nc.tensor.matmul(PS[hh % 2 * HD:(hh % 2 + 1) * HD, 6 + hh // 2 % 2, i * P:T],
                                              v_tok[:, i, hh * HD:(hh + 1) * HD], wts[hh % 2][:, SB_AT[i]:SB_AT[i] + SB_W[i]],
                                              start=i == 0, stop=i == NB - 1)
                    mm.then_inc(o_ready, 1)

                scores(0, zb, True).then_inc(z_ready, 1)
                pe.wait_ge(sp_ready, 1)
                scores(1, zb, True).then_inc(z_ready, 1)
                for hh in range(H):
                    pe.wait_ge(late_masked, hh + 1)
                    if hh >= 1:
                        pe.wait_ge(w_clamped, hh)
                    for i in range(NB):
                        nc.tensor.matmul(wb[:, SB_AT[i]:SB_AT[i] + SB_W[i]], head(k_, hh, i * P, (i + 1) * P),
                                         head(q, hh, i * P, T), start=True, stop=False)
                        for j in range(i, NB):
                            mm = nc.tensor.matmul(wb[:, SB_AT[i] + (j - i) * P:SB_AT[i] + SB_W[i]],
                                                  mat("neg_ge" if i == j else "neg_ones"),
                                                  sp_m[hh % 2][:, SB_AT[j]:SB_AT[j] + SB_W[j]], start=False, stop=j == NB - 1)
                    mm.then_inc(w_ready, 1)
                    if hh + 2 < H:
                        pe.wait_ge(sp_ready, hh + 2)
                        scores(hh + 2, zb, True).then_inc(z_ready, 1)
                    if hh >= 1:
                        products(hh - 1)
                products(H - 1)

            @block.vector
            def _(dve):
                def softplus(hh):
                    dve.wait_ge(z_ready, hh + 1)
                    if hh >= 2:
                        dve.wait_ge(sp_ready, hh - 1)
                    nc.vector.tensor_scalar(clamped[hh % 2], zb[:, 0:SB_N], 80.0, None, ALU.min).then_inc(clamp_ready, 1)
                    dve.wait_ge(log_ready, hh + 1)
                    if hh >= 2:
                        dve.wait_ge(w_ready, hh - 1)
                    nc.vector.tensor_tensor(sp_m[hh % 2], clamped[hh % 2], zb[:, 0:SB_N], ALU.max).then_inc(sp_ready, 1)
                softplus(0)
                for hh in range(H):
                    if hh + 1 < H:
                        softplus(hh + 1)
                    dve.wait_ge(w_ready, hh + 1)
                    if hh >= 2:
                        dve.wait_ge(o_ready, hh - 1)
                    nc.vector.scalar_tensor_tensor(out=wts[hh % 2], in0=wb[:, 0:SB_N], scalar=0.0, in1=late[:, :],
                                                   op0=ALU.min, op1=ALU.add).then_inc(w_clamped, 1)

            @block.scalar
            def _(act):
                def out_pair(p):
                    act.wait_ge(o_ready, 2 * p + 2)
                    nc.scalar.copy(o[:, p, :], PS[:, 6 + p % 2, :]).then_inc(o_taken, 1)

                def logs(hh):
                    act.wait_ge(clamp_ready, hh + 1)
                    nc.scalar.activation(clamped[hh % 2], clamped[hh % 2], ACT.Exp).then_inc(exp_done, 1)
                    act.wait_ge(exp_done, hh + 1)
                    nc.scalar.activation(clamped[hh % 2], clamped[hh % 2], ACT.Ln, bias=1.0).then_inc(log_ready, 1)
                logs(0)
                for hh in range(H):
                    if hh + 1 < H:
                        logs(hh + 1)
                    act.wait_ge(w_clamped, hh + 1)
                    nc.scalar.activation(wts[hh % 2], wts[hh % 2], ACT.Exp).then_inc(wts_ready, 1)
                    if hh % 2 == 0 and hh >= 2:
                        out_pair(hh // 2 - 1)
                out_pair(H // 2 - 1)

            @block.gpsimd
            def _(pool):
                for hh in range(H):
                    pool.wait_ge(sp_ready, hh + 1)
                    for a, n in ((0, 1), (512, 1), (896, 2)):
                        part = sp_m[hh % 2][:, a:a + n * P].rearrange("p (n c) -> p n c", c=P)
                        last = nc.gpsimd.tensor_tensor(part, part, mat("lt").unsqueeze(1).to_broadcast([P, n, P]), ALU.mult)
                    last.then_inc(late_masked, 1)
        checkpoint("o", o[:, :, :])

        def conv_gemm(name, n_tiles, rhs, taps, w_col, b_col, dst, pair_out=None):
            first = at["used"]
            step, silu_done = sem(name + "_step"), sem(name + "_silu")
            per_pair = 2 * taps + 1

            def steps(n):
                return n // 2 * per_pair + taps * (n % 2 + 1) if pair_out else taps * (n + 1)

            with nc.Block() as block:
                @block.tensor
                def _(pe):
                    for n in range(n_tiles):
                        if n >= 4:
                            pe.wait_ge(step, steps(n - 4))
                        w = next_chunk(pe)
                        for k in range(8):
                            mm = nc.tensor.matmul(PS[:, n % 4, :], w[:, k * P:(k + 1) * P], rhs(k), start=k == 0, stop=k == 7)
                        mm.then_inc(weight_used, 1)

                @block.vector
                def _(dve):
                    for n in range(n_tiles):
                        dve.wait_ge(weight_used, first + n + 1)
                        if pair_out and n >= 4 and n % 2 == 0:
                            pass
                        nc.vector.tensor_scalar(dst(n), PS[:, n % 4, :], w_col(n, taps - 1), b_col(n), ALU.mult, ALU.add).then_inc(step, 1)
                        for j in range(1, taps):
                            dve.wait_ge(step, steps(n) - taps + j)
                            nc.vector.scalar_tensor_tensor(out=dst(n)[:, j:], in0=PS[:, n % 4, 0:T - j], scalar=w_col(n, taps - 1 - j),
                                                           in1=dst(n)[:, j:], op0=ALU.mult, op1=ALU.add).then_inc(step, 1)
                        if pair_out and n % 2 == 1:
                            dve.wait_ge(silu_done, n // 2 + 1)
                            dve.wait_ge(step, steps(n))
                            nc.vector.tensor_tensor(pair_out(n // 2), dst(n - 1), dst(n), ALU.mult).then_inc(step, 1)

                @block.scalar
                def _(act):
                    for n in range(n_tiles):
                        if pair_out and n % 2 == 1:
                            continue
                        act.wait_ge(step, steps(n))
                        nc.scalar.activation(dst(n), dst(n), ACT.Silu).then_inc(silu_done, 1)

                @block.sync
                def _(sp):
                    stream(sp)

        def multiply(name, dst, a, b):
            with nc.Block() as block:
                @block.vector
                def _(dve):
                    nc.vector.tensor_tensor(dst, a, b, ALU.mult)

                @block.sync
                def _(sp):
                    stream(sp)

        y_attn = F[2]
        norm("norm_sb", rows(o), 8, D, 1e-6, lambda i: col("sb_norm_gain", i), rows(y_attn), scratch=rows(F[3]))
        gemm("z_attn", 8, 8, rows(h), {"act": lambda e, n, b: nc.scalar.activation(F[3][:, n, :], b, ACT.Silu)})
        multiply("gate_attn", y_attn[:, :, :], y_attn[:, :, :], F[3][:, :, :])
        checkpoint("ya", y_attn[:, :, :])
        xs, bc = F[3], F[4]
        conv_gemm("xbc", 12, rows(h), 4, lambda n, j: col("conv_w", j * 12 + n), lambda n: col("conv_b", n),
                  lambda n: xs[:, n, :] if n < 8 else bc[:, n - 8, :])
        checkpoint("xbc", xs[:, :, :])

        flat = lambda t: t[:, :, :].rearrange("p a b -> p (a b)")
        sdt = flat(F[7])
        slot = lambda i: sdt[:, i * 64:(i + 1) * 64]
        by_block = lambda ap: ap.rearrange("p (b h) -> p b h", b=NB)
        over_blocks = lambda name: cols[:, COL_AT[name]:COL_AT[name] + H].unsqueeze(1).to_broadcast([P, NB, H])
        z_, m_, dt_, ea_, da_ = (slot(i) for i in range(5))
        dt_step, dt_act = sem("dt_step"), sem("dt_act")
        first = at["used"]
        with nc.Block() as block:
            @block.tensor
            def _(pe):
                w = next_chunk(pe)
                for b in range(NB):
                    for k in range(8):
                        mm = nc.tensor.matmul(PS[:, 0, b * H:(b + 1) * H], h[:, k, b * P:(b + 1) * P], w[:, k * H:(k + 1) * H], start=k == 0, stop=k == 7)
                mm.then_inc(weight_used, 1)

            @block.scalar
            def _(act):
                nc.scalar.activation(by_block(ea_), over_blocks("a_log"), ACT.Exp).then_inc(dt_act, 1)
                act.wait_ge(dt_step, 2)
                nc.scalar.activation(m_, m_, ACT.Exp).then_inc(dt_act, 1)
                act.wait_ge(dt_act, 2)
                nc.scalar.activation(m_, m_, ACT.Ln, bias=1.0).then_inc(dt_act, 1)

            @block.vector
            def _(dve):
                dve.wait_ge(weight_used, first + 1)
                nc.vector.tensor_tensor(by_block(z_), by_block(PS[:, 0, 0:64]), over_blocks("dt_bias"), ALU.add).then_inc(dt_step, 1)
                dve.wait_ge(dt_step, 1)
                nc.vector.tensor_scalar(m_, z_, 80.0, None, ALU.min).then_inc(dt_step, 1)
                dve.wait_ge(dt_act, 3)
                nc.vector.tensor_tensor(dt_, m_, z_, ALU.max).then_inc(dt_step, 1)
                dve.wait_ge(dt_step, 3)
                nc.vector.scalar_tensor_tensor(out=da_, in0=dt_, scalar=-1.0, in1=ea_, op0=ALU.mult, op1=ALU.mult).then_inc(dt_step, 1)

            @block.sync
            def _(sp):
                stream(sp)

        y = F[5]
        state = sdt[:, 512:1536]
        acum, total, cend, etot = sdt[:, 320:336], sdt[:, 336:352], sdt[:, 352:368], sdt[:, 368:384]
        b_tok = sdt[:, 1536:1792]
        cb = sdt[:, 1792:2048]
        x_dt, x_end = sdt[:, 2048:3072], sdt[:, 3072:4096]
        seg, c_exp = flat(F[6])[:, 0:2048], flat(F[6])[:, 2048:4096]
        per_head = lambda ap, w: ap.unsqueeze(2).to_broadcast([P, ap.shape[1], w])
        zeroed = sem("state_zeroed")
        with nc.Block() as block:
            @block.vector
            def _(dve):
                nc.vector.memset(state, 0.0).then_inc(zeroed, 1)
        for c in range(NB):
            t0, t1 = c * P, (c + 1) * P
            da_c, dt_c = da_[:, c * H:(c + 1) * H], dt_[:, c * H:(c + 1) * H]
            cums, moved, cbs, broad = (sem(f"scan{c}_{n}") for n in ("cums", "moved", "cb", "broadcast"))
            vec, sca, outs, states = (sem(f"scan{c}_{n}") for n in ("vec", "act", "y_ready", "state_ready"))
            with nc.Block() as block:
                @block.tensor
                def _(pe):
                    nc.tensor.matmul(PS[:, 0, 0:16], mat("le"), da_c, start=True, stop=True)
                    nc.tensor.matmul(PS[:, 0, 16:32], mat("ones"), da_c, start=True, stop=True).then_inc(cums, 1)
                    for i in range(8):
                        mm = nc.tensor.transpose(PS[:, 1 + i // 4, i % 4 * P:(i % 4 + 1) * P], xs[:, i, t0:t1], mat("ident"))
                        if i == 7:
                            mm.then_inc(moved, 1)
                    for g in range(2):
                        nc.tensor.transpose(PS[:, 3, g * P:(g + 1) * P], bc[:, g, t0:t1], mat("ident"))
                    for g in range(2):
                        mm = nc.tensor.matmul(PS[:, 3, (2 + g) * P:(3 + g) * P], bc[:, g, t0:t1], bc[:, 2 + g, t0:t1], start=True, stop=True)
                    mm.then_inc(cbs, 1)
                    for hh in range(H):
                        mm = nc.tensor.matmul(PS[:, 4 + hh // 4, hh % 4 * P:(hh % 4 + 1) * P],
                                              da_c[:, hh:hh + 1].to_broadcast([P, P]), mat("le"), start=True, stop=True)
                        if hh % 4 == 3:
                            mm.then_inc(broad, 1)

                @block.vector
                def _(dve):
                    dve.wait_ge(cums, 1)
                    nc.vector.tensor_copy(sdt[:, 320:352], PS[:, 0, 0:32]).then_inc(vec, 1)
                    dve.wait_ge(vec, 1)
                    nc.vector.tensor_tensor(cend, total, acum, ALU.subtract).then_inc(vec, 1)
                    dve.wait_ge(moved, 1)
                    nc.vector.tensor_tensor(x_dt.rearrange("p (h c) -> p h c", h=H),
                                            PS[:, 1:3, :].rearrange("p a (h c) -> p (a h) c", c=HD), per_head(dt_c, HD), ALU.mult).then_inc(vec, 1)
                    dve.wait_ge(cbs, 1)
                    nc.vector.tensor_tensor(cb.rearrange("p (g l) -> p g l", g=2), PS[:, 3, 2 * P:4 * P].rearrange("p (g l) -> p g l", g=2),
                                            mat("le").unsqueeze(1).to_broadcast([P, 2, P]), ALU.mult).then_inc(vec, 1)
                    dve.wait_ge(sca, 2)
                    dve.wait_ge(vec, 4)
                    nc.vector.tensor_tensor(x_end.rearrange("p (h c) -> p h c", h=H), x_dt.rearrange("p (h c) -> p h c", h=H),
                                            per_head(cend, HD), ALU.mult).then_inc(vec, 1)
                    for q4 in range(4):
                        dve.wait_ge(broad, q4 + 1)
                        part = seg[:, q4 * T:(q4 + 1) * T]
                        nc.vector.tensor_tensor(part.rearrange("p (h l) -> p h l", h=4), PS[:, 4 + q4, :].rearrange("p (h l) -> p h l", h=4),
                                                per_head(acum[:, q4 * 4:q4 * 4 + 4], P), ALU.subtract).then_inc(vec, 1)
                        dve.wait_ge(vec, 6 + 2 * q4)
                        nc.vector.tensor_scalar(part, part, 0.0, None, ALU.min).then_inc(vec, 1)
                    for q4 in range(4):
                        dve.wait_ge(sca, 5 + 2 * q4)
                        for t, m in ((seg, cb[:, q4 // 2 * P:(q4 // 2 + 1) * P]), (c_exp, bc[:, 2 + q4 // 2, t0:t1])):
                            part = t[:, q4 * T:(q4 + 1) * T].rearrange("p (h l) -> p h l", h=4)
                            nc.vector.tensor_tensor(part, part, m.unsqueeze(1).to_broadcast([P, 4, P]), ALU.mult).then_inc(vec, 1)
                    for i in range(8):
                        if i % 4 == 0:
                            dve.wait_ge(outs, i // 4 + 1)
                        nc.vector.scalar_tensor_tensor(out=y[:, i, t0:t1], in0=xs[:, i, t0:t1], scalar=col("d_skip", i),
                                                       in1=PS[:, 1 + i // 4, i % 4 * P:(i % 4 + 1) * P], op0=ALU.mult, op1=ALU.add).then_inc(vec, 1)
                    dve.wait_ge(outs, 2)
                    sv = state.rearrange("p (h c) -> p h c", h=H)
                    nc.vector.tensor_tensor(sv, sv, per_head(etot, HD), ALU.mult).then_inc(vec, 1)
                    dve.wait_ge(states, 1)
                    dve.wait_ge(vec, 30)
                    for g in range(2):
                        nc.vector.tensor_tensor(state[:, g * T:(g + 1) * T], state[:, g * T:(g + 1) * T], PS[:, 6 + g, :], ALU.add).then_inc(vec, 1)

                @block.scalar
                def _(act):
                    act.wait_ge(vec, 1)
                    nc.scalar.activation(etot, total, ACT.Exp).then_inc(sca, 1)
                    act.wait_ge(vec, 2)
                    nc.scalar.activation(cend, cend, ACT.Exp).then_inc(sca, 1)
                    act.wait_ge(vec, 4)
                    nc.scalar.copy(b_tok, PS[:, 3, 0:2 * P]).then_inc(sca, 1)
                    for q4 in range(4):
                        act.wait_ge(vec, 6 + 2 * q4)
                        nc.scalar.activation(c_exp[:, q4 * T:(q4 + 1) * T], PS[:, 4 + q4, :], ACT.Exp).then_inc(sca, 1)
                        act.wait_ge(vec, 7 + 2 * q4)
                        part = seg[:, q4 * T:(q4 + 1) * T]
                        nc.scalar.activation(part, part, ACT.Exp).then_inc(sca, 1)

                @block.tensor
                def _(pe):
                    for hh in range(H):
                        if hh % 4 == 0:
                            pe.wait_ge(vec, 15 + 2 * (hh // 4))
                        dst = PS[hh % 2 * HD:(hh % 2 + 1) * HD, 1 + hh // 8, hh // 2 % 4 * P:(hh // 2 % 4 + 1) * P]
                        nc.tensor.matmul(dst, x_dt[:, hh * HD:(hh + 1) * HD], seg[:, hh * P:(hh + 1) * P], start=True, stop=False)
                        mm = nc.tensor.matmul(dst, state[:, hh * HD:(hh + 1) * HD], c_exp[:, hh * P:(hh + 1) * P], start=False, stop=True)
                        if hh % 8 == 7:
                            mm.then_inc(outs, 1)
                    pe.wait_ge(sca, 11)
                    for g in range(2):
                        mm = nc.tensor.matmul(PS[:, 6 + g, :], b_tok[:, g * P:(g + 1) * P], x_end[:, g * T:(g + 1) * T], start=True, stop=True)
                    mm.then_inc(states, 1)
        checkpoint("yssd", y[:, :, :])

        gemm("z_ssm", 8, 8, rows(h), {"act": lambda e, n, b: nc.scalar.activation(F[3][:, n, :], b, ACT.Silu)})
        multiply("gate_ssm", F[3][:, :, :], F[3][:, :, :], y[:, :, :])
        y_ssm = F[4]
        norm("norm_ssm", rows(F[3]), 8, D, 1e-6, lambda i: col("ssm_norm_gain", i), rows(y_ssm), scratch=rows(F[6]))
        checkpoint("ys", y_ssm[:, :, :])
        gemm("w_out", 8, 16, lambda k: y_attn[:, k, :] if k < 8 else y_ssm[:, k - 8, :],
             {"dve": lambda e, n, b: nc.vector.scalar_tensor_tensor(out=x[:, n, :], in0=b, scalar=mod[:, 16 + n:17 + n], in1=x[:, n, :],
                                                                    op0=ALU.mult, op1=ALU.add)})
        norm("norm_f", rows(x), 8, D, 1e-6, lambda i: col("norm_f_gain", i), rows(x), scratch=rows(F[6]))
        checkpoint("x1", x[:, :, :])
        end_section()

        r, kx, v, sig, a_, xx, xm, tmp = F[1:9]
        ALL = lambda t: t[:, :, :]

        def differences(dst):
            with nc.Block() as block:
                @block.vector
                def _(dve):
                    nc.vector.tensor_tensor(dst[:, :, 1:T], x[:, :, 0:T - 1], x[:, :, 1:T], ALU.subtract)
                    nc.vector.tensor_scalar(dst[:, :, 0:1], x[:, :, 0:1], -1.0, None, ALU.mult)

                @block.sync
                def _(sp):
                    stream(sp)

        def mixed(dst, diff, branch):
            return lambda k: nc.vector.scalar_tensor_tensor(out=dst[:, k, :], in0=diff[:, k, :], scalar=col("mix", branch * 8 + k),
                                                            in1=x[:, k, :], op0=ALU.mult, op1=ALU.add)

        def lora_out(name, parts, evac):
            ready, taken = sem(name + "_ready"), sem(name + "_taken")
            with nc.Block() as block:
                @block.tensor
                def _(pe):
                    for n in range(8):
                        if n >= 4:
                            pe.wait_ge(taken, n - 3)
                        for j, (w, hid) in enumerate(parts):
                            mm = nc.tensor.matmul(PS[:, n % 4, :], w[:, n * P:(n + 1) * P], hid, start=j == 0, stop=j == len(parts) - 1)
                        mm.then_inc(ready, 1)

                def run(eng):
                    for n in range(8):
                        eng.wait_ge(ready, n + 1)
                        evac["act" if "act" in evac else "dve"](eng, n, PS[:, n % 4, :]).then_inc(taken, 1)

                if "act" in evac:
                    @block.scalar
                    def _(act):
                        run(act)
                else:
                    @block.vector
                    def _(dve):
                        run(dve)

        differences(xx)
        for b, (name, dst) in enumerate((("r", r), ("k7", kx), ("v7", v))):
            gemm(name, 8, 8, rows(xm), {"act": copy_act(rows(dst))}, prepare=mixed(xm, xx, b))
        lw = flat(tmp)
        w2_, a2_, hid_w, hid_a = lw[0:64, 0:D], lw[0:64, D:2 * D], lw[0:64, 2 * D:2 * D + T], lw[0:64, 2 * D + T:3 * D]
        loads("lora_loaded", [(w2_, A["w_w2"]), (a2_, A["w_a2"])])
        gemm("lora_w", 1, 8, rows(xm), {"act": lambda e, n, b: nc.scalar.activation(hid_w, b, ACT.Tanh)}, n_cols=64, prepare=mixed(xm, xx, 3))
        lora_out("decay", [(w2_, hid_w)], {"act": lambda e, n, b: nc.scalar.activation(sig[:, n, :], b, ACT.Sigmoid, bias=col("w0", n))})
        gemm("lora_a", 1, 8, rows(xm), {"act": copy_act(lambda n: hid_a)}, n_cols=64, prepare=mixed(xm, xx, 4))
        lora_out("rate", [(a2_, hid_a)], {"act": lambda e, n, b: nc.scalar.activation(a_[:, n, :], b, ACT.Sigmoid, bias=col("a0", n))})

        kk, bonus = xm, xx
        e1, e2, e3 = sem("kk_vec"), sem("kk_act"), sem("kk_sums")
        of_heads, to_heads = aux[:, 1024:1024 + KT * H], aux[0:H, 0:D]
        sums16 = aux[0:H, 1280:1280 + T]
        loads("selectors_loaded", [(of_heads, A["of_heads"]), (to_heads, A["to_heads"])])
        with nc.Block() as block:
            @block.vector
            def _(dve):
                for i in range(8):
                    nc.vector.tensor_scalar(kk[:, i, :], kx[:, i, :], col("k_k", i), None, ALU.mult).then_inc(e1, 1)
                dve.wait_ge(e2, 9)
                nc.vector.tensor_scalar(sums16, sums16, 1e-12, None, ALU.max).then_inc(e1, 1)
                dve.wait_ge(e1, 9)
                nc.vector.reciprocal(sums16, sums16).then_inc(e1, 1)
                dve.wait_ge(e3, 2)
                nc.vector.tensor_tensor(ALL(kk), ALL(kk), PS[:, :, :], ALU.mult).then_inc(e1, 1)
                dve.wait_ge(e1, 11)
                for i in range(8):
                    nc.vector.tensor_scalar(tmp[:, i, :], a_[:, i, :], 1.0, col("k_a", i), ALU.subtract, ALU.mult).then_inc(e1, 1)
                dve.wait_ge(e1, 19)
                nc.vector.scalar_tensor_tensor(out=ALL(kx), in0=ALL(tmp), scalar=1.0, in1=ALL(kx), op0=ALU.add, op1=ALU.mult).then_inc(e1, 1)
                dve.wait_ge(e1, 20)
                for i in range(8):
                    nc.vector.scalar_tensor_tensor(out=tmp[:, i, :], in0=r[:, i, :], scalar=col("r_k", i), in1=kx[:, i, :],
                                                   op0=ALU.mult, op1=ALU.mult).then_inc(e1, 1)
                dve.wait_ge(e3, 3)
                nc.vector.tensor_tensor(ALL(bonus), PS[:, :, :], ALL(v), ALU.mult).then_inc(e1, 1)

            @block.scalar
            def _(act):
                for i in range(8):
                    act.wait_ge(e1, i + 1)
                    nc.scalar.activation(tmp[:, i, :], kk[:, i, :], ACT.Square).then_inc(e2, 1)
                act.wait_ge(e3, 1)
                nc.scalar.activation(sums16, PS[0:H, 0, :], ACT.Sqrt).then_inc(e2, 1)

            @block.tensor
            def _(pe):
                for i in range(8):
                    pe.wait_ge(e2, i + 1)
                    mm = nc.tensor.matmul(PS[0:H, 0, :], of_heads[:, i * H:(i + 1) * H], tmp[:, i, :], start=i == 0, stop=i == 7)
                mm.then_inc(e3, 1)
                pe.wait_ge(e1, 10)
                for i in range(8):
                    mm = nc.tensor.matmul(PS[:, i, :], to_heads[:, i * P:(i + 1) * P], sums16, start=True, stop=True)
                mm.then_inc(e3, 1)
                pe.wait_ge(e1, 11)
                for i in range(8):
                    pe.wait_ge(e1, 21 + i)
                    mm = nc.tensor.matmul(PS[:, i, :], mat("head_ones"), tmp[:, i, :], start=True, stop=True)
                mm.then_inc(e3, 1)

        ch = lambda t: t[:, :, :].rearrange("p a (c l) -> p (a c) l", c=NB)
        mid, e_mid, e_end, fac = (small[:, 16 + 32 * i:48 + 32 * i] for i in range(4))
        s1, s2 = sem("decay_vec"), sem("decay_act")
        with nc.Block() as block:
            @block.vector
            def _(dve):
                for i in range(8):
                    for c in range(NB):
                        part = slice(c * P, (c + 1) * P)
                        nc.vector.tensor_tensor_scan(tmp[:, i, part], mat("ones"), sig[:, i, part], 0.0, ALU.mult, ALU.add).then_inc(s1, 1)
                dve.wait_ge(s1, 32)
                nc.vector.tensor_copy(mid.unsqueeze(2), ch(tmp)[:, :, 63:64]).then_inc(s1, 1)
                dve.wait_ge(s1, 33)
                nc.vector.tensor_tensor(ch(tmp), ch(tmp), mid.unsqueeze(2).to_broadcast([P, 32, P]), ALU.subtract).then_inc(s1, 1)
                dve.wait_ge(s1, 34)
                nc.vector.tensor_tensor(ALL(sig), ALL(tmp), ALL(sig), ALU.subtract).then_inc(s1, 1)
                nc.vector.tensor_tensor(ALL(a_), ALL(a_), ALL(kk), ALU.mult).then_inc(s1, 1)
                dve.wait_ge(s1, 36)
                dve.wait_ge(s2, 1)
                nc.vector.scalar_tensor_tensor(out=ALL(kk), in0=ALL(sig), scalar=-1.0, in1=ALL(kk), op0=ALU.mult, op1=ALU.mult).then_inc(s1, 1)
                dve.wait_ge(s2, 2)
                nc.vector.tensor_tensor(ALL(a_), ALL(a_), ALL(sig), ALU.mult).then_inc(s1, 1)
                nc.vector.tensor_tensor(ALL(kx), ALL(kx), ALL(sig), ALU.mult).then_inc(s1, 1)
                dve.wait_ge(s2, 3)
                nc.vector.tensor_tensor(ALL(r), ALL(r), ALL(tmp), ALU.mult).then_inc(s1, 1)
                nc.vector.tensor_copy(e_end.unsqueeze(2), ch(tmp)[:, :, P - 1:P]).then_inc(s1, 1)
                dve.wait_ge(s1, 41)
                dve.wait_ge(s2, 4)
                by_c = lambda t: t.rearrange("p (a c) -> p a c", c=NB)
                nc.vector.tensor_tensor(by_c(fac)[:, :, 0:NB - 1], by_c(e_end)[:, :, 0:NB - 1], by_c(e_mid)[:, :, 1:NB], ALU.mult).then_inc(s1, 1)

            @block.scalar
            def _(act):
                act.wait_ge(s1, 35)
                nc.scalar.activation(ALL(sig), ALL(sig), ACT.Exp, scale=-C0).then_inc(s2, 1)
                act.wait_ge(s1, 37)
                nc.scalar.activation(ALL(sig), ALL(tmp), ACT.Exp, scale=C0).then_inc(s2, 1)
                act.wait_ge(s2, 2)
                nc.scalar.activation(ALL(tmp), ALL(tmp), ACT.Exp, scale=-C0).then_inc(s2, 1)
                nc.scalar.activation(e_mid, mid, ACT.Exp, scale=-C0).then_inc(s2, 1)

        rt, kt, at_, bt = r, kx, kk, a_
        UNITS = 2 * NB
        LEVELS = 7
        held = [[flat(t)[:, i * 1024:(i + 1) * 1024] for i in range(4)] for t in (sig, tmp)]
        N_, GT, Q = flat(stat_t), late[:, 0:1024], aux[:, 2560:3584]
        k_tok, b_tok, W_, U_ = (aux[:, i * T:(i + 1) * T] for i in range(4))
        S_ = [aux[:, 2048 + i * 256:2048 + (i + 1) * 256] for i in range(2)]
        names = ["grams", "gram_moved", "start_made", "q_made", "q_moved", "g_made", "g_moved", "gt_moved",
                 "turned", "turned_moved", "w_made", "w_moved", "u_made", "u_moved", "y_made", "y_moved", "s_made", "s_moved"]
        (grams, gram_moved, start_made, q_made, q_moved, g_made, g_moved, gt_moved, turned, turned_moved, w_made, w_moved,
         u_made, u_moved, y_made, y_moved, s_made, s_moved) = (sem("wkv_" + n) for n in names)
        s_zero = sem("wkv_state_zeroed")
        with nc.Block() as block:
            @block.vector
            def _(dve):
                nc.vector.memset(aux[:, 2048:2560], 0.0).then_inc(s_zero, 1)
        four = lambda t, g: t[:, g * T:(g + 1) * T].rearrange("p (h l) -> p h l", h=4)
        bank4 = lambda b: PS[:, b, :].rearrange("p (h l) -> p h l", h=4)
        at_group = lambda j: j % 2 * 4 + j // 2
        half_p = lambda j: slice(j % 2 * HD, (j % 2 + 1) * HD)
        group_cols = lambda j, w: slice(at_group(j) * w, (at_group(j) + 1) * w)
        span = lambda u: slice(u // 2 * P, (u // 2 + 1) * P)

        def of_head(t, u, j):
            return t[half_p(j), u % 2 * 4 + j // 2, span(u)]

        def v_tok(u, j):
            return v[:, u % 2 * 4 + j // 2, u // 2 * P + j % 2 * HD:u // 2 * P + (j % 2 + 1) * HD]

        def has_next(u):
            return u // 2 < NB - 1

        with nc.Block() as block:
            @block.tensor
            def _(pe):
                def gram(u, bank, g, l_, r_):
                    for j in range(4):
                        mm = nc.tensor.matmul(PS[:, bank, j * P:(j + 1) * P], of_head(l_, u, 2 * j + g), of_head(r_, u, 2 * j + g), start=True, stop=True)
                    mm.then_inc(grams, 1)

                def all_grams(u):
                    if u:
                        pe.wait_ge(g_moved, 12 * u)
                    for g in range(2):
                        gram(u, g, g, bt, at_)
                        gram(u, 2 + g, g, at_, bt)
                        gram(u, 4 + g, g, kt, at_)
                    for g in range(2):
                        pe.wait_ge(gram_moved, 10 * u + 3 * g + 1)
                        gram(u, g, g, bt, rt)
                    for g in range(2):
                        pe.wait_ge(gram_moved, 10 * u + 3 * g + 2)
                        gram(u, 2 + g, g, kt, rt)

                def q_level(u, l):
                    for g in range(2):
                        if l == 1:
                            pe.wait_ge(start_made, 6 * u + 3 * g + 3)
                            pe.wait_ge(gram_moved, 10 * u + 7 + g)
                        else:
                            pe.wait_ge(gt_moved, 10 * u + 2 * (l - 2) + g + 1)
                        for j in range(4):
                            mm = nc.tensor.matmul(PS[:, g, j * P:(j + 1) * P], four(N_, g)[:, j, :], four(GT, g)[:, j, :], start=True, stop=True)
                        mm.then_inc(q_made, 1)

                def g_level(u, l):
                    G = held[u % 2][0]
                    for g in range(2):
                        pe.wait_ge(q_moved, 12 * u + 2 * (l - 1) + g + 1)
                        if l == 1:
                            pe.wait_ge(gram_moved, 10 * u + 9 + g)
                        else:
                            pe.wait_ge(g_moved, 12 * u + 2 * (l - 2) + g + 1)
                        for j in range(4):
                            mm = nc.tensor.matmul(PS[:, 2 + g, j * P:(j + 1) * P], four(Q, g)[:, j, :], four(G, g)[:, j, :], start=True, stop=True)
                        if l < LEVELS - 1:
                            for j in range(4):
                                mm = nc.tensor.matmul(PS[:, 4 + g, j * P:(j + 1) * P], four(G, g)[:, j, :], four(Q, g)[:, j, :], start=True, stop=True)
                        mm.then_inc(g_made, 1)

                def carry(u, step):
                    G, Rb, Rk, Ak = held[u % 2]
                    S = S_[u % 2]
                    if step == 1:
                        if u:
                            pe.wait_ge(s_moved, 2 * min(u, UNITS - 2))
                            pe.wait_ge(y_moved, u)
                        for n, (bank, t) in enumerate(((6, v), (7, kt), (6, bt))):
                            if n == 2:
                                pe.wait_ge(turned_moved, 3 * u + 1)
                            for i in range(4):
                                mm = nc.tensor.transpose(PS[:, bank, i * P:(i + 1) * P], t[:, u % 2 * 4 + i, span(u)], mat("ident"))
                            mm.then_inc(turned, 1)
                    elif step == 2:
                        pe.wait_ge(turned_moved, 3 * u + 3)
                        for j in range(8):
                            dst = PS[:, 6 + j % 2, j // 2 * HD:(j // 2 + 1) * HD]
                            nc.tensor.matmul(dst, of_head(at_, u, j), S[half_p(j), j // 2 * HD:(j // 2 + 1) * HD], start=True, stop=False)
                            mm = nc.tensor.matmul(dst, Ak[:, group_cols(j, P)], v_tok(u, j), start=False, stop=True)
                        mm.then_inc(w_made, 1)
                    elif step == 3:
                        pe.wait_ge(w_moved, u + 1)
                        for j in range(8):
                            mm = nc.tensor.matmul(PS[:, 6, j * HD:(j + 1) * HD], G[:, j * P:(j + 1) * P], W_[:, j * HD:(j + 1) * HD], start=True, stop=True)
                        mm.then_inc(u_made, 1)
                    elif step == 4:
                        pe.wait_ge(u_moved, u + 1)
                        for j in range(8):
                            dst = PS[half_p(j), 7, j // 2 * P:(j // 2 + 1) * P]
                            nc.tensor.matmul(dst, S[half_p(j), j // 2 * HD:(j // 2 + 1) * HD], of_head(rt, u, j), start=True, stop=False)
                            nc.tensor.matmul(dst, v_tok(u, j), Rk[:, group_cols(j, P)], start=False, stop=False)
                            mm = nc.tensor.matmul(dst, U_[:, group_cols(j, HD)], Rb[:, group_cols(j, P)], start=False, stop=True)
                        mm.then_inc(y_made, 1)
                    elif step == 5 and has_next(u):
                        for j in range(8):
                            dst = PS[half_p(j), 6, j // 2 * HD:(j // 2 + 1) * HD]
                            nc.tensor.matmul(dst, b_tok[:, j * HD:(j + 1) * HD], U_[:, group_cols(j, HD)], start=True, stop=False)
                            mm = nc.tensor.matmul(dst, k_tok[:, j * HD:(j + 1) * HD], v_tok(u, j), start=False, stop=True)
                        mm.then_inc(s_made, 1)

                for u in range(UNITS + 1):
                    if u < UNITS:
                        all_grams(u)
                    for l in range(1, LEVELS):
                        if u < UNITS:
                            q_level(u, l)
                        if u:
                            carry(u - 1, l)
                        if u < UNITS:
                            g_level(u, l)

            @block.vector
            def _(dve):
                def take_grams(u):
                    G, Rb, Rk, Ak = held[u % 2]
                    if u >= 2:
                        dve.wait_ge(y_made, u - 1)
                    order = [(N_, 0, "lt"), (GT, 2, "pair0"), (Ak, 4, "lt"), (N_, 1, "lt"), (GT, 3, "pair0"), (Ak, 5, "lt"),
                             (Rb, 0, "le"), (Rb, 1, "le"), (Rk, 2, "le"), (Rk, 3, "le")]
                    for n, (dst, bank, m) in enumerate(order):
                        dve.wait_ge(grams, 10 * u + n + 1)
                        nc.vector.tensor_tensor(four(dst, bank % 2), bank4(bank), mat4(m), ALU.mult).then_inc(gram_moved, 1)

                def take_q(u, l):
                    for g in range(2):
                        n = 12 * u + 2 * (l - 1) + g
                        dve.wait_ge(q_made, n + 1)
                        if n >= 2:
                            dve.wait_ge(g_made, n - 1)
                        nc.vector.tensor_tensor(four(Q, g), bank4(g), mat4(f"pair{l}"), ALU.mult).then_inc(q_moved, 1)

                def take_g(u, l):
                    G = held[u % 2][0]
                    for g in range(2):
                        n = 12 * u + 2 * (l - 1) + g
                        dve.wait_ge(g_made, n + 1)
                        if l > 1:
                            dve.wait_ge(g_moved, n - 1)
                        if l < LEVELS - 1:
                            if l > 1:
                                dve.wait_ge(gt_moved, 10 * u + 2 * (l - 2) + g + 1)
                            nc.vector.tensor_tensor(four(GT, g), bank4(4 + g), four(GT, g), ALU.add).then_inc(gt_moved, 1)
                        nc.vector.tensor_tensor(four(G, g), bank4(2 + g), four(G, g), ALU.add).then_inc(g_moved, 1)

                def carry(u, step):
                    S = S_[u % 2]
                    if step == 2:
                        dve.wait_ge(w_made, u + 1)
                        nc.vector.tensor_copy(W_.rearrange("p (g w) -> p g w", g=2), PS[:, 6:8, 0:256]).then_inc(w_moved, 1)
                    elif step == 3:
                        dve.wait_ge(u_made, u + 1)
                        nc.vector.tensor_copy(U_, PS[:, 6, :]).then_inc(u_moved, 1)
                    elif step == 5 and has_next(u):
                        dve.wait_ge(s_made, u + 1)
                        nc.vector.tensor_tensor(S, S, PS[:, 6, 0:256], ALU.add).then_inc(s_moved, 1)
                        dve.wait_ge(s_moved, 2 * u + 1)
                        fv = fac.rearrange("p (a c) -> p a c", c=NB)[:, u % 2 * 4:u % 2 * 4 + 4, u // 2:u // 2 + 1].to_broadcast([P, 4, HD])
                        sv = S.rearrange("p (a v) -> p a v", a=4)
                        nc.vector.tensor_tensor(sv, sv, fv, ALU.mult).then_inc(s_moved, 1)

                for u in range(UNITS + 1):
                    if u < UNITS:
                        take_grams(u)
                    for l in range(1, LEVELS):
                        if u < UNITS:
                            take_q(u, l)
                        if u:
                            carry(u - 1, l)
                        if u < UNITS:
                            take_g(u, l)

            @block.gpsimd
            def _(pool):
                for u in range(UNITS):
                    G = held[u % 2][0]
                    for g in range(2):
                        pool.wait_ge(gram_moved, 10 * u + 3 * g + 2)
                        nc.gpsimd.tensor_tensor(four(G, g), four(N_, g), mat4("pair0_t"), ALU.mult).then_inc(start_made, 1)
                        nc.gpsimd.tensor_tensor(four(GT, g), four(GT, g), mat4("ident"), ALU.add).then_inc(start_made, 1)
                        pool.wait_ge(start_made, 6 * u + 3 * g + 2)
                        nc.gpsimd.tensor_tensor(four(G, g), four(G, g), mat4("ident"), ALU.add).then_inc(start_made, 1)

            @block.scalar
            def _(act):
                for u in range(UNITS):
                    half = slice(u % 2 * 4, u % 2 * 4 + 4)
                    if u:
                        act.wait_ge(s_made, min(u, UNITS - 2))
                    for n, (bank, dst) in enumerate(((6, v[:, half, span(u)]), (7, k_tok.rearrange("p (h l) -> p h l", h=4)),
                                                     (6, b_tok.rearrange("p (h l) -> p h l", h=4)))):
                        act.wait_ge(turned, 3 * u + n + 1)
                        nc.scalar.copy(dst, bank4(bank)).then_inc(turned_moved, 1)
                    act.wait_ge(y_made, u + 1)
                    nc.scalar.copy(rt[:, half, span(u)], bank4(7)).then_inc(y_moved, 1)
        checkpoint("wkv", ALL(r))

        yy, sq = r, tmp
        n1, n2, n3 = sem("gn_vec"), sem("gn_act"), sem("gn_sums")
        loads("selectors_loaded_again", [(of_heads, A["of_heads"]), (to_heads, A["to_heads"])])
        with nc.Block() as block:
            @block.tensor
            def _(pe):
                for i in range(8):
                    mm = nc.tensor.matmul(PS[:, i, :], mat("head_ones"), yy[:, i, :], start=True, stop=True).then_inc(n3, 1)
                for i in range(8):
                    pe.wait_ge(n2, i + 1)
                    mm = nc.tensor.matmul(PS[0:H, 0, :], of_heads[:, i * H:(i + 1) * H], sq[:, i, :], start=i == 0, stop=i == 7)
                mm.then_inc(n3, 1)
                pe.wait_ge(n1, 10)
                for i in range(8):
                    nc.tensor.matmul(PS[:, i, :], to_heads[:, i * P:(i + 1) * P], sums16, start=True, stop=True).then_inc(n3, 1)

            @block.vector
            def _(dve):
                for i in range(8):
                    dve.wait_ge(n3, i + 1)
                    nc.vector.scalar_tensor_tensor(out=yy[:, i, :], in0=PS[:, i, :], scalar=-1.0 / HD, in1=yy[:, i, :],
                                                   op0=ALU.mult, op1=ALU.add).then_inc(n1, 1)
                nc.vector.memset(small[:, 250:251], 64e-5).then_inc(n1, 1)
                dve.wait_ge(n2, 9)
                nc.vector.reciprocal(sums16, sums16).then_inc(n1, 1)
                for i in range(8):
                    dve.wait_ge(n3, 10 + i)
                    nc.vector.scalar_tensor_tensor(out=yy[:, i, :], in0=yy[:, i, :], scalar=col("lnx_g", i), in1=PS[:, i, :],
                                                   op0=ALU.mult, op1=ALU.mult).then_inc(n1, 1)
                    dve.wait_ge(n1, 11 + 2 * i)
                    nc.vector.scalar_tensor_tensor(out=yy[:, i, :], in0=yy[:, i, :], scalar=col("lnx_b", i), in1=bonus[:, i, :],
                                                   op0=ALU.add, op1=ALU.add).then_inc(n1, 1)

            @block.scalar
            def _(act):
                for i in range(8):
                    act.wait_ge(n1, i + 1)
                    nc.scalar.activation(sq[:, i, :], yy[:, i, :], ACT.Square, scale=HD ** -0.5).then_inc(n2, 1)
                act.wait_ge(n1, 9)
                act.wait_ge(n3, 9)
                nc.scalar.activation(sums16, PS[0:H, 0, :], ACT.Sqrt, bias=small[0:H, 250:251]).then_inc(n2, 1)

        differences(F[2])
        g2_ = [flat(F[4])[0:80, i * D:(i + 1) * D] for i in range(2)]
        hid_g = [flat(F[4])[0:80, 2 * D + i * T:2 * D + (i + 1) * T] for i in range(2)]
        loads("g2_loaded", [(g2_[0], A["w_g2"][0:80, :]), (g2_[1], A["w_g2"][80:160, :])])
        gemm("lora_g", 2, 8, rows(F[3]), {"act": lambda e, n, b: nc.scalar.activation(hid_g[n], b, ACT.Sigmoid)}, n_cols=80,
             prepare=mixed(F[3], F[2], 5))
        lora_out("gate7", [(g2_[0], hid_g[0]), (g2_[1], hid_g[1])],
                 {"dve": lambda e, n, b: nc.vector.tensor_tensor(yy[:, n, :], yy[:, n, :], b, ALU.mult)})

        def add_to_x(e, n, b):
            return nc.vector.scalar_tensor_tensor(out=x[:, n, :], in0=x[:, n, :], scalar=ALPHA, in1=b, op0=ALU.mult, op1=ALU.add)

        def layer_norm(layer, which):
            i0 = (2 * layer + which) * 8
            norm(f"ln{layer}{which}", rows(x), 8, D, 1e-5, lambda i: col("ln_g", i0 + i), rows(x), centered=True,
                 bias=lambda i: col("ln_b", i0 + i), scratch=rows(F[8]))

        def ffn(layer):
            hid = lambda i: F[1 + i // 8][:, i % 8, :]
            tile_of = lambda n: n // 2 + n % 2 * FT
            conv_gemm(f"up{layer}", 2 * FT, rows(x), 3,
                      lambda n, j: col("ffn_conv_w", (layer * 3 + j) * 2 * FT + tile_of(n)),
                      lambda n: col("ffn_conv_b", layer * 2 * FT + tile_of(n)),
                      lambda n: F[8][:, n // 2 % 2, :] if n % 2 else hid(n // 2), pair_out=hid)
            gemm(f"down{layer}", 8, FT, hid, {"dve": add_to_x})
            layer_norm(layer, 1)

        gemm("w_o", 8, 8, rows(yy), {"dve": add_to_x})
        layer_norm(0, 0)
        checkpoint("x2", ALL(x))
        ffn(0)
        checkpoint("x3", ALL(x))
        end_section()

        low = F[1]
        c_q, c_kv, k_idx = rows(low), low[:, 2, :], low[:, 3, :]
        gemm("d_in", 4, 8, rows(x), {"act": copy_act(rows(low))})
        w_idx = small[:, 144:176]
        w_idx_taken = sem("w_idx_taken")
        first = at["used"]
        with nc.Block() as block:
            @block.tensor
            def _(pe):
                w = next_chunk(pe)
                for b in range(NB):
                    for k in range(8):
                        mm = nc.tensor.matmul(PS[:, 0, b * 8:(b + 1) * 8], x[:, k, b * P:(b + 1) * P], w[:, k * 8:(k + 1) * 8], start=k == 0, stop=k == 7)
                mm.then_inc(weight_used, 1)

            @block.vector
            def _(dve):
                dve.wait_ge(weight_used, first + 1)
                nc.vector.tensor_scalar(w_idx, PS[:, 0, 0:32], 8 ** -0.5 * 64 ** -0.5, None, ALU.mult).then_inc(w_idx_taken, 1)

            @block.sync
            def _(sp):
                stream(sp)
        norm("norm_cq", c_q, 2, 256, 1e-6, lambda i: col("q_norm_g", i), c_q, scratch=rows(F[8]))
        norm("norm_ckv", lambda i: c_kv, 1, P, 1e-6, lambda i: col("kv_norm_g", 0), lambda i: c_kv, scratch=rows(F[8]))
        norm("norm_kidx", lambda i: k_idx, 1, P, 1e-5, lambda i: col("kidx_g", 0), lambda i: k_idx, centered=True,
             bias=lambda i: col("kidx_b", 0), scratch=rows(F[8]))
        qd, qi = F[2], F[3]
        gemm("d_uq", 8, 2, c_q, {"act": lambda e, n, b: nc.scalar.mul(qd[:, n, :], b, HD ** -0.5)})
        gemm("d_qidx", 4, 2, c_q, {"dve": copy_dve(rows(qi))})

        f8 = flat(F[8])
        uk, uv = f8[:, 0:1024], f8[:, 1024:2048]
        qabs = [f8[:, 2048 + i * T:2048 + (i + 1) * T] for i in range(2)]
        lg = [flat(F[3])[:, 1280 + i * SB_N:1280 + (i + 1) * SB_N] for i in range(2)]
        rb, oneh, band = flat(F[7])[0:32, 0:16], flat(F[7])[0:32, 512:512 + BAND], flat(F[7])[0:16, 2048:2048 + BAND]
        loads("dsa_loaded", [(rb, A["rel_bias"]), (oneh, A["bucket1h"]), (uk, A["d_uk"]), (uv, A["d_uv"])])
        band_dram = nc.dram_tensor("band", (H, BAND), f32, kind="Internal")
        toep = [F[5], F[6]]
        band_made, band_taken, band_stored, toep_loaded = sem("band_made"), sem("band_taken"), sem("band_stored"), sem("toeplitz_loaded")
        ckv_tok = aux[:, 0:T]
        tok_made, tok_taken = sem("ckv_tok_made"), sem("ckv_tok_taken")
        with nc.Block() as block:
            @block.tensor
            def _(pe):
                nc.tensor.matmul(PS[0:16, 0, :], rb, oneh[:, 0:T], start=True, stop=True)
                nc.tensor.matmul(PS[0:16, 1, 0:P], rb, oneh[:, T:BAND], start=True, stop=True).then_inc(band_made, 1)
                for b in range(NB):
                    mm = nc.tensor.transpose(PS[:, 2, b * P:(b + 1) * P], low[:, 2, b * P:(b + 1) * P], mat("ident"))
                mm.then_inc(tok_made, 1)

            @block.scalar
            def _(act):
                act.wait_ge(band_made, 1)
                nc.scalar.copy(band, PS[0:16, 0:2, :].rearrange("p a b -> p (a b)")[:, 0:BAND]).then_inc(band_taken, 1)
                act.wait_ge(tok_made, 1)
                nc.scalar.copy(ckv_tok, PS[:, 2, :]).then_inc(tok_taken, 1)

            @block.sync
            def _(sp):
                sp.wait_ge(band_taken, 1)
                sp.dma_start(band_dram.ap(), band).then_inc(band_stored, 16)
                sp.wait_ge(band_stored, 16)
                for i in range(2):
                    src = bass.AP(band_dram, i * 8 * BAND, [[1, P], [BAND, 8], [1, T]])
                    sp.dma_start(toep[i][:, :, :], src).then_inc(toep_loaded, 16)
                stream(sp)

        mask, left = F[4], lambda b: F[4][:, 4 + b, :]
        best = small[:, 176:208]
        rel = [F[7][:, i, :] for i in range(8)]
        sc_made, sc_relu, sc_added, select = sem("index_scores_made"), sem("index_relu"), sem("index_added"), sem("selected")
        with nc.Block() as block:
            @block.tensor
            def _(pe):
                for b in range(1, NB):
                    n = (b + 1) * P
                    for i in range(8):
                        half_p = slice(i % 2 * HD, (i % 2 + 1) * HD)
                        if b > 1:
                            pe.wait_ge(sc_relu, 8 * (b - 2) + i + 1)
                        nc.tensor.matmul(PS[:, i, 0:n], qi[half_p, i // 2, b * P:(b + 1) * P], low[half_p, 3, 0:n], start=True, stop=True).then_inc(sc_made, 1)

            @block.scalar
            def _(act):
                for b in range(1, NB):
                    n = (b + 1) * P
                    for i in range(8):
                        act.wait_ge(sc_made, 8 * (b - 1) + i + 1)
                        if b > 1:
                            act.wait_ge(sc_added, 9 * (b - 2) + i + 1)
                        nc.scalar.activation(rel[i][:, 0:n], PS[:, i, 0:n], ACT.Relu).then_inc(sc_relu, 1)

            @block.vector
            def _(dve):
                for b in range(1, NB):
                    n = (b + 1) * P
                    for i in range(8):
                        dve.wait_ge(sc_relu, 8 * (b - 1) + i + 1)
                        wcol = w_idx[:, b * 8 + i:b * 8 + i + 1]
                        if i == 0:
                            nc.vector.tensor_scalar(left(b)[:, 0:n], rel[i][:, 0:n], wcol, None, ALU.mult).then_inc(sc_added, 1)
                        else:
                            dve.wait_ge(sc_added, 9 * (b - 1) + i)
                            nc.vector.scalar_tensor_tensor(out=left(b)[:, 0:n], in0=rel[i][:, 0:n], scalar=wcol, in1=left(b)[:, 0:n],
                                                           op0=ALU.mult, op1=ALU.add).then_inc(sc_added, 1)
                    dve.wait_ge(sc_added, 9 * (b - 1) + 8)
                    nc.vector.tensor_tensor(left(b)[:, b * P:n], left(b)[:, b * P:n], mat("neg_after"), ALU.add).then_inc(sc_added, 1)
                dve.wait_ge(sc_added, 27)
                for k in range(TOPK // 8):
                    for b in range(1, NB):
                        if k:
                            dve.wait_ge(select, 6 * k - 3 + b)
                        nc.vector.max(out=best[:, 8 * b:8 * b + 8], in_=left(b)[:, 0:(b + 1) * P]).then_inc(select, 1)
                    for b in range(1, NB):
                        dve.wait_ge(select, 6 * k + b)
                        nc.vector.match_replace(out=left(b)[:, 0:(b + 1) * P], in_to_replace=best[:, 8 * b:8 * b + 8],
                                                in_values=left(b)[:, 0:(b + 1) * P], imm_value=TAKEN).then_inc(select, 1)
                dve.wait_ge(select, 6 * (TOPK // 8))
                for b in range(1, NB):
                    n = (b + 1) * P
                    nc.vector.tensor_scalar(mask[:, b, 0:n], left(b)[:, 0:n], TAKEN / 2, NEG, ALU.is_ge, ALU.mult).then_inc(select, 1)
                nc.vector.tensor_copy(mask[:, 0, 0:P], mat("neg_after")).then_inc(select, 1)

            @block.sync
            def _(sp):
                sp.wait_ge(toep_loaded, 32)

        LG_BANK = [(2, 0), (3, 0), (2, P), (4, 0)]
        L_AT = [0, P, 3 * P, 6 * P]
        att = F[7]
        pt_ = aux[:, T:T + SB_N]
        olat = aux[:, 1792:2304]
        mx, sm = small[:, 208:216], small[:, 216:224]
        nmx, rs = small[:, 224:232], small[:, 232:240]
        names = ["qabs_made", "qabs_moved", "logits_made", "masked", "negated", "exped", "inverted", "scaled", "turned",
                 "turned_moved", "olat_made", "olat_moved", "o_made", "o_moved"]
        (qa_made, qa_moved, lg_made, lg_masked, negated, exped, inverted, scaled, pt_made, pt_moved, ol_made, ol_moved,
         oo_made, oo_moved) = (sem("dsa_" + n) for n in names)
        with nc.Block() as block:
            @block.tensor
            def _(pe):
                def absorb(hh):
                    half_p = slice(hh % 2 * HD, (hh % 2 + 1) * HD)
                    if hh:
                        pe.wait_ge(qa_moved, hh)
                    if hh >= 4:
                        pe.wait_ge(oo_moved, hh - 3)
                    nc.tensor.matmul(PS[:, 0, :], uk[half_p, hh // 2 * P:(hh // 2 + 1) * P], qd[half_p, hh // 2, :], start=True, stop=True).then_inc(qa_made, 1)

                def logits(hh):
                    pe.wait_ge(qa_moved, hh + 1)
                    if hh:
                        pe.wait_ge(lg_masked, 4 * hh)
                    for b in range(NB):
                        n = (b + 1) * P
                        bank, at0 = LG_BANK[b]
                        dst = PS[:, bank, at0:at0 + n]
                        nc.tensor.matmul(dst, qabs[hh % 2][:, b * P:(b + 1) * P], low[:, 2, 0:n], start=True, stop=False)
                        mm = nc.tensor.matmul(dst, mat("flip"), toep[hh // 8][:, hh % 8, T - n:T], start=False, stop=True)
                    mm.then_inc(lg_made, 1)

                def turn(hh):
                    pe.wait_ge(scaled, 4 * hh + 4)
                    if hh:
                        pe.wait_ge(pt_moved, hh)
                    for i in range(NB):
                        for b in range(i, NB):
                            at0 = SB_AT[i] + (b - i) * P
                            mm = nc.tensor.transpose(PS[:, 5 + at0 // T, at0 % T:at0 % T + P], lg[hh % 2][:, L_AT[b] + i * P:L_AT[b] + (i + 1) * P], mat("ident"))
                    mm.then_inc(pt_made, 1)

                def latent(hh):
                    pe.wait_ge(pt_moved, hh + 1)
                    if hh:
                        pe.wait_ge(ol_moved, hh)
                    for i in range(NB):
                        mm = nc.tensor.matmul(PS[:, 1, i * P:T], ckv_tok[:, i * P:(i + 1) * P], pt_[:, SB_AT[i]:SB_AT[i] + SB_W[i]],
                                              start=i == 0, stop=i == NB - 1)
                    mm.then_inc(ol_made, 1)

                def values(hh):
                    pe.wait_ge(ol_moved, hh + 1)
                    pe.wait_ge(qa_moved, min(hh + 4, H))
                    half_p = slice(hh % 2 * HD, (hh % 2 + 1) * HD)
                    nc.tensor.matmul(PS[half_p, 0, :], uv[:, hh * HD:(hh + 1) * HD], olat, start=True, stop=True).then_inc(oo_made, 1)

                absorb(0)
                absorb(1)
                logits(0)
                for hh in range(H + 1):
                    if hh + 2 < H:
                        absorb(hh + 2)
                    if hh + 1 < H:
                        logits(hh + 1)
                    if hh < H:
                        turn(hh)
                    if hh:
                        values(hh - 1)
                    if hh < H:
                        latent(hh)

            @block.vector
            def _(dve):
                for hh in range(H):
                    p = hh % 2
                    dve.wait_ge(lg_made, hh + 1)
                    if hh >= 2:
                        dve.wait_ge(pt_made, hh - 1)
                    for b in range(NB):
                        n = (b + 1) * P
                        bank, at0 = LG_BANK[b]
                        nc.vector.tensor_tensor_reduce(out=lg[p][:, L_AT[b]:L_AT[b] + n], in0=PS[:, bank, at0:at0 + n], in1=mask[:, b, 0:n],
                                                       scale=1.0, scalar=-3e38, op0=ALU.add, op1=ALU.max,
                                                       accum_out=mx[:, 4 * p + b:4 * p + b + 1]).then_inc(lg_masked, 1)
                    dve.wait_ge(lg_masked, 4 * hh + 4)
                    nc.vector.tensor_scalar(nmx[:, 4 * p:4 * p + 4], mx[:, 4 * p:4 * p + 4], -1.0, None, ALU.mult).then_inc(negated, 1)
                    dve.wait_ge(exped, 4 * hh + 4)
                    nc.vector.reciprocal(rs[:, 4 * p:4 * p + 4], sm[:, 4 * p:4 * p + 4]).then_inc(inverted, 1)
                    dve.wait_ge(inverted, hh + 1)
                    for b in range(NB):
                        part = lg[p][:, L_AT[b]:L_AT[b] + (b + 1) * P]
                        nc.vector.tensor_scalar(part, part, rs[:, 4 * p + b:4 * p + b + 1], None, ALU.mult).then_inc(scaled, 1)

            @block.scalar
            def _(act):
                def absorbed(hh):
                    act.wait_ge(qa_made, hh + 1)
                    if hh >= 2:
                        act.wait_ge(lg_made, hh - 1)
                    nc.scalar.copy(qabs[hh % 2], PS[:, 0, :]).then_inc(qa_moved, 1)

                def exps(hh):
                    p = hh % 2
                    act.wait_ge(negated, hh + 1)
                    for b in range(NB):
                        part = lg[p][:, L_AT[b]:L_AT[b] + (b + 1) * P]
                        nc.scalar.activation(part, part, ACT.Exp, bias=nmx[:, 4 * p + b:4 * p + b + 1],
                                             accum_out=sm[:, 4 * p + b:4 * p + b + 1]).then_inc(exped, 1)
                absorbed(0)
                absorbed(1)
                exps(0)
                for hh in range(H + 1):
                    if hh + 2 < H:
                        absorbed(hh + 2)
                    if hh < H:
                        act.wait_ge(pt_made, hh + 1)
                        if hh:
                            act.wait_ge(ol_made, hh)
                        nc.scalar.copy(pt_, PS[:, 5:8, :].rearrange("p a b -> p (a b)")[:, 0:SB_N]).then_inc(pt_moved, 1)
                    if hh:
                        act.wait_ge(oo_made, hh)
                        half_p = slice((hh - 1) % 2 * HD, ((hh - 1) % 2 + 1) * HD)
                        nc.scalar.copy(att[half_p, (hh - 1) // 2, :], PS[half_p, 0, :]).then_inc(oo_moved, 1)
                    if hh + 1 < H:
                        exps(hh + 1)
                    if hh < H:
                        act.wait_ge(ol_made, hh + 1)
                        nc.scalar.copy(olat, PS[:, 1, :]).then_inc(ol_moved, 1)

        gemm("d_wo", 8, 8, rows(att), {"dve": add_to_x})
        layer_norm(1, 0)
        checkpoint("x4", ALL(x))
        ffn(1)

        with nc.Block() as block:
            @block.sync
            def _(sp):
                sp.dma_start(out, ALL(x)).then_inc(stored, 16)
                sp.wait_ge(stored, 16)


def weight_tiles(w, n_cols=P):
    k, n = w.shape
    return np.ascontiguousarray(w.reshape(k // P, P, n // n_cols, n_cols).transpose(2, 1, 0, 3).reshape(n // n_cols, P, -1))


def columns(v):
    return np.ascontiguousarray(v).reshape(-1, P).T


def lay_out(i):
    row = lambda v: np.broadcast_to(v.reshape(1, -1), (P, v.size))
    c = {"c": columns(i["c"]), "b_ada": columns(i["b_ada"]), "norm_in_gain": columns(i["norm_in_gain"]),
         "conv_w": columns(i["conv_w"][0]), "conv_b": columns(i["conv_b"]), "d_skip": columns(np.repeat(i["d_skip"], HD)),
         "sb_norm_gain": columns(i["sb_norm_gain"]), "ssm_norm_gain": columns(i["ssm_norm_gain"]),
         "norm_f_gain": columns(i["norm_f_gain"]), "dt_bias": row(i["dt_bias"]), "a_log": row(i["a_log"]),
         "ln_g": columns(i["ln_g_2"]), "ln_b": columns(i["ln_b_2"]), "mix": columns(i["rwkv_mix_2"]),
         "w0": columns(i["rwkv_w0_2"]), "a0": columns(i["rwkv_a0_2"]), "k_k": columns(i["rwkv_k_k_2"]),
         "k_a": columns(i["rwkv_k_a_2"]), "r_k": columns(i["rwkv_r_k_2"]), "lnx_g": columns(i["rwkv_lnx_g_2"]),
         "lnx_b": columns(i["rwkv_lnx_b_2"]), "q_norm_g": columns(i["dsa_q_norm_g_2"]),
         "kv_norm_g": columns(i["dsa_kv_norm_g_2"]), "kidx_g": columns(np.tile(i["dsa_kidx_g_2"][0], 2)),
         "kidx_b": columns(np.tile(i["dsa_kidx_b_2"][0], 2)),
         "ffn_conv_w": columns(i["ffn_conv_w_2"]), "ffn_conv_b": columns(i["ffn_conv_b_2"])}
    w_in = i["w_in"][0]
    d_in = i["dsa_w_in_2"][0]
    at = D_XBC0 = 4096 + 1536
    a = {"xT": np.ascontiguousarray(i["x"][0].T.reshape(KT, P, T).transpose(1, 0, 2)),
         "cols": np.ascontiguousarray(np.concatenate([c[n] for n, _ in COLS], axis=1)),
         "squares": square_constants(), "late": late_constant(), "bucket1h": bucket_constant(),
         "w_ada": weight_tiles(i["w_ada"][0]),
         "w_in": weight_tiles(np.concatenate([w_in[:, :at], w_in[:, at + 16:]], axis=1)),
         "w_dt": weight_tiles(w_in[:, at:at + 16], 16), "w_out": weight_tiles(i["w_out"][0]),
         "w_rkv": np.concatenate([weight_tiles(w) for w in i["rwkv_w_rkv_2"][0]]),
         "w_w1": weight_tiles(i["rwkv_w1_2"][0], 64), "w_a1": weight_tiles(i["rwkv_a1_2"][0], 64),
         "w_g1": weight_tiles(i["rwkv_g1_2"][0], 80), "w_w2": i["rwkv_w2_2"][0], "w_a2": i["rwkv_a2_2"][0],
         "w_g2": i["rwkv_g2_2"][0], "w_o": weight_tiles(i["rwkv_w_o_2"][0]),
         "d_in": weight_tiles(np.concatenate([d_in[:, :384], d_in[:, 384:448], d_in[:, 384:448]], axis=1)),
         "d_widx": weight_tiles(d_in[:, 448:456], 8),
         "d_uq": weight_tiles(i["dsa_w_uq_2"][0]), "d_uk": i["dsa_w_uk_2"][0].reshape(H // 2, P, P).transpose(1, 0, 2).reshape(P, -1),
         "d_uv": i["dsa_w_uv_2"][0].transpose(1, 0, 2).reshape(P, -1), "d_qidx": weight_tiles(i["dsa_w_qidx_2"][0]),
         "d_wo": weight_tiles(i["dsa_w_o_2"][0]), "rel_bias": i["rel_bias_2"]}
    a["of_heads"], a["to_heads"] = head_selectors()
    for l in range(2):
        a[f"up{l}"] = weight_tiles(i["ffn_w_up_2"][l])
        a[f"down{l}"] = weight_tiles(i["ffn_w_down_2"][l])
    return {n: np.ascontiguousarray(v) for n, v in a.items()}


def kernel(**inputs):
    import concourse.bacc as bacc
    from concourse.bass_utils import run_bass_kernel_spmd

    arrays = lay_out({n: np.asarray(v) for n, v in inputs.items()})
    nc = bacc.Bacc("TRN2", target_bir_lowering=False, num_devices=1)
    dram = {n: nc.dram_tensor("in_" + n, a.shape, mybir.dt.float32, kind="ExternalInput").ap() for n, a in arrays.items()}
    out = nc.dram_tensor("out", (P, KT, T), mybir.dt.float32, kind="ExternalOutput").ap()
    program(nc, dram, out)
    r = run_bass_kernel_spmd(nc, [{"in_" + n: a for n, a in arrays.items()}], core_ids=[0])
    got = r.results[0]["out"]
    return np.ascontiguousarray(got.transpose(1, 0, 2).reshape(D, T).T).reshape(1, T, D)
```

```python
import numpy as np
import concourse.bass as bass
from concourse import mybir
from contextlib import ExitStack

P = 128
T = 512
D = 1024
KT = D // P
NB = T // P
HD = 64
H = D // HD
D_SSM = 1024
XBC_T = 12
D_FF = 2816
FT = D_FF // P
BUCKETS = 32
TOPK = min(256, T // 4)
RING = 6
CHUNK = 8 * P
ALPHA = 4 ** 0.25
NEG = -1e30
C0 = float(np.exp(-0.5))
BAND = T + P
TAKEN = -3e38

SB_W = [T - P * i for i in range(NB)]
SB_AT = [0, 512, 1024, 896]
SB_N = 1280

COLS = [("c", 8), ("b_ada", 24), ("norm_in_gain", 8), ("conv_w", 48), ("conv_b", 12), ("d_skip", 8),
        ("sb_norm_gain", 8), ("ssm_norm_gain", 8), ("norm_f_gain", 8), ("dt_bias", 16), ("a_log", 16),
        ("ln_g", 32), ("ln_b", 32), ("mix", 48), ("w0", 8), ("a0", 8), ("k_k", 8), ("k_a", 8),
        ("r_k", 8), ("lnx_g", 8), ("lnx_b", 8), ("q_norm_g", 2), ("kv_norm_g", 1), ("kidx_g", 1),
        ("kidx_b", 1), ("ffn_conv_w", 2 * 3 * 2 * FT), ("ffn_conv_b", 2 * 2 * FT)]
COL_AT = {}
_n = 0
for _name, _w in COLS:
    COL_AT[_name] = _n
    _n += _w
N_COLS = _n

MATS = ["ident", "ones", "head_ones", "lt", "le", "gt", "neg_ge", "neg_ones", "flip", "neg_after"] + [f"pair{i}" for i in range(7)] + ["pair0_t"]
MAT_AT = {m: i for i, m in enumerate(MATS)}


def square_constants():
    p, f = np.arange(P)[:, None], np.arange(P)[None, :]
    out = {"ident": p == f, "ones": p >= 0 * f, "head_ones": p // HD == f // HD, "lt": p < f, "le": p <= f,
           "gt": p > f, "neg_ge": -1.0 * (p >= f), "neg_ones": -1.0 * (p >= 0 * f),
           "flip": p + f == P - 1, "neg_after": np.where(f > p, NEG, 0)}
    for i in range(7):
        out[f"pair{i}"] = (p >> (i + 1) == f >> (i + 1)) & (((p >> i) & 1) == 1) & (((f >> i) & 1) == 0)
    out["pair0_t"] = out["pair0"].T
    return np.concatenate([np.asarray(out[m], np.float32) for m in MATS], axis=1)


def late_constant():
    out = np.zeros((P, SB_N), np.float32)
    p, f = np.arange(P)[:, None], np.arange(P)[None, :]
    for i in range(NB):
        out[:, SB_AT[i]:SB_AT[i] + P] = np.where(p >= f, NEG, 0)
    return out


def bucket_constant():
    n = np.maximum(T - 1 - np.arange(BAND), 0)
    nf = np.maximum(n, 1).astype(np.float32)
    large = 16 + (np.log(nf / 16) / np.log(128 / 16) * 16).astype(np.int32)
    b = np.where(n < 16, n, np.minimum(large, BUCKETS - 1))
    return (np.arange(BUCKETS)[:, None] == b[None, :]).astype(np.float32)


def head_selectors():
    channel, head = np.arange(D)[:, None] // HD, np.arange(H)[None, :]
    one = (channel == head).astype(np.float32)
    return one.reshape(KT, P, H).transpose(1, 0, 2).reshape(P, KT * H), one.T


ORDER = ["xT", "cols", "squares", "late", "bucket1h", "w_ada", "w_q", "w_k", "w_in", "w_z", "w_dt", "w_out", "w_rkv", "w_w1", "w_a1",
         "w_g1", "w_w2", "w_a2", "w_g2", "w_o", "d_in", "d_uq", "d_widx", "d_uk", "d_uv", "d_qidx", "d_wo", "rel_bias",
         "up0", "up1", "down0", "down1"]


def program(nc, A, out, stop=None, dump=None):
    f32 = mybir.dt.float32
    ALU = mybir.AluOpType
    ACT = mybir.ActivationFunctionType
    AX = mybir.AxisListType.X
    ctx = ExitStack()
    assert TOPK == P

    def sb(name, shape):
        return ctx.enter_context(nc.sbuf_tensor(name, shape, f32))

    section = []

    def sem(name):
        section.append(nc.alloc_semaphore(name))
        return section[-1]

    def end_section():
        nc.clear_and_free_semaphores(section)
        section.clear()
        nc.all_engine_barrier()

    with ctx:
        F = [sb(f"act{i}", [P, KT, T]) for i in range(5)]
        ring = sb("weight_ring", [P, RING, CHUNK])
        cols = sb("cols", [P, N_COLS])
        squares = sb("squares", [P, len(MATS) * P])
        small = sb("small", [P, 256])
        mod = sb("mod", [P, 24])
        stat = sb("stat", [P, 2, T])
        stat_t = stat

        above = []

        def give_up(first):
            while above and above[-1][0] >= first:
                above.pop()[1].close()

        def open_above(key, name, shape, dtype):
            one = ExitStack()
            above.append((key, one))
            return one.enter_context(nc.sbuf_tensor(name, shape, dtype))

        def restore(name):
            give_up(9)
            for i in range(5 + len(above), 9):
                F[i:] = [open_above(i, f"{name}_act{i}", [P, KT, T], f32)]

        def open_split(name, first, x_tiles):
            give_up(first)
            return [open_above(9, f"{name}_{part}", shape, mybir.dt.float32r) for part, shape in
                    (("x_high", [P, x_tiles, T]), ("x_low", [P, x_tiles, T]), ("w_high", [P, 2, CHUNK]), ("w_low", [P, 2, CHUNK]))]

        PS = ctx.enter_context(nc.psum_tensor("banks", [P, 8, T], f32))
        late = sb("late", [P, SB_N])
        aux = sb("aux", [P, 3584])
        ctx.callback(give_up, 0)
        restore("first")

        def col(name, i):
            return cols[:, COL_AT[name] + i:COL_AT[name] + i + 1]

        def mat(name):
            return squares[:, MAT_AT[name] * P:MAT_AT[name] * P + P]

        def mat4(name):
            return mat(name).unsqueeze(1).to_broadcast([P, 4, P])

        plan = []

        def planned(array, n_tiles, k_tiles, n_cols=P):
            for n in n_tiles:
                for k in range(0, k_tiles, 8):
                    w = min(8, k_tiles - k)
                    plan.append((array[n, :, k * n_cols:(k + w) * n_cols], w * n_cols))

        planned(A["w_ada"], range(24), 8)
        planned(A["w_q"], range(8), 8)
        planned(A["w_k"], range(8), 8)
        planned(A["w_in"], range(28), 8)
        planned(A["w_dt"], range(1), 8, 16)
        planned(A["w_z"], range(8), 8)
        planned(A["w_out"], range(8), 16)
        planned(A["w_rkv"], range(24), 8)
        planned(A["w_w1"], range(1), 8, 64)
        planned(A["w_a1"], range(1), 8, 64)
        planned(A["w_g1"], range(2), 8, 80)
        planned(A["w_o"], range(8), 8)
        planned(A["up0"], [i + j * FT for i in range(FT) for j in range(2)], 8)
        planned(A["down0"], range(FT), 8)
        planned(A["d_in"], range(4), 8)
        planned(A["d_widx"], range(1), 8, 8)
        planned(A["d_uq"], range(8), 2)
        planned(A["d_qidx"], range(4), 2)
        planned(A["d_wo"], range(8), 8)
        planned(A["up1"], [i + j * FT for i in range(FT) for j in range(2)], 8)
        planned(A["down1"], range(FT), 8)
        weight_loaded = [nc.alloc_semaphore(f"weight_loaded{i}") for i in range(RING)]
        weight_used = nc.alloc_semaphore("weight_used")
        stored = nc.alloc_semaphore("out_stored")
        at = {"issued": 0, "used": 0, "ahead": 0}

        def next_chunk(pe):
            i = at["used"]
            pe.wait_ge(weight_loaded[i % RING], 16 * (i // RING + 1))
            at["used"] += 1
            at["ahead"] = max(0, at["ahead"] - 1)
            return ring[:, i % RING, :]

        def run_stage(*programs):
            with nc.Block() as block:
                @block.tensor
                def _(pe):
                    for p in programs:
                        p["tensor"](pe)

                @block.vector
                def _(dve):
                    for p in programs:
                        p["vector"](dve)

                @block.scalar
                def _(act):
                    for p in programs:
                        p["scalar"](act)

                @block.sync
                def _(sp):
                    stream(sp)

        def gemm_program(name, n_tiles, k_tiles, rhs, evac, n_cols=P, prepare=None, rhs_ready=None):
            per = -(-k_tiles // 8)
            first = at["used"] + at["ahead"]
            at["ahead"] += per * n_tiles
            names = list(evac)
            taken = {e: sem(name + "_taken_by_" + e) for e in names}
            who = lambda n: names[n % len(names)]
            nth = lambda n: n // len(names) + 1
            prepared = sem(name + "_prepared") if prepare else None

            def tensor(pe):
                for n in range(n_tiles):
                    if n >= 4:
                        pe.wait_ge(taken[who(n - 4)], nth(n - 4))
                    for k in range(k_tiles):
                        if k % 8 == 0:
                            w = next_chunk(pe)
                        if prepare and n == 0:
                            pe.wait_ge(prepared, k + 1)
                        if rhs_ready and n == 0:
                            rhs_ready(pe, k)
                        mm = nc.tensor.matmul(PS[0:n_cols, n % 4, :], w[:, k % 8 * n_cols:(k % 8 + 1) * n_cols],
                                              rhs(k), start=k == 0, stop=k == k_tiles - 1)
                        if k % 8 == 7 or k == k_tiles - 1:
                            mm.then_inc(weight_used, 1)

            def run(e, eng):
                for n in range(n_tiles):
                    if who(n) == e:
                        eng.wait_ge(weight_used, first + per * (n + 1))
                        evac[e](eng, n, PS[0:n_cols, n % 4, :]).then_inc(taken[e], 1)

            def scalar(act):
                if "act" in evac:
                    run("act", act)

            def vector(dve):
                if prepare:
                    for k in range(k_tiles):
                        prepare(k).then_inc(prepared, 1)
                if "dve" in evac:
                    run("dve", dve)
            return {"tensor": tensor, "vector": vector, "scalar": scalar}

        def gemm(*args, **kw):
            run_stage(gemm_program(*args, **kw))

        def split_program(name, k_tiles, rhs, evac, prepare=None, rhs_ready=None):
            x_high, x_low, w_high, w_low = open_split(name, 7, 2)
            first = at["used"] + at["ahead"]
            at["ahead"] += k_tiles
            (e, take), = evac.items()
            xh_made, xl_made, wh_made, wl_made, prepared, complete = (
                sem(f"{name}_{n}") for n in ("x_high", "x_low", "w_high", "w_low", "prepared", "complete"))

            def tensor(pe):
                for k in range(k_tiles):
                    next_chunk(pe)
                    pe.wait_ge(wl_made, k + 1)
                    pe.wait_ge(xl_made, k + 1)
                    last = k == k_tiles - 1
                    for n in range(8):
                        high, low = (w[:, k % 2, n * P:(n + 1) * P] for w in (w_high, w_low))
                        nc.tensor.matmul(PS[:, n, :], high, x_high[:, k % 2, :], start=k == 0, stop=False)
                        nc.tensor.matmul(PS[:, n, :], high, x_low[:, k % 2, :], start=False, stop=False)
                        mm = nc.tensor.matmul(PS[:, n, :], low, x_high[:, k % 2, :], start=False, stop=last)
                        if last and n < 7:
                            mm.then_inc(complete, 1)
                    mm.then_inc(weight_used, 1)

            def take_all(eng):
                for n in range(8):
                    if n < 7:
                        eng.wait_ge(complete, n + 1)
                    else:
                        eng.wait_ge(weight_used, first + k_tiles)
                    take(eng, n, PS[:, n, :])

            def scalar(act):
                for k in range(k_tiles):
                    i = first + k
                    act.wait_ge(weight_loaded[i % RING], 16 * (i // RING + 1))
                    if k >= 2:
                        act.wait_ge(weight_used, i - 1)
                    nc.scalar.copy(w_high[:, k % 2, :], ring[:, i % RING, :]).then_inc(wh_made, 1)
                    if prepare:
                        act.wait_ge(prepared, k + 1)
                    if rhs_ready:
                        rhs_ready(act, k)
                    nc.scalar.copy(x_high[:, k % 2, :], rhs(k)).then_inc(xh_made, 1)
                if e == "act":
                    take_all(act)

            def vector(dve):
                if prepare:
                    prepare(0).then_inc(prepared, 1)
                for k in range(k_tiles):
                    if prepare and k + 1 < k_tiles:
                        prepare(k + 1).then_inc(prepared, 1)
                    dve.wait_ge(wh_made, k + 1)
                    nc.vector.tensor_tensor(w_low[:, k % 2, :], ring[:, (first + k) % RING, :], w_high[:, k % 2, :].bitcast(f32), ALU.subtract).then_inc(wl_made, 1)
                    dve.wait_ge(xh_made, k + 1)
                    nc.vector.tensor_tensor(x_low[:, k % 2, :], rhs(k), x_high[:, k % 2, :].bitcast(f32), ALU.subtract).then_inc(xl_made, 1)
                if e == "dve":
                    take_all(dve)
            return {"tensor": tensor, "vector": vector, "scalar": scalar}

        def split_gemm(name, *args, **kw):
            run_stage(split_program(name, *args, **kw))
            restore(name)

        def stream(sp):
            while at["issued"] < min(len(plan), at["used"] + RING):
                i = at["issued"]
                src, w = plan[i]
                if i >= RING:
                    sp.wait_ge(weight_used, i - RING + 1)
                sp.dma_start(ring[:, i % RING, 0:w], src).then_inc(weight_loaded[i % RING], 16)
                at["issued"] += 1

        def norm_program(name, x, n_tiles, n_channels, eps, gain, write, centered=False, bias=None, scratch=None):
            summed, squared = sem(name + "_summed"), sem(name + "_squared")
            step, shifted, rooted = sem(name + "_step"), sem(name + "_shifted"), sem(name + "_rooted")
            sq = scratch
            sums = 1 if centered else 0
            before = n_tiles if centered else 0
            def tensor(pe):
                if centered:
                    for i in range(n_tiles):
                        mm = nc.tensor.matmul(PS[:, 4, :], mat("ones"), x(i), start=i == 0, stop=i == n_tiles - 1)
                    mm.then_inc(summed, 1)
                for b in range(NB):
                    for i in range(n_tiles):
                        if b == 0:
                            pe.wait_ge(squared, i + 1)
                        mm = nc.tensor.matmul(PS[:, 5, b:b + 1], sq(i)[:, b * P:(b + 1) * P], mat("ones")[:, 0:1],
                                              start=i == 0, stop=i == n_tiles - 1)
                mm.then_inc(summed, 1)
                pe.wait_ge(step, before + 3)
                nc.tensor.matmul(PS[:, 5, :], mat("ones"), stat[:, 0, :], start=True, stop=True).then_inc(summed, 1)

            def scalar(act):
                for i in range(n_tiles):
                    if centered:
                        act.wait_ge(step, i + 1)
                    nc.scalar.activation(sq(i), x(i), ACT.Square, scale=n_channels ** -0.5).then_inc(squared, 1)
                act.wait_ge(summed, sums + 1)
                act.wait_ge(step, before + 1)
                nc.scalar.activation(small[:, 240:244], PS[:, 5, 0:4], ACT.Sqrt, bias=small[:, 250:251]).then_inc(rooted, 1)
                if bias is not None:
                    for i in range(n_tiles):
                        act.wait_ge(step, before + 4 + i)
                        nc.scalar.activation(write(i), write(i), ACT.Identity, bias=bias(i)).then_inc(shifted, 1)

            def vector(dve):
                if centered:
                    dve.wait_ge(summed, 1)
                    for i in range(n_tiles):
                        nc.vector.scalar_tensor_tensor(out=x(i), in0=PS[:, 4, :], scalar=-1.0 / n_channels, in1=x(i),
                                                       op0=ALU.mult, op1=ALU.add).then_inc(step, 1)
                nc.vector.memset(small[:, 250:251], eps).then_inc(step, 1)
                dve.wait_ge(rooted, 1)
                nc.vector.reciprocal(small[:, 244:248], small[:, 240:244]).then_inc(step, 1)
                dve.wait_ge(step, before + 2)
                nc.vector.tensor_tensor(stat[:, 0, :].rearrange("p (b t) -> p b t", b=NB), mat4("ident"),
                                        small[:, 244:248].unsqueeze(2).to_broadcast([P, NB, P]), ALU.mult).then_inc(step, 1)
                dve.wait_ge(summed, sums + 2)
                for i in range(n_tiles):
                    nc.vector.scalar_tensor_tensor(out=write(i), in0=x(i), scalar=gain(i), in1=PS[:, 5, :],
                                                   op0=ALU.mult, op1=ALU.mult).then_inc(step, 1)

            def written(pe, i):
                if bias is not None:
                    pe.wait_ge(shifted, i + 1)
                else:
                    pe.wait_ge(step, before + 4 + i)
            return {"tensor": tensor, "vector": vector, "scalar": scalar}, written

        def norm(*args, **kw):
            run_stage(norm_program(*args, **kw)[0])

        def loads(name, pairs):
            loaded = sem(name)
            with nc.Block() as block:
                @block.scalar
                def _(act):
                    for dst, src in pairs:
                        act.dma_start(dst, src).then_inc(loaded, 16)
                    act.wait_ge(loaded, 16 * len(pairs))

                @block.sync
                def _(sp):
                    stream(sp)

        def copy_act(dst):
            return lambda eng, n, bank: nc.scalar.copy(dst(n), bank)

        def copy_dve(dst):
            return lambda eng, n, bank: nc.vector.tensor_copy(dst(n), bank)

        class Stop(Exception):
            pass

        def checkpoint(name, ap=None):
            if stop == name:
                w = sem("dumped")
                with nc.Block() as block:
                    @block.sync
                    def _(sp):
                        sp.dma_start(dump, ap).then_inc(w, 16)
                        for i in range(RING):
                            sp.wait_ge(weight_loaded[i], 16 * len(range(i, at["issued"], RING)))
                        sp.wait_ge(w, 16)
                raise Stop

        def rows(t):
            return lambda i: t[:, i, :]

        x, h = F[0], F[1]
        loads("inputs_loaded", [(cols[:, :], A["cols"]), (squares[:, :], A["squares"]), (x[:, :, :], A["xT"]),
                                (late[:, :], A["late"])])

        c_ready, mod_taken = sem("c_ready"), sem("mod_taken")
        first = at["used"]
        with nc.Block() as block:
            @block.scalar
            def _(act):
                nc.scalar.activation(small[:, 0:8], cols[:, COL_AT["c"]:COL_AT["c"] + 8], ACT.Silu).then_inc(c_ready, 1)

            @block.tensor
            def _(pe):
                pe.wait_ge(c_ready, 1)
                for n in range(24):
                    w = next_chunk(pe)
                    for k in range(8):
                        mm = nc.tensor.matmul(PS[:, 0, n:n + 1], w[:, k * P:(k + 1) * P], small[:, k:k + 1], start=k == 0, stop=k == 7)
                    mm.then_inc(weight_used, 1)

            @block.vector
            def _(dve):
                dve.wait_ge(weight_used, first + 24)
                nc.vector.tensor_tensor(mod[:, :], PS[:, 0, 0:24], cols[:, COL_AT["b_ada"]:COL_AT["b_ada"] + 24], ALU.add).then_inc(mod_taken, 1)
                dve.wait_ge(mod_taken, 1)
                nc.vector.scalar_tensor_tensor(out=small[:, 8:16], in0=mod[:, 8:16], scalar=1.0,
                                               in1=cols[:, COL_AT["norm_in_gain"]:COL_AT["norm_in_gain"] + 8],
                                               op0=ALU.add, op1=ALU.mult).then_inc(mod_taken, 1)

            @block.sync
            def _(sp):
                stream(sp)
        norm_in, h_ready = norm_program("norm_in", rows(x), 8, D, 1e-6, lambda i: small[:, 8 + i:9 + i], rows(h),
                                        bias=lambda i: mod[:, i:i + 1], scratch=rows(F[3]))

        q, k_, v = F[2], F[3], F[4]
        run_stage(norm_in, split_program("q", 8, rows(h), {"act": lambda e, n, b: nc.scalar.mul(q[:, n, :], b, HD ** -0.5)},
                                         rhs_ready=h_ready))
        split_gemm("k", 8, rows(h), {"act": copy_act(rows(k_))})

        def gemm_tokens(name, n_tiles, rhs_tokens, dst):
            first = at["used"]
            taken = sem(name + "_taken")
            with nc.Block() as block:
                @block.tensor
                def _(pe):
                    for n in range(n_tiles):
                        if n >= 4:
                            pe.wait_ge(taken, n - 3)
                        w = next_chunk(pe)
                        for b in range(NB):
                            for k in range(8):
                                mm = nc.tensor.matmul(PS[:, n % 4, b * P:(b + 1) * P], rhs_tokens(k, b), w[:, k * P:(k + 1) * P],
                                                      start=k == 0, stop=k == 7)
                        mm.then_inc(weight_used, 1)

                @block.scalar
                def _(act):
                    for n in range(n_tiles):
                        act.wait_ge(weight_used, first + n + 1)
                        nc.scalar.copy(dst(n), PS[:, n % 4, :].rearrange("p (b c) -> p b c", b=NB)).then_inc(taken, 1)

                @block.sync
                def _(sp):
                    stream(sp)

        v_tok = v[:, :, :].rearrange("p a b -> p (a b)").rearrange("p (b c) -> p b c", b=NB)
        gemm_tokens("v", 8, lambda k, b: h[:, k, b * P:(b + 1) * P], lambda n: v_tok[:, :, n * P:(n + 1) * P])
        checkpoint("v", v[:, :, :])

        o = F[5]
        work = F[6][:, :, :].rearrange("p a b -> p (a b)")
        clamped = [work[:, 0:SB_N], work[:, SB_N:2 * SB_N]]
        sp_m = [F[7][:, :, :].rearrange("p a b -> p (a b)")[:, i * SB_N:(i + 1) * SB_N] for i in range(2)]
        wts = [F[8][:, :, :].rearrange("p a b -> p (a b)")[:, i * SB_N:(i + 1) * SB_N] for i in range(2)]
        zb = PS[:, 0:3, :].rearrange("p a b -> p (a b)")
        wb = PS[:, 3:6, :].rearrange("p a b -> p (a b)")
        z_ready, z_taken, sp_step = sem("z_ready"), sem("z_taken"), sem("softplus_step")
        clamp_ready, log_ready, sp_ready = sem("clamp_ready"), sem("log_ready"), sem("sp_ready")
        w_ready, w_clamped, wts_ready = sem("w_ready"), sem("w_clamped"), sem("wts_ready")
        o_ready, o_taken, exp_done, late_masked = sem("o_ready"), sem("o_taken"), sem("sb_exp_done"), sem("sp_masked")
        with nc.Block() as block:
            def head(t, hh, a, b):
                return t[hh % 2 * HD:(hh % 2 + 1) * HD, hh // 2, a:b]

            @block.tensor
            def _(pe):
                def scores(hh, dst, stop):
                    for i in range(NB):
                        mm = nc.tensor.matmul(dst[:, SB_AT[i]:SB_AT[i] + SB_W[i]], head(k_, hh, i * P, (i + 1) * P),
                                              head(q, hh, i * P, T), start=True, stop=stop)
                    return mm

                def products(hh):
                    pe.wait_ge(wts_ready, hh + 1)
                    if hh >= 4 and hh % 2 == 0:
                        pe.wait_ge(o_taken, (hh - 4) // 2 + 1)
                    for i in range(NB):
                        mm = nc.tensor.matmul(PS[hh % 2 * HD:(hh % 2 + 1) * HD, 6 + hh // 2 % 2, i * P:T],
                                              v_tok[:, i, hh * HD:(hh + 1) * HD], wts[hh % 2][:, SB_AT[i]:SB_AT[i] + SB_W[i]],
                                              start=i == 0, stop=i == NB - 1)
                    mm.then_inc(o_ready, 1)

                scores(0, zb, True).then_inc(z_ready, 1)
                pe.wait_ge(sp_ready, 1)
                scores(1, zb, True).then_inc(z_ready, 1)
                for hh in range(H):
                    pe.wait_ge(late_masked, hh + 1)
                    if hh >= 1:
                        pe.wait_ge(w_clamped, hh)
                    for i in range(NB):
                        nc.tensor.matmul(wb[:, SB_AT[i]:SB_AT[i] + SB_W[i]], head(k_, hh, i * P, (i + 1) * P),
                                         head(q, hh, i * P, T), start=True, stop=False)
                        for j in range(i, NB):
                            mm = nc.tensor.matmul(wb[:, SB_AT[i] + (j - i) * P:SB_AT[i] + SB_W[i]],
                                                  mat("neg_ge" if i == j else "neg_ones"),
                                                  sp_m[hh % 2][:, SB_AT[j]:SB_AT[j] + SB_W[j]], start=False, stop=j == NB - 1)
                    mm.then_inc(w_ready, 1)
                    if hh + 2 < H:
                        pe.wait_ge(sp_ready, hh + 2)
                        scores(hh + 2, zb, True).then_inc(z_ready, 1)
                    if hh >= 1:
                        products(hh - 1)
                products(H - 1)

            @block.vector
            def _(dve):
                def softplus(hh):
                    dve.wait_ge(z_ready, hh + 1)
                    if hh >= 2:
                        dve.wait_ge(sp_ready, hh - 1)
                    nc.vector.tensor_scalar(clamped[hh % 2], zb[:, 0:SB_N], 80.0, None, ALU.min).then_inc(clamp_ready, 1)
                    dve.wait_ge(log_ready, hh + 1)
                    if hh >= 2:
                        dve.wait_ge(w_ready, hh - 1)
                    nc.vector.tensor_tensor(sp_m[hh % 2], clamped[hh % 2], zb[:, 0:SB_N], ALU.max).then_inc(sp_ready, 1)
                softplus(0)
                for hh in range(H):
                    if hh + 1 < H:
                        softplus(hh + 1)
                    dve.wait_ge(w_ready, hh + 1)
                    if hh >= 2:
                        dve.wait_ge(o_ready, hh - 1)
                    nc.vector.scalar_tensor_tensor(out=wts[hh % 2], in0=wb[:, 0:SB_N], scalar=0.0, in1=late[:, :],
                                                   op0=ALU.min, op1=ALU.add).then_inc(w_clamped, 1)

            @block.scalar
            def _(act):
                def out_pair(p):
                    act.wait_ge(o_ready, 2 * p + 2)
                    nc.scalar.copy(o[:, p, :], PS[:, 6 + p % 2, :]).then_inc(o_taken, 1)

                def logs(hh):
                    act.wait_ge(clamp_ready, hh + 1)
                    nc.scalar.activation(clamped[hh % 2], clamped[hh % 2], ACT.Exp).then_inc(exp_done, 1)
                    act.wait_ge(exp_done, hh + 1)
                    nc.scalar.activation(clamped[hh % 2], clamped[hh % 2], ACT.Ln, bias=1.0).then_inc(log_ready, 1)
                logs(0)
                for hh in range(H):
                    if hh + 1 < H:
                        logs(hh + 1)
                    act.wait_ge(w_clamped, hh + 1)
                    nc.scalar.activation(wts[hh % 2], wts[hh % 2], ACT.Exp).then_inc(wts_ready, 1)
                    if hh % 2 == 0 and hh >= 2:
                        out_pair(hh // 2 - 1)
                out_pair(H // 2 - 1)

            @block.gpsimd
            def _(pool):
                for hh in range(H):
                    pool.wait_ge(sp_ready, hh + 1)
                    for a, n in ((0, 1), (512, 1), (896, 2)):
                        part = sp_m[hh % 2][:, a:a + n * P].rearrange("p (n c) -> p n c", c=P)
                        last = nc.gpsimd.tensor_tensor(part, part, mat("lt").unsqueeze(1).to_broadcast([P, n, P]), ALU.mult)
                    last.then_inc(late_masked, 1)
        checkpoint("o", o[:, :, :])

        def conv_program(name, n_tiles, rhs, taps, w_col, b_col, dst, pair_out=None, split=None):
            first = at["used"] + at["ahead"]
            at["ahead"] += n_tiles
            step, silu_done = sem(name + "_step"), sem(name + "_silu")
            per_pair = 2 * taps + 1
            if split:
                x_high, x_low, w_high, w_low, x_src, x_ready = split
                xh_made, xl_made, wh_made, wl_made = (sem(f"{name}_{n}") for n in ("x_high", "x_low", "w_high", "w_low"))

            def high_of_weights(n):
                i = first + n
                nc.scalar.wait_ge(weight_loaded[i % RING], 16 * (i // RING + 1))
                if n >= 2:
                    nc.scalar.wait_ge(weight_used, i - 1)
                nc.scalar.copy(w_high[:, n % 2, :], ring[:, i % RING, :]).then_inc(wh_made, 1)

            def low_of_weights(n):
                i = first + n
                nc.vector.wait_ge(wh_made, n + 1)
                nc.vector.tensor_tensor(w_low[:, n % 2, :], ring[:, i % RING, :], w_high[:, n % 2, :].bitcast(f32), ALU.subtract).then_inc(wl_made, 1)

            def steps(n):
                return n // 2 * per_pair + taps * (n % 2 + 1) if pair_out else taps * (n + 1)

            def tensor(pe):
                for n in range(n_tiles):
                    if n >= 4:
                        pe.wait_ge(step, steps(n - 4))
                    w = next_chunk(pe)
                    if split:
                        pe.wait_ge(wl_made, n + 1)
                    for k in range(8):
                        if split:
                            if n == 0:
                                pe.wait_ge(xl_made, k + 1)
                            high, low = (w[:, n % 2, k * P:(k + 1) * P] for w in (w_high, w_low))
                            nc.tensor.matmul(PS[:, n % 4, :], high, x_high[:, k, :], start=k == 0, stop=False)
                            nc.tensor.matmul(PS[:, n % 4, :], high, x_low[:, k, :], start=False, stop=False)
                            mm = nc.tensor.matmul(PS[:, n % 4, :], low, x_high[:, k, :], start=False, stop=k == 7)
                        else:
                            mm = nc.tensor.matmul(PS[:, n % 4, :], w[:, k * P:(k + 1) * P], rhs(k), start=k == 0, stop=k == 7)
                    mm.then_inc(weight_used, 1)

            def vector(dve):
                if split:
                    for n in range(2):
                        low_of_weights(n)
                    for k in range(8):
                        dve.wait_ge(xh_made, k + 1)
                        nc.vector.tensor_tensor(x_low[:, k, :], x_src(k), x_high[:, k, :].bitcast(f32), ALU.subtract).then_inc(xl_made, 1)
                for n in range(n_tiles):
                    dve.wait_ge(weight_used, first + n + 1)
                    if split and n + 2 < n_tiles:
                        low_of_weights(n + 2)
                    nc.vector.tensor_scalar(dst(n), PS[:, n % 4, :], w_col(n, taps - 1), b_col(n), ALU.mult, ALU.add).then_inc(step, 1)
                    for j in range(1, taps):
                        dve.wait_ge(step, steps(n) - taps + j)
                        nc.vector.scalar_tensor_tensor(out=dst(n)[:, j:], in0=PS[:, n % 4, 0:T - j], scalar=w_col(n, taps - 1 - j),
                                                       in1=dst(n)[:, j:], op0=ALU.mult, op1=ALU.add).then_inc(step, 1)
                    if pair_out and n % 2 == 1:
                        dve.wait_ge(silu_done, n // 2 + 1)
                        dve.wait_ge(step, steps(n))
                        nc.vector.tensor_tensor(pair_out(n // 2), dst(n - 1), dst(n), ALU.mult).then_inc(step, 1)

            def scalar(act):
                if split:
                    for n in range(2):
                        high_of_weights(n)
                    for k in range(8):
                        if x_ready:
                            x_ready(act, k)
                        nc.scalar.copy(x_high[:, k, :], x_src(k)).then_inc(xh_made, 1)
                for n in range(n_tiles):
                    if split and n + 2 < n_tiles:
                        high_of_weights(n + 2)
                    if pair_out and n % 2 == 1:
                        continue
                    act.wait_ge(step, steps(n))
                    nc.scalar.activation(dst(n), dst(n), ACT.Silu).then_inc(silu_done, 1)
            return {"tensor": tensor, "vector": vector, "scalar": scalar}

        def conv_gemm(*args, **kw):
            run_stage(conv_program(*args, **kw))

        def multiply(name, dst, a, b):
            with nc.Block() as block:
                @block.vector
                def _(dve):
                    nc.vector.tensor_tensor(dst, a, b, ALU.mult)

                @block.sync
                def _(sp):
                    stream(sp)

        y_attn = F[2]
        run_stage(norm_program("norm_sb", rows(o), 8, D, 1e-6, lambda i: col("sb_norm_gain", i), rows(y_attn), scratch=rows(F[4]))[0],
                  gemm_program("z_attn", 8, 8, rows(h), {"act": lambda e, n, b: nc.scalar.activation(F[3][:, n, :], b, ACT.Silu)}))
        multiply("gate_attn", y_attn[:, :, :], y_attn[:, :, :], F[3][:, :, :])
        checkpoint("ya", y_attn[:, :, :])
        xs, bc = F[3], F[4]
        run_stage(conv_program("xbc", 12, None, 4, lambda n, j: col("conv_w", j * 12 + n), lambda n: col("conv_b", n),
                               lambda n: xs[:, n, :] if n < 8 else bc[:, n - 8, :], split=(*open_split("xbc", 5, KT), rows(h), None)))
        restore("after_conv")
        checkpoint("xbc", xs[:, :, :])

        flat = lambda t: t[:, :, :].rearrange("p a b -> p (a b)")
        sdt = flat(F[7])
        slot = lambda i: sdt[:, i * 64:(i + 1) * 64]
        by_block = lambda ap: ap.rearrange("p (b h) -> p b h", b=NB)
        over_blocks = lambda name: cols[:, COL_AT[name]:COL_AT[name] + H].unsqueeze(1).to_broadcast([P, NB, H])
        z_, m_, dt_, ea_, da_ = (slot(i) for i in range(5))
        dt_step, dt_act = sem("dt_step"), sem("dt_act")
        first = at["used"]
        with nc.Block() as block:
            @block.tensor
            def _(pe):
                w = next_chunk(pe)
                for b in range(NB):
                    for k in range(8):
                        mm = nc.tensor.matmul(PS[:, 0, b * H:(b + 1) * H], h[:, k, b * P:(b + 1) * P], w[:, k * H:(k + 1) * H], start=k == 0, stop=k == 7)
                mm.then_inc(weight_used, 1)

            @block.scalar
            def _(act):
                nc.scalar.activation(by_block(ea_), over_blocks("a_log"), ACT.Exp).then_inc(dt_act, 1)
                act.wait_ge(dt_step, 2)
                nc.scalar.activation(m_, m_, ACT.Exp).then_inc(dt_act, 1)
                act.wait_ge(dt_act, 2)
                nc.scalar.activation(m_, m_, ACT.Ln, bias=1.0).then_inc(dt_act, 1)

            @block.vector
            def _(dve):
                dve.wait_ge(weight_used, first + 1)
                nc.vector.tensor_tensor(by_block(z_), by_block(PS[:, 0, 0:64]), over_blocks("dt_bias"), ALU.add).then_inc(dt_step, 1)
                dve.wait_ge(dt_step, 1)
                nc.vector.tensor_scalar(m_, z_, 80.0, None, ALU.min).then_inc(dt_step, 1)
                dve.wait_ge(dt_act, 3)
                nc.vector.tensor_tensor(dt_, m_, z_, ALU.max).then_inc(dt_step, 1)
                dve.wait_ge(dt_step, 3)
                nc.vector.scalar_tensor_tensor(out=da_, in0=dt_, scalar=-1.0, in1=ea_, op0=ALU.mult, op1=ALU.mult).then_inc(dt_step, 1)

            @block.sync
            def _(sp):
                stream(sp)

        y = F[5]
        state = sdt[:, 512:1536]
        acum, total, cend, etot = sdt[:, 320:336], sdt[:, 336:352], sdt[:, 352:368], sdt[:, 368:384]
        b_tok = sdt[:, 1536:1792]
        cb = sdt[:, 1792:2048]
        x_dt, x_end = sdt[:, 2048:3072], sdt[:, 3072:4096]
        seg, c_exp = flat(F[6])[:, 0:2048], flat(F[6])[:, 2048:4096]
        per_head = lambda ap, w: ap.unsqueeze(2).to_broadcast([P, ap.shape[1], w])
        zeroed = sem("state_zeroed")
        with nc.Block() as block:
            @block.vector
            def _(dve):
                nc.vector.memset(state, 0.0).then_inc(zeroed, 1)
        for c in range(NB):
            t0, t1 = c * P, (c + 1) * P
            da_c, dt_c = da_[:, c * H:(c + 1) * H], dt_[:, c * H:(c + 1) * H]
            cums, moved, cbs, broad = (sem(f"scan{c}_{n}") for n in ("cums", "moved", "cb", "broadcast"))
            vec, sca, outs, states = (sem(f"scan{c}_{n}") for n in ("vec", "act", "y_ready", "state_ready"))
            with nc.Block() as block:
                @block.tensor
                def _(pe):
                    nc.tensor.matmul(PS[:, 0, 0:16], mat("le"), da_c, start=True, stop=True)
                    nc.tensor.matmul(PS[:, 0, 16:32], mat("ones"), da_c, start=True, stop=True).then_inc(cums, 1)
                    for i in range(8):
                        mm = nc.tensor.transpose(PS[:, 1 + i // 4, i % 4 * P:(i % 4 + 1) * P], xs[:, i, t0:t1], mat("ident"))
                        if i == 7:
                            mm.then_inc(moved, 1)
                    for g in range(2):
                        nc.tensor.transpose(PS[:, 3, g * P:(g + 1) * P], bc[:, g, t0:t1], mat("ident"))
                    for g in range(2):
                        mm = nc.tensor.matmul(PS[:, 3, (2 + g) * P:(3 + g) * P], bc[:, g, t0:t1], bc[:, 2 + g, t0:t1], start=True, stop=True)
                    mm.then_inc(cbs, 1)
                    for hh in range(H):
                        mm = nc.tensor.matmul(PS[:, 4 + hh // 4, hh % 4 * P:(hh % 4 + 1) * P],
                                              da_c[:, hh:hh + 1].to_broadcast([P, P]), mat("le"), start=True, stop=True)
                        if hh % 4 == 3:
                            mm.then_inc(broad, 1)

                @block.vector
                def _(dve):
                    dve.wait_ge(cums, 1)
                    nc.vector.tensor_copy(sdt[:, 320:352], PS[:, 0, 0:32]).then_inc(vec, 1)
                    dve.wait_ge(vec, 1)
                    nc.vector.tensor_tensor(cend, total, acum, ALU.subtract).then_inc(vec, 1)
                    dve.wait_ge(moved, 1)
                    nc.vector.tensor_tensor(x_dt.rearrange("p (h c) -> p h c", h=H),
                                            PS[:, 1:3, :].rearrange("p a (h c) -> p (a h) c", c=HD), per_head(dt_c, HD), ALU.mult).then_inc(vec, 1)
                    dve.wait_ge(cbs, 1)
                    nc.vector.tensor_tensor(cb.rearrange("p (g l) -> p g l", g=2), PS[:, 3, 2 * P:4 * P].rearrange("p (g l) -> p g l", g=2),
                                            mat("le").unsqueeze(1).to_broadcast([P, 2, P]), ALU.mult).then_inc(vec, 1)
                    dve.wait_ge(sca, 2)
                    dve.wait_ge(vec, 4)
                    nc.vector.tensor_tensor(x_end.rearrange("p (h c) -> p h c", h=H), x_dt.rearrange("p (h c) -> p h c", h=H),
                                            per_head(cend, HD), ALU.mult).then_inc(vec, 1)
                    for q4 in range(4):
                        dve.wait_ge(broad, q4 + 1)
                        part = seg[:, q4 * T:(q4 + 1) * T]
                        nc.vector.tensor_tensor(part.rearrange("p (h l) -> p h l", h=4), PS[:, 4 + q4, :].rearrange("p (h l) -> p h l", h=4),
                                                per_head(acum[:, q4 * 4:q4 * 4 + 4], P), ALU.subtract).then_inc(vec, 1)
                        dve.wait_ge(vec, 6 + 2 * q4)
                        nc.vector.tensor_scalar(part, part, 0.0, None, ALU.min).then_inc(vec, 1)
                    for q4 in range(4):
                        dve.wait_ge(sca, 5 + 2 * q4)
                        for t, m in ((seg, cb[:, q4 // 2 * P:(q4 // 2 + 1) * P]), (c_exp, bc[:, 2 + q4 // 2, t0:t1])):
                            part = t[:, q4 * T:(q4 + 1) * T].rearrange("p (h l) -> p h l", h=4)
                            nc.vector.tensor_tensor(part, part, m.unsqueeze(1).to_broadcast([P, 4, P]), ALU.mult).then_inc(vec, 1)
                    for i in range(8):
                        if i % 4 == 0:
                            dve.wait_ge(outs, i // 4 + 1)
                        nc.vector.scalar_tensor_tensor(out=y[:, i, t0:t1], in0=xs[:, i, t0:t1], scalar=col("d_skip", i),
                                                       in1=PS[:, 1 + i // 4, i % 4 * P:(i % 4 + 1) * P], op0=ALU.mult, op1=ALU.add).then_inc(vec, 1)
                    dve.wait_ge(outs, 2)
                    sv = state.rearrange("p (h c) -> p h c", h=H)
                    nc.vector.tensor_tensor(sv, sv, per_head(etot, HD), ALU.mult).then_inc(vec, 1)
                    dve.wait_ge(states, 1)
                    dve.wait_ge(vec, 30)
                    for g in range(2):
                        nc.vector.tensor_tensor(state[:, g * T:(g + 1) * T], state[:, g * T:(g + 1) * T], PS[:, 6 + g, :], ALU.add).then_inc(vec, 1)

                @block.scalar
                def _(act):
                    act.wait_ge(vec, 1)
                    nc.scalar.activation(etot, total, ACT.Exp).then_inc(sca, 1)
                    act.wait_ge(vec, 2)
                    nc.scalar.activation(cend, cend, ACT.Exp).then_inc(sca, 1)
                    act.wait_ge(vec, 4)
                    nc.scalar.copy(b_tok, PS[:, 3, 0:2 * P]).then_inc(sca, 1)
                    for q4 in range(4):
                        act.wait_ge(vec, 6 + 2 * q4)
                        nc.scalar.activation(c_exp[:, q4 * T:(q4 + 1) * T], PS[:, 4 + q4, :], ACT.Exp).then_inc(sca, 1)
                        act.wait_ge(vec, 7 + 2 * q4)
                        part = seg[:, q4 * T:(q4 + 1) * T]
                        nc.scalar.activation(part, part, ACT.Exp).then_inc(sca, 1)

                @block.tensor
                def _(pe):
                    for hh in range(H):
                        if hh % 4 == 0:
                            pe.wait_ge(vec, 15 + 2 * (hh // 4))
                        dst = PS[hh % 2 * HD:(hh % 2 + 1) * HD, 1 + hh // 8, hh // 2 % 4 * P:(hh // 2 % 4 + 1) * P]
                        nc.tensor.matmul(dst, x_dt[:, hh * HD:(hh + 1) * HD], seg[:, hh * P:(hh + 1) * P], start=True, stop=False)
                        mm = nc.tensor.matmul(dst, state[:, hh * HD:(hh + 1) * HD], c_exp[:, hh * P:(hh + 1) * P], start=False, stop=True)
                        if hh % 8 == 7:
                            mm.then_inc(outs, 1)
                    pe.wait_ge(sca, 11)
                    for g in range(2):
                        mm = nc.tensor.matmul(PS[:, 6 + g, :], b_tok[:, g * P:(g + 1) * P], x_end[:, g * T:(g + 1) * T], start=True, stop=True)
                    mm.then_inc(states, 1)
        checkpoint("yssd", y[:, :, :])

        split_gemm("z_ssm", 8, rows(h), {"act": lambda e, n, b: nc.scalar.activation(F[3][:, n, :], b, ACT.Silu)})
        multiply("gate_ssm", F[3][:, :, :], F[3][:, :, :], y[:, :, :])
        y_ssm = F[4]
        norm_ssm, y_ssm_ready = norm_program("norm_ssm", rows(F[3]), 8, D, 1e-6, lambda i: col("ssm_norm_gain", i), rows(y_ssm),
                                             scratch=rows(F[6]))
        run_stage(norm_ssm, gemm_program("w_out", 8, 16, lambda k: y_attn[:, k, :] if k < 8 else y_ssm[:, k - 8, :],
             {"dve": lambda e, n, b: nc.vector.scalar_tensor_tensor(out=x[:, n, :], in0=b, scalar=mod[:, 16 + n:17 + n], in1=x[:, n, :],
                                                                    op0=ALU.mult, op1=ALU.add)},
             rhs_ready=lambda pe, k: y_ssm_ready(pe, k - 8) if k >= 8 else None))
        norm("norm_f", rows(x), 8, D, 1e-6, lambda i: col("norm_f_gain", i), rows(x), scratch=rows(F[6]))
        checkpoint("x1", x[:, :, :])
        end_section()

        r, kx, v, xx, xm, a_, sig, tmp = F[1:9]
        ALL = lambda t: t[:, :, :]

        def differences(dst):
            with nc.Block() as block:
                @block.vector
                def _(dve):
                    nc.vector.tensor_tensor(dst[:, :, 1:T], x[:, :, 0:T - 1], x[:, :, 1:T], ALU.subtract)
                    nc.vector.tensor_scalar(dst[:, :, 0:1], x[:, :, 0:1], -1.0, None, ALU.mult)

                @block.sync
                def _(sp):
                    stream(sp)

        def mixed(dst, diff, branch):
            return lambda k: nc.vector.scalar_tensor_tensor(out=dst[:, k, :], in0=diff[:, k, :], scalar=col("mix", branch * 8 + k),
                                                            in1=x[:, k, :], op0=ALU.mult, op1=ALU.add)

        def lora_out(name, parts, evac):
            ready, taken = sem(name + "_ready"), sem(name + "_taken")
            with nc.Block() as block:
                @block.tensor
                def _(pe):
                    for n in range(8):
                        if n >= 4:
                            pe.wait_ge(taken, n - 3)
                        for j, (w, hid) in enumerate(parts):
                            mm = nc.tensor.matmul(PS[:, n % 4, :], w[:, n * P:(n + 1) * P], hid, start=j == 0, stop=j == len(parts) - 1)
                        mm.then_inc(ready, 1)

                def run(eng):
                    for n in range(8):
                        eng.wait_ge(ready, n + 1)
                        evac["act" if "act" in evac else "dve"](eng, n, PS[:, n % 4, :]).then_inc(taken, 1)

                if "act" in evac:
                    @block.scalar
                    def _(act):
                        run(act)
                else:
                    @block.vector
                    def _(dve):
                        run(dve)

        differences(xx)
        for b, (name, dst) in enumerate((("r", r), ("k7", kx), ("v7", v))):
            split_gemm(name, 8, rows(xm), {"act": copy_act(rows(dst))}, prepare=mixed(xm, xx, b))
        a_, sig, tmp = F[6:9]
        lw = flat(tmp)
        w2_, a2_, hid_w, hid_a = lw[0:64, 0:D], lw[0:64, D:2 * D], lw[0:64, 2 * D:2 * D + T], lw[0:64, 2 * D + T:3 * D]
        loads("lora_loaded", [(w2_, A["w_w2"]), (a2_, A["w_a2"])])
        gemm("lora_w", 1, 8, rows(xm), {"act": lambda e, n, b: nc.scalar.activation(hid_w, b, ACT.Tanh)}, n_cols=64, prepare=mixed(xm, xx, 3))
        lora_out("decay", [(w2_, hid_w)], {"act": lambda e, n, b: nc.scalar.activation(sig[:, n, :], b, ACT.Sigmoid, bias=col("w0", n))})
        gemm("lora_a", 1, 8, rows(xm), {"act": copy_act(lambda n: hid_a)}, n_cols=64, prepare=mixed(xm, xx, 4))
        lora_out("rate", [(a2_, hid_a)], {"act": lambda e, n, b: nc.scalar.activation(a_[:, n, :], b, ACT.Sigmoid, bias=col("a0", n))})

        kk, bonus = xm, xx
        e1, e2, e3 = sem("kk_vec"), sem("kk_act"), sem("kk_sums")
        of_heads, to_heads = aux[:, 1024:1024 + KT * H], aux[0:H, 0:D]
        sums16 = aux[0:H, 1280:1280 + T]
        loads("selectors_loaded", [(of_heads, A["of_heads"]), (to_heads, A["to_heads"])])
        with nc.Block() as block:
            @block.vector
            def _(dve):
                for i in range(8):
                    nc.vector.tensor_scalar(kk[:, i, :], kx[:, i, :], col("k_k", i), None, ALU.mult).then_inc(e1, 1)
                dve.wait_ge(e2, 9)
                nc.vector.tensor_scalar(sums16, sums16, 1e-12, None, ALU.max).then_inc(e1, 1)
                dve.wait_ge(e1, 9)
                nc.vector.reciprocal(sums16, sums16).then_inc(e1, 1)
                dve.wait_ge(e3, 2)
                nc.vector.tensor_tensor(ALL(kk), ALL(kk), PS[:, :, :], ALU.mult).then_inc(e1, 1)
                dve.wait_ge(e1, 11)
                for i in range(8):
                    nc.vector.tensor_scalar(tmp[:, i, :], a_[:, i, :], 1.0, col("k_a", i), ALU.subtract, ALU.mult).then_inc(e1, 1)
                dve.wait_ge(e1, 19)
                nc.vector.scalar_tensor_tensor(out=ALL(kx), in0=ALL(tmp), scalar=1.0, in1=ALL(kx), op0=ALU.add, op1=ALU.mult).then_inc(e1, 1)
                dve.wait_ge(e1, 20)
                for i in range(8):
                    nc.vector.scalar_tensor_tensor(out=tmp[:, i, :], in0=r[:, i, :], scalar=col("r_k", i), in1=kx[:, i, :],
                                                   op0=ALU.mult, op1=ALU.mult).then_inc(e1, 1)
                dve.wait_ge(e3, 3)
                nc.vector.tensor_tensor(ALL(bonus), PS[:, :, :], ALL(v), ALU.mult).then_inc(e1, 1)

            @block.scalar
            def _(act):
                for i in range(8):
                    act.wait_ge(e1, i + 1)
                    nc.scalar.activation(tmp[:, i, :], kk[:, i, :], ACT.Square).then_inc(e2, 1)
                act.wait_ge(e3, 1)
                nc.scalar.activation(sums16, PS[0:H, 0, :], ACT.Sqrt).then_inc(e2, 1)

            @block.tensor
            def _(pe):
                for i in range(8):
                    pe.wait_ge(e2, i + 1)
                    mm = nc.tensor.matmul(PS[0:H, 0, :], of_heads[:, i * H:(i + 1) * H], tmp[:, i, :], start=i == 0, stop=i == 7)
                mm.then_inc(e3, 1)
                pe.wait_ge(e1, 10)
                for i in range(8):
                    mm = nc.tensor.matmul(PS[:, i, :], to_heads[:, i * P:(i + 1) * P], sums16, start=True, stop=True)
                mm.then_inc(e3, 1)
                pe.wait_ge(e1, 11)
                for i in range(8):
                    pe.wait_ge(e1, 21 + i)
                    mm = nc.tensor.matmul(PS[:, i, :], mat("head_ones"), tmp[:, i, :], start=True, stop=True)
                mm.then_inc(e3, 1)

        ch = lambda t: t[:, :, :].rearrange("p a (c l) -> p (a c) l", c=NB)
        mid, e_mid, e_end, fac = (small[:, 16 + 32 * i:48 + 32 * i] for i in range(4))
        s1, s2 = sem("decay_vec"), sem("decay_act")
        with nc.Block() as block:
            @block.vector
            def _(dve):
                for i in range(8):
                    for c in range(NB):
                        part = slice(c * P, (c + 1) * P)
                        nc.vector.tensor_tensor_scan(tmp[:, i, part], mat("ones"), sig[:, i, part], 0.0, ALU.mult, ALU.add).then_inc(s1, 1)
                dve.wait_ge(s1, 32)
                nc.vector.tensor_copy(mid.unsqueeze(2), ch(tmp)[:, :, 63:64]).then_inc(s1, 1)
                dve.wait_ge(s1, 33)
                nc.vector.tensor_tensor(ch(tmp), ch(tmp), mid.unsqueeze(2).to_broadcast([P, 32, P]), ALU.subtract).then_inc(s1, 1)
                dve.wait_ge(s1, 34)
                nc.vector.tensor_tensor(ALL(sig), ALL(tmp), ALL(sig), ALU.subtract).then_inc(s1, 1)
                nc.vector.tensor_tensor(ALL(a_), ALL(a_), ALL(kk), ALU.mult).then_inc(s1, 1)
                dve.wait_ge(s1, 36)
                dve.wait_ge(s2, 1)
                nc.vector.scalar_tensor_tensor(out=ALL(kk), in0=ALL(sig), scalar=-1.0, in1=ALL(kk), op0=ALU.mult, op1=ALU.mult).then_inc(s1, 1)
                dve.wait_ge(s2, 2)
                nc.vector.tensor_tensor(ALL(a_), ALL(a_), ALL(sig), ALU.mult).then_inc(s1, 1)
                nc.vector.tensor_tensor(ALL(kx), ALL(kx), ALL(sig), ALU.mult).then_inc(s1, 1)
                dve.wait_ge(s2, 3)
                nc.vector.tensor_tensor(ALL(r), ALL(r), ALL(tmp), ALU.mult).then_inc(s1, 1)
                nc.vector.tensor_copy(e_end.unsqueeze(2), ch(tmp)[:, :, P - 1:P]).then_inc(s1, 1)
                dve.wait_ge(s1, 41)
                dve.wait_ge(s2, 4)
                by_c = lambda t: t.rearrange("p (a c) -> p a c", c=NB)
                nc.vector.tensor_tensor(by_c(fac)[:, :, 0:NB - 1], by_c(e_end)[:, :, 0:NB - 1], by_c(e_mid)[:, :, 1:NB], ALU.mult).then_inc(s1, 1)

            @block.scalar
            def _(act):
                act.wait_ge(s1, 35)
                nc.scalar.activation(ALL(sig), ALL(sig), ACT.Exp, scale=-C0).then_inc(s2, 1)
                act.wait_ge(s1, 37)
                nc.scalar.activation(ALL(sig), ALL(tmp), ACT.Exp, scale=C0).then_inc(s2, 1)
                act.wait_ge(s2, 2)
                nc.scalar.activation(ALL(tmp), ALL(tmp), ACT.Exp, scale=-C0).then_inc(s2, 1)
                nc.scalar.activation(e_mid, mid, ACT.Exp, scale=-C0).then_inc(s2, 1)

        rt, kt, at_, bt = r, kx, kk, a_
        UNITS = 2 * NB
        LEVELS = 7
        held = [[flat(t)[:, i * 1024:(i + 1) * 1024] for i in range(4)] for t in (sig, tmp)]
        N_, GT, Q = flat(stat_t), late[:, 0:1024], aux[:, 2560:3584]
        k_tok, b_tok, W_, U_ = (aux[:, i * T:(i + 1) * T] for i in range(4))
        S_ = [aux[:, 2048 + i * 256:2048 + (i + 1) * 256] for i in range(2)]
        names = ["grams", "gram_moved", "start_made", "q_made", "q_moved", "g_made", "g_moved", "gt_moved",
                 "turned", "turned_moved", "w_made", "w_moved", "u_made", "u_moved", "y_made", "y_moved", "s_made", "s_moved"]
        (grams, gram_moved, start_made, q_made, q_moved, g_made, g_moved, gt_moved, turned, turned_moved, w_made, w_moved,
         u_made, u_moved, y_made, y_moved, s_made, s_moved) = (sem("wkv_" + n) for n in names)
        s_zero = sem("wkv_state_zeroed")
        with nc.Block() as block:
            @block.vector
            def _(dve):
                nc.vector.memset(aux[:, 2048:2560], 0.0).then_inc(s_zero, 1)
        four = lambda t, g: t[:, g * T:(g + 1) * T].rearrange("p (h l) -> p h l", h=4)
        bank4 = lambda b: PS[:, b, :].rearrange("p (h l) -> p h l", h=4)
        at_group = lambda j: j % 2 * 4 + j // 2
        half_p = lambda j: slice(j % 2 * HD, (j % 2 + 1) * HD)
        group_cols = lambda j, w: slice(at_group(j) * w, (at_group(j) + 1) * w)
        span = lambda u: slice(u // 2 * P, (u // 2 + 1) * P)

        def of_head(t, u, j):
            return t[half_p(j), u % 2 * 4 + j // 2, span(u)]

        def v_tok(u, j):
            return v[:, u % 2 * 4 + j // 2, u // 2 * P + j % 2 * HD:u // 2 * P + (j % 2 + 1) * HD]

        def has_next(u):
            return u // 2 < NB - 1

        with nc.Block() as block:
            @block.tensor
            def _(pe):
                def gram(u, bank, g, l_, r_):
                    for j in range(4):
                        mm = nc.tensor.matmul(PS[:, bank, j * P:(j + 1) * P], of_head(l_, u, 2 * j + g), of_head(r_, u, 2 * j + g), start=True, stop=True)
                    mm.then_inc(grams, 1)

                def all_grams(u):
                    if u:
                        pe.wait_ge(g_moved, 12 * u)
                    for g in range(2):
                        gram(u, g, g, bt, at_)
                        gram(u, 2 + g, g, at_, bt)
                        gram(u, 4 + g, g, kt, at_)
                    for g in range(2):
                        pe.wait_ge(gram_moved, 10 * u + 3 * g + 1)
                        gram(u, g, g, bt, rt)
                    for g in range(2):
                        pe.wait_ge(gram_moved, 10 * u + 3 * g + 2)
                        gram(u, 2 + g, g, kt, rt)

                def q_level(u, l):
                    for g in range(2):
                        if l == 1:
                            pe.wait_ge(start_made, 6 * u + 3 * g + 3)
                            pe.wait_ge(gram_moved, 10 * u + 7 + g)
                        else:
                            pe.wait_ge(gt_moved, 10 * u + 2 * (l - 2) + g + 1)
                        for j in range(4):
                            mm = nc.tensor.matmul(PS[:, g, j * P:(j + 1) * P], four(N_, g)[:, j, :], four(GT, g)[:, j, :], start=True, stop=True)
                        mm.then_inc(q_made, 1)

                def g_level(u, l):
                    G = held[u % 2][0]
                    for g in range(2):
                        pe.wait_ge(q_moved, 12 * u + 2 * (l - 1) + g + 1)
                        if l == 1:
                            pe.wait_ge(gram_moved, 10 * u + 9 + g)
                        else:
                            pe.wait_ge(g_moved, 12 * u + 2 * (l - 2) + g + 1)
                        for j in range(4):
                            mm = nc.tensor.matmul(PS[:, 2 + g, j * P:(j + 1) * P], four(Q, g)[:, j, :], four(G, g)[:, j, :], start=True, stop=True)
                        if l < LEVELS - 1:
                            for j in range(4):
                                mm = nc.tensor.matmul(PS[:, 4 + g, j * P:(j + 1) * P], four(G, g)[:, j, :], four(Q, g)[:, j, :], start=True, stop=True)
                        mm.then_inc(g_made, 1)

                def carry(u, step):
                    G, Rb, Rk, Ak = held[u % 2]
                    S = S_[u % 2]
                    if step == 1:
                        if u:
                            pe.wait_ge(s_moved, 2 * min(u, UNITS - 2))
                            pe.wait_ge(y_moved, u)
                        for n, (bank, t) in enumerate(((6, v), (7, kt), (6, bt))):
                            if n == 2:
                                pe.wait_ge(turned_moved, 3 * u + 1)
                            for i in range(4):
                                mm = nc.tensor.transpose(PS[:, bank, i * P:(i + 1) * P], t[:, u % 2 * 4 + i, span(u)], mat("ident"))
                            mm.then_inc(turned, 1)
                    elif step == 2:
                        pe.wait_ge(turned_moved, 3 * u + 3)
                        for j in range(8):
                            dst = PS[:, 6 + j % 2, j // 2 * HD:(j // 2 + 1) * HD]
                            nc.tensor.matmul(dst, of_head(at_, u, j), S[half_p(j), j // 2 * HD:(j // 2 + 1) * HD], start=True, stop=False)
                            mm = nc.tensor.matmul(dst, Ak[:, group_cols(j, P)], v_tok(u, j), start=False, stop=True)
                        mm.then_inc(w_made, 1)
                    elif step == 3:
                        pe.wait_ge(w_moved, u + 1)
                        for j in range(8):
                            mm = nc.tensor.matmul(PS[:, 6, j * HD:(j + 1) * HD], G[:, j * P:(j + 1) * P], W_[:, j * HD:(j + 1) * HD], start=True, stop=True)
                        mm.then_inc(u_made, 1)
                    elif step == 4:
                        pe.wait_ge(u_moved, u + 1)
                        for j in range(8):
                            dst = PS[half_p(j), 7, j // 2 * P:(j // 2 + 1) * P]
                            nc.tensor.matmul(dst, S[half_p(j), j // 2 * HD:(j // 2 + 1) * HD], of_head(rt, u, j), start=True, stop=False)
                            nc.tensor.matmul(dst, v_tok(u, j), Rk[:, group_cols(j, P)], start=False, stop=False)
                            mm = nc.tensor.matmul(dst, U_[:, group_cols(j, HD)], Rb[:, group_cols(j, P)], start=False, stop=True)
                        mm.then_inc(y_made, 1)
                    elif step == 5 and has_next(u):
                        for j in range(8):
                            dst = PS[half_p(j), 6, j // 2 * HD:(j // 2 + 1) * HD]
                            nc.tensor.matmul(dst, b_tok[:, j * HD:(j + 1) * HD], U_[:, group_cols(j, HD)], start=True, stop=False)
                            mm = nc.tensor.matmul(dst, k_tok[:, j * HD:(j + 1) * HD], v_tok(u, j), start=False, stop=True)
                        mm.then_inc(s_made, 1)

                for u in range(UNITS + 1):
                    if u < UNITS:
                        all_grams(u)
                    for l in range(1, LEVELS):
                        if u < UNITS:
                            q_level(u, l)
                        if u:
                            carry(u - 1, l)
                        if u < UNITS:
                            g_level(u, l)

            @block.vector
            def _(dve):
                def take_grams(u):
                    G, Rb, Rk, Ak = held[u % 2]
                    if u >= 2:
                        dve.wait_ge(y_made, u - 1)
                    order = [(N_, 0, "lt"), (GT, 2, "pair0"), (Ak, 4, "lt"), (N_, 1, "lt"), (GT, 3, "pair0"), (Ak, 5, "lt"),
                             (Rb, 0, "le"), (Rb, 1, "le"), (Rk, 2, "le"), (Rk, 3, "le")]
                    for n, (dst, bank, m) in enumerate(order):
                        dve.wait_ge(grams, 10 * u + n + 1)
                        nc.vector.tensor_tensor(four(dst, bank % 2), bank4(bank), mat4(m), ALU.mult).then_inc(gram_moved, 1)

                def take_q(u, l):
                    for g in range(2):
                        n = 12 * u + 2 * (l - 1) + g
                        dve.wait_ge(q_made, n + 1)
                        if n >= 2:
                            dve.wait_ge(g_made, n - 1)
                        nc.vector.tensor_tensor(four(Q, g), bank4(g), mat4(f"pair{l}"), ALU.mult).then_inc(q_moved, 1)

                def take_g(u, l):
                    G = held[u % 2][0]
                    for g in range(2):
                        n = 12 * u + 2 * (l - 1) + g
                        dve.wait_ge(g_made, n + 1)
                        if l > 1:
                            dve.wait_ge(g_moved, n - 1)
                        if l < LEVELS - 1:
                            if l > 1:
                                dve.wait_ge(gt_moved, 10 * u + 2 * (l - 2) + g + 1)
                            nc.vector.tensor_tensor(four(GT, g), bank4(4 + g), four(GT, g), ALU.add).then_inc(gt_moved, 1)
                        nc.vector.tensor_tensor(four(G, g), bank4(2 + g), four(G, g), ALU.add).then_inc(g_moved, 1)

                def carry(u, step):
                    S = S_[u % 2]
                    if step == 2:
                        dve.wait_ge(w_made, u + 1)
                        nc.vector.tensor_copy(W_.rearrange("p (g w) -> p g w", g=2), PS[:, 6:8, 0:256]).then_inc(w_moved, 1)
                    elif step == 3:
                        dve.wait_ge(u_made, u + 1)
                        nc.vector.tensor_copy(U_, PS[:, 6, :]).then_inc(u_moved, 1)
                    elif step == 5 and has_next(u):
                        dve.wait_ge(s_made, u + 1)
                        nc.vector.tensor_tensor(S, S, PS[:, 6, 0:256], ALU.add).then_inc(s_moved, 1)
                        dve.wait_ge(s_moved, 2 * u + 1)
                        fv = fac.rearrange("p (a c) -> p a c", c=NB)[:, u % 2 * 4:u % 2 * 4 + 4, u // 2:u // 2 + 1].to_broadcast([P, 4, HD])
                        sv = S.rearrange("p (a v) -> p a v", a=4)
                        nc.vector.tensor_tensor(sv, sv, fv, ALU.mult).then_inc(s_moved, 1)

                for u in range(UNITS + 1):
                    if u < UNITS:
                        take_grams(u)
                    for l in range(1, LEVELS):
                        if u < UNITS:
                            take_q(u, l)
                        if u:
                            carry(u - 1, l)
                        if u < UNITS:
                            take_g(u, l)

            @block.gpsimd
            def _(pool):
                for u in range(UNITS):
                    G = held[u % 2][0]
                    for g in range(2):
                        pool.wait_ge(gram_moved, 10 * u + 3 * g + 2)
                        nc.gpsimd.tensor_tensor(four(G, g), four(N_, g), mat4("pair0_t"), ALU.mult).then_inc(start_made, 1)
                        nc.gpsimd.tensor_tensor(four(GT, g), four(GT, g), mat4("ident"), ALU.add).then_inc(start_made, 1)
                        pool.wait_ge(start_made, 6 * u + 3 * g + 2)
                        nc.gpsimd.tensor_tensor(four(G, g), four(G, g), mat4("ident"), ALU.add).then_inc(start_made, 1)

            @block.scalar
            def _(act):
                for u in range(UNITS):
                    half = slice(u % 2 * 4, u % 2 * 4 + 4)
                    if u:
                        act.wait_ge(s_made, min(u, UNITS - 2))
                    for n, (bank, dst) in enumerate(((6, v[:, half, span(u)]), (7, k_tok.rearrange("p (h l) -> p h l", h=4)),
                                                     (6, b_tok.rearrange("p (h l) -> p h l", h=4)))):
                        act.wait_ge(turned, 3 * u + n + 1)
                        nc.scalar.copy(dst, bank4(bank)).then_inc(turned_moved, 1)
                    act.wait_ge(y_made, u + 1)
                    nc.scalar.copy(rt[:, half, span(u)], bank4(7)).then_inc(y_moved, 1)
        checkpoint("wkv", ALL(r))

        yy, sq = r, tmp
        n1, n2, n3 = sem("gn_vec"), sem("gn_act"), sem("gn_sums")
        loads("selectors_loaded_again", [(of_heads, A["of_heads"]), (to_heads, A["to_heads"])])
        with nc.Block() as block:
            @block.tensor
            def _(pe):
                for i in range(8):
                    mm = nc.tensor.matmul(PS[:, i, :], mat("head_ones"), yy[:, i, :], start=True, stop=True).then_inc(n3, 1)
                for i in range(8):
                    pe.wait_ge(n2, i + 1)
                    mm = nc.tensor.matmul(PS[0:H, 0, :], of_heads[:, i * H:(i + 1) * H], sq[:, i, :], start=i == 0, stop=i == 7)
                mm.then_inc(n3, 1)
                pe.wait_ge(n1, 10)
                for i in range(8):
                    nc.tensor.matmul(PS[:, i, :], to_heads[:, i * P:(i + 1) * P], sums16, start=True, stop=True).then_inc(n3, 1)

            @block.vector
            def _(dve):
                for i in range(8):
                    dve.wait_ge(n3, i + 1)
                    nc.vector.scalar_tensor_tensor(out=yy[:, i, :], in0=PS[:, i, :], scalar=-1.0 / HD, in1=yy[:, i, :],
                                                   op0=ALU.mult, op1=ALU.add).then_inc(n1, 1)
                nc.vector.memset(small[:, 250:251], 64e-5).then_inc(n1, 1)
                dve.wait_ge(n2, 9)
                nc.vector.reciprocal(sums16, sums16).then_inc(n1, 1)
                for i in range(8):
                    dve.wait_ge(n3, 10 + i)
                    nc.vector.scalar_tensor_tensor(out=yy[:, i, :], in0=yy[:, i, :], scalar=col("lnx_g", i), in1=PS[:, i, :],
                                                   op0=ALU.mult, op1=ALU.mult).then_inc(n1, 1)
                    dve.wait_ge(n1, 11 + 2 * i)
                    nc.vector.scalar_tensor_tensor(out=yy[:, i, :], in0=yy[:, i, :], scalar=col("lnx_b", i), in1=bonus[:, i, :],
                                                   op0=ALU.add, op1=ALU.add).then_inc(n1, 1)

            @block.scalar
            def _(act):
                for i in range(8):
                    act.wait_ge(n1, i + 1)
                    nc.scalar.activation(sq[:, i, :], yy[:, i, :], ACT.Square, scale=HD ** -0.5).then_inc(n2, 1)
                act.wait_ge(n1, 9)
                act.wait_ge(n3, 9)
                nc.scalar.activation(sums16, PS[0:H, 0, :], ACT.Sqrt, bias=small[0:H, 250:251]).then_inc(n2, 1)

        differences(F[2])
        g2_ = [flat(F[4])[0:80, i * D:(i + 1) * D] for i in range(2)]
        hid_g = [flat(F[4])[0:80, 2 * D + i * T:2 * D + (i + 1) * T] for i in range(2)]
        loads("g2_loaded", [(g2_[0], A["w_g2"][0:80, :]), (g2_[1], A["w_g2"][80:160, :])])
        gemm("lora_g", 2, 8, rows(F[3]), {"act": lambda e, n, b: nc.scalar.activation(hid_g[n], b, ACT.Sigmoid)}, n_cols=80,
             prepare=mixed(F[3], F[2], 5))
        lora_out("gate7", [(g2_[0], hid_g[0]), (g2_[1], hid_g[1])],
                 {"dve": lambda e, n, b: nc.vector.tensor_tensor(yy[:, n, :], yy[:, n, :], b, ALU.mult)})

        def add_to_x(e, n, b):
            return nc.vector.scalar_tensor_tensor(out=x[:, n, :], in0=x[:, n, :], scalar=ALPHA, in1=b, op0=ALU.mult, op1=ALU.add)

        def layer_norm(layer, which):
            i0 = (2 * layer + which) * 8
            return norm_program(f"ln{layer}{which}", rows(x), 8, D, 1e-5, lambda i: col("ln_g", i0 + i), rows(x), centered=True,
                 bias=lambda i: col("ln_b", i0 + i), scratch=rows(F[3]))

        def ffn(layer):
            hid = lambda i: F[1 + i // 8][:, i % 8, :]
            tile_of = lambda n: n // 2 + n % 2 * FT
            ln, ln_ready = layer_norm(layer, 0)
            parts = open_split(f"up{layer}", 5, KT)
            run_stage(ln, conv_program(f"up{layer}", 2 * FT, None, 3,
                      lambda n, j: col("ffn_conv_w", (layer * 3 + j) * 2 * FT + tile_of(n)),
                      lambda n: col("ffn_conv_b", layer * 2 * FT + tile_of(n)),
                      lambda n: F[4][:, n // 2 % 2, :] if n % 2 else hid(n // 2), pair_out=hid, split=(*parts, rows(x), ln_ready)))
            split_gemm(f"down{layer}", FT, hid, {"dve": add_to_x})

        split_gemm("w_o", 8, rows(yy), {"dve": add_to_x})
        ffn(0)
        end_section()

        low = F[1]
        c_q, c_kv, k_idx = rows(low), low[:, 2, :], low[:, 3, :]
        ln, ln_ready = layer_norm(0, 1)
        run_stage(ln, gemm_program("d_in", 4, 8, rows(x), {"act": copy_act(rows(low))}, rhs_ready=ln_ready))
        w_idx = small[:, 144:176]
        w_idx_taken = sem("w_idx_taken")
        first = at["used"]
        with nc.Block() as block:
            @block.tensor
            def _(pe):
                w = next_chunk(pe)
                for b in range(NB):
                    for k in range(8):
                        mm = nc.tensor.matmul(PS[:, 0, b * 8:(b + 1) * 8], x[:, k, b * P:(b + 1) * P], w[:, k * 8:(k + 1) * 8], start=k == 0, stop=k == 7)
                mm.then_inc(weight_used, 1)

            @block.vector
            def _(dve):
                dve.wait_ge(weight_used, first + 1)
                nc.vector.tensor_scalar(w_idx, PS[:, 0, 0:32], 8 ** -0.5 * 64 ** -0.5, None, ALU.mult).then_inc(w_idx_taken, 1)

            @block.sync
            def _(sp):
                stream(sp)
        norm("norm_cq", c_q, 2, 256, 1e-6, lambda i: col("q_norm_g", i), c_q, scratch=rows(F[8]))
        norm("norm_ckv", lambda i: c_kv, 1, P, 1e-6, lambda i: col("kv_norm_g", 0), lambda i: c_kv, scratch=rows(F[8]))
        norm("norm_kidx", lambda i: k_idx, 1, P, 1e-5, lambda i: col("kidx_g", 0), lambda i: k_idx, centered=True,
             bias=lambda i: col("kidx_b", 0), scratch=rows(F[8]))
        qd, qi = F[2], F[3]
        gemm("d_uq", 8, 2, c_q, {"act": lambda e, n, b: nc.scalar.mul(qd[:, n, :], b, HD ** -0.5)})
        gemm("d_qidx", 4, 2, c_q, {"dve": copy_dve(rows(qi))})

        f8 = flat(F[8])
        uk, uv = f8[:, 0:1024], f8[:, 1024:2048]
        qabs = [f8[:, 2048 + i * T:2048 + (i + 1) * T] for i in range(2)]
        lg = [flat(F[3])[:, 1280 + i * SB_N:1280 + (i + 1) * SB_N] for i in range(2)]
        rb, oneh, band = flat(F[5])[0:32, 0:16], flat(F[5])[0:32, 512:512 + BAND], flat(F[5])[0:16, 2048:2048 + BAND]
        loads("dsa_loaded", [(rb, A["rel_bias"]), (oneh, A["bucket1h"]), (uk, A["d_uk"]), (uv, A["d_uv"])])
        band_dram = nc.dram_tensor("band", (H, BAND), f32, kind="Internal")
        toep = [F[6], F[7]]
        band_made, band_taken, band_stored, toep_loaded = sem("band_made"), sem("band_taken"), sem("band_stored"), sem("toeplitz_loaded")
        ckv_tok = aux[:, 0:T]
        tok_made, tok_taken = sem("ckv_tok_made"), sem("ckv_tok_taken")
        with nc.Block() as block:
            @block.tensor
            def _(pe):
                nc.tensor.matmul(PS[0:16, 0, :], rb, oneh[:, 0:T], start=True, stop=True)
                nc.tensor.matmul(PS[0:16, 1, 0:P], rb, oneh[:, T:BAND], start=True, stop=True).then_inc(band_made, 1)
                for b in range(NB):
                    mm = nc.tensor.transpose(PS[:, 2, b * P:(b + 1) * P], low[:, 2, b * P:(b + 1) * P], mat("ident"))
                mm.then_inc(tok_made, 1)

            @block.scalar
            def _(act):
                act.wait_ge(band_made, 1)
                nc.scalar.copy(band, PS[0:16, 0:2, :].rearrange("p a b -> p (a b)")[:, 0:BAND]).then_inc(band_taken, 1)
                act.wait_ge(tok_made, 1)
                nc.scalar.copy(ckv_tok, PS[:, 2, :]).then_inc(tok_taken, 1)

            @block.sync
            def _(sp):
                sp.wait_ge(band_taken, 1)
                sp.dma_start(band_dram.ap(), band).then_inc(band_stored, 16)
                sp.wait_ge(band_stored, 16)
                for i in range(2):
                    src = bass.AP(band_dram, i * 8 * BAND, [[1, P], [BAND, 8], [1, T]])
                    sp.dma_start(toep[i][:, :, :], src).then_inc(toep_loaded, 16)
                stream(sp)

        mask, left = F[4], lambda b: F[4][:, 4 + b, :]
        best = small[:, 176:208]
        rel = [F[5][:, i, :] for i in range(8)]
        sc_made, sc_relu, sc_added, select = sem("index_scores_made"), sem("index_relu"), sem("index_added"), sem("selected")
        with nc.Block() as block:
            @block.tensor
            def _(pe):
                for b in range(1, NB):
                    n = (b + 1) * P
                    for i in range(8):
                        half_p = slice(i % 2 * HD, (i % 2 + 1) * HD)
                        if b > 1:
                            pe.wait_ge(sc_relu, 8 * (b - 2) + i + 1)
                        nc.tensor.matmul(PS[:, i, 0:n], qi[half_p, i // 2, b * P:(b + 1) * P], low[half_p, 3, 0:n], start=True, stop=True).then_inc(sc_made, 1)

            @block.scalar
            def _(act):
                for b in range(1, NB):
                    n = (b + 1) * P
                    for i in range(8):
                        act.wait_ge(sc_made, 8 * (b - 1) + i + 1)
                        if b > 1:
                            act.wait_ge(sc_added, 9 * (b - 2) + i + 1)
                        nc.scalar.activation(rel[i][:, 0:n], PS[:, i, 0:n], ACT.Relu).then_inc(sc_relu, 1)

            @block.vector
            def _(dve):
                for b in range(1, NB):
                    n = (b + 1) * P
                    for i in range(8):
                        dve.wait_ge(sc_relu, 8 * (b - 1) + i + 1)
                        wcol = w_idx[:, b * 8 + i:b * 8 + i + 1]
                        if i == 0:
                            nc.vector.tensor_scalar(left(b)[:, 0:n], rel[i][:, 0:n], wcol, None, ALU.mult).then_inc(sc_added, 1)
                        else:
                            dve.wait_ge(sc_added, 9 * (b - 1) + i)
                            nc.vector.scalar_tensor_tensor(out=left(b)[:, 0:n], in0=rel[i][:, 0:n], scalar=wcol, in1=left(b)[:, 0:n],
                                                           op0=ALU.mult, op1=ALU.add).then_inc(sc_added, 1)
                    dve.wait_ge(sc_added, 9 * (b - 1) + 8)
                    nc.vector.tensor_tensor(left(b)[:, b * P:n], left(b)[:, b * P:n], mat("neg_after"), ALU.add).then_inc(sc_added, 1)
                dve.wait_ge(sc_added, 27)
                for k in range(TOPK // 8):
                    for b in range(1, NB):
                        if k:
                            dve.wait_ge(select, 6 * k - 3 + b)
                        nc.vector.max(out=best[:, 8 * b:8 * b + 8], in_=left(b)[:, 0:(b + 1) * P]).then_inc(select, 1)
                    for b in range(1, NB):
                        dve.wait_ge(select, 6 * k + b)
                        nc.vector.match_replace(out=left(b)[:, 0:(b + 1) * P], in_to_replace=best[:, 8 * b:8 * b + 8],
                                                in_values=left(b)[:, 0:(b + 1) * P], imm_value=TAKEN).then_inc(select, 1)
                dve.wait_ge(select, 6 * (TOPK // 8))
                for b in range(1, NB):
                    n = (b + 1) * P
                    nc.vector.tensor_scalar(mask[:, b, 0:n], left(b)[:, 0:n], TAKEN / 2, NEG, ALU.is_ge, ALU.mult).then_inc(select, 1)
                nc.vector.tensor_copy(mask[:, 0, 0:P], mat("neg_after")).then_inc(select, 1)

            @block.sync
            def _(sp):
                sp.wait_ge(toep_loaded, 32)

        LG_BANK = [(2, 0), (3, 0), (2, P), (4, 0)]
        L_AT = [0, P, 3 * P, 6 * P]
        att = F[5]
        pt_ = aux[:, T:T + SB_N]
        olat = aux[:, 1792:2304]
        mx, sm = small[:, 208:216], small[:, 216:224]
        nmx, rs = small[:, 224:232], small[:, 232:240]
        names = ["qabs_made", "qabs_moved", "logits_made", "masked", "negated", "exped", "inverted", "scaled", "turned",
                 "turned_moved", "olat_made", "olat_moved", "o_made", "o_moved"]
        (qa_made, qa_moved, lg_made, lg_masked, negated, exped, inverted, scaled, pt_made, pt_moved, ol_made, ol_moved,
         oo_made, oo_moved) = (sem("dsa_" + n) for n in names)
        with nc.Block() as block:
            @block.tensor
            def _(pe):
                def absorb(hh):
                    half_p = slice(hh % 2 * HD, (hh % 2 + 1) * HD)
                    if hh:
                        pe.wait_ge(qa_moved, hh)
                    if hh >= 4:
                        pe.wait_ge(oo_moved, hh - 3)
                    nc.tensor.matmul(PS[:, 0, :], uk[half_p, hh // 2 * P:(hh // 2 + 1) * P], qd[half_p, hh // 2, :], start=True, stop=True).then_inc(qa_made, 1)

                def logits(hh):
                    pe.wait_ge(qa_moved, hh + 1)
                    if hh:
                        pe.wait_ge(lg_masked, 4 * hh)
                    for b in range(NB):
                        n = (b + 1) * P
                        bank, at0 = LG_BANK[b]
                        dst = PS[:, bank, at0:at0 + n]
                        nc.tensor.matmul(dst, qabs[hh % 2][:, b * P:(b + 1) * P], low[:, 2, 0:n], start=True, stop=False)
                        mm = nc.tensor.matmul(dst, mat("flip"), toep[hh // 8][:, hh % 8, T - n:T], start=False, stop=True)
                    mm.then_inc(lg_made, 1)

                def turn(hh):
                    pe.wait_ge(scaled, 4 * hh + 4)
                    if hh:
                        pe.wait_ge(pt_moved, hh)
                    for i in range(NB):
                        for b in range(i, NB):
                            at0 = SB_AT[i] + (b - i) * P
                            mm = nc.tensor.transpose(PS[:, 5 + at0 // T, at0 % T:at0 % T + P], lg[hh % 2][:, L_AT[b] + i * P:L_AT[b] + (i + 1) * P], mat("ident"))
                    mm.then_inc(pt_made, 1)

                def latent(hh):
                    pe.wait_ge(pt_moved, hh + 1)
                    if hh:
                        pe.wait_ge(ol_moved, hh)
                    for i in range(NB):
                        mm = nc.tensor.matmul(PS[:, 1, i * P:T], ckv_tok[:, i * P:(i + 1) * P], pt_[:, SB_AT[i]:SB_AT[i] + SB_W[i]],
                                              start=i == 0, stop=i == NB - 1)
                    mm.then_inc(ol_made, 1)

                def values(hh):
                    pe.wait_ge(ol_moved, hh + 1)
                    pe.wait_ge(qa_moved, min(hh + 4, H))
                    half_p = slice(hh % 2 * HD, (hh % 2 + 1) * HD)
                    nc.tensor.matmul(PS[half_p, 0, :], uv[:, hh * HD:(hh + 1) * HD], olat, start=True, stop=True).then_inc(oo_made, 1)

                absorb(0)
                absorb(1)
                logits(0)
                for hh in range(H + 1):
                    if hh + 2 < H:
                        absorb(hh + 2)
                    if hh + 1 < H:
                        logits(hh + 1)
                    if hh < H:
                        turn(hh)
                    if hh:
                        values(hh - 1)
                    if hh < H:
                        latent(hh)

            @block.vector
            def _(dve):
                for hh in range(H):
                    p = hh % 2
                    dve.wait_ge(lg_made, hh + 1)
                    if hh >= 2:
                        dve.wait_ge(pt_made, hh - 1)
                    for b in range(NB):
                        n = (b + 1) * P
                        bank, at0 = LG_BANK[b]
                        nc.vector.tensor_tensor_reduce(out=lg[p][:, L_AT[b]:L_AT[b] + n], in0=PS[:, bank, at0:at0 + n], in1=mask[:, b, 0:n],
                                                       scale=1.0, scalar=-3e38, op0=ALU.add, op1=ALU.max,
                                                       accum_out=mx[:, 4 * p + b:4 * p + b + 1]).then_inc(lg_masked, 1)
                    dve.wait_ge(lg_masked, 4 * hh + 4)
                    nc.vector.tensor_scalar(nmx[:, 4 * p:4 * p + 4], mx[:, 4 * p:4 * p + 4], -1.0, None, ALU.mult).then_inc(negated, 1)
                    dve.wait_ge(exped, 4 * hh + 4)
                    nc.vector.reciprocal(rs[:, 4 * p:4 * p + 4], sm[:, 4 * p:4 * p + 4]).then_inc(inverted, 1)
                    dve.wait_ge(inverted, hh + 1)
                    for b in range(NB):
                        part = lg[p][:, L_AT[b]:L_AT[b] + (b + 1) * P]
                        nc.vector.tensor_scalar(part, part, rs[:, 4 * p + b:4 * p + b + 1], None, ALU.mult).then_inc(scaled, 1)

            @block.scalar
            def _(act):
                def absorbed(hh):
                    act.wait_ge(qa_made, hh + 1)
                    if hh >= 2:
                        act.wait_ge(lg_made, hh - 1)
                    nc.scalar.copy(qabs[hh % 2], PS[:, 0, :]).then_inc(qa_moved, 1)

                def exps(hh):
                    p = hh % 2
                    act.wait_ge(negated, hh + 1)
                    for b in range(NB):
                        part = lg[p][:, L_AT[b]:L_AT[b] + (b + 1) * P]
                        nc.scalar.activation(part, part, ACT.Exp, bias=nmx[:, 4 * p + b:4 * p + b + 1],
                                             accum_out=sm[:, 4 * p + b:4 * p + b + 1]).then_inc(exped, 1)
                absorbed(0)
                absorbed(1)
                exps(0)
                for hh in range(H + 1):
                    if hh + 2 < H:
                        absorbed(hh + 2)
                    if hh < H:
                        act.wait_ge(pt_made, hh + 1)
                        if hh:
                            act.wait_ge(ol_made, hh)
                        nc.scalar.copy(pt_, PS[:, 5:8, :].rearrange("p a b -> p (a b)")[:, 0:SB_N]).then_inc(pt_moved, 1)
                    if hh:
                        act.wait_ge(oo_made, hh)
                        half_p = slice((hh - 1) % 2 * HD, ((hh - 1) % 2 + 1) * HD)
                        nc.scalar.copy(att[half_p, (hh - 1) // 2, :], PS[half_p, 0, :]).then_inc(oo_moved, 1)
                    if hh + 1 < H:
                        exps(hh + 1)
                    if hh < H:
                        act.wait_ge(ol_made, hh + 1)
                        nc.scalar.copy(olat, PS[:, 1, :]).then_inc(ol_moved, 1)

        split_gemm("d_wo", 8, rows(att), {"dve": add_to_x})
        ffn(1)
        run_stage(layer_norm(1, 1)[0])
        checkpoint("x5", ALL(x))

        with nc.Block() as block:
            @block.sync
            def _(sp):
                sp.dma_start(out, ALL(x)).then_inc(stored, 16)
                sp.wait_ge(stored, 16)


def weight_tiles(w, n_cols=P):
    k, n = w.shape
    return np.ascontiguousarray(w.reshape(k // P, P, n // n_cols, n_cols).transpose(2, 1, 0, 3).reshape(n // n_cols, P, -1))


def weight_rows(w):
    return np.ascontiguousarray(w).reshape(-1, P, D)


def columns(v):
    return np.ascontiguousarray(v).reshape(-1, P).T


def lay_out(i):
    row = lambda v: np.broadcast_to(v.reshape(1, -1), (P, v.size))
    c = {"c": columns(i["c"]), "b_ada": columns(i["b_ada"]), "norm_in_gain": columns(i["norm_in_gain"]),
         "conv_w": columns(i["conv_w"][0]), "conv_b": columns(i["conv_b"]), "d_skip": columns(np.repeat(i["d_skip"], HD)),
         "sb_norm_gain": columns(i["sb_norm_gain"]), "ssm_norm_gain": columns(i["ssm_norm_gain"]),
         "norm_f_gain": columns(i["norm_f_gain"]), "dt_bias": row(i["dt_bias"]), "a_log": row(i["a_log"]),
         "ln_g": columns(i["ln_g_2"]), "ln_b": columns(i["ln_b_2"]), "mix": columns(i["rwkv_mix_2"]),
         "w0": columns(i["rwkv_w0_2"]), "a0": columns(i["rwkv_a0_2"]), "k_k": columns(i["rwkv_k_k_2"]),
         "k_a": columns(i["rwkv_k_a_2"]), "r_k": columns(i["rwkv_r_k_2"]), "lnx_g": columns(i["rwkv_lnx_g_2"]),
         "lnx_b": columns(i["rwkv_lnx_b_2"]), "q_norm_g": columns(i["dsa_q_norm_g_2"]),
         "kv_norm_g": columns(i["dsa_kv_norm_g_2"]), "kidx_g": columns(np.tile(i["dsa_kidx_g_2"][0], 2)),
         "kidx_b": columns(np.tile(i["dsa_kidx_b_2"][0], 2)),
         "ffn_conv_w": columns(i["ffn_conv_w_2"]), "ffn_conv_b": columns(i["ffn_conv_b_2"])}
    w_in = i["w_in"][0]
    d_in = i["dsa_w_in_2"][0]
    at = D_XBC0 = 4096 + 1536
    a = {"xT": np.ascontiguousarray(i["x"][0].T.reshape(KT, P, T).transpose(1, 0, 2)),
         "cols": np.ascontiguousarray(np.concatenate([c[n] for n, _ in COLS], axis=1)),
         "squares": square_constants(), "late": late_constant(), "bucket1h": bucket_constant(),
         "w_ada": weight_tiles(i["w_ada"][0]),
         "w_q": weight_rows(w_in[:, :D]), "w_k": weight_rows(w_in[:, D:2 * D]),
         "w_in": weight_tiles(w_in[:, 2 * D:at]), "w_z": weight_rows(w_in[:, at + 16:]),
         "w_dt": weight_tiles(w_in[:, at:at + 16], 16), "w_out": weight_tiles(i["w_out"][0]),
         "w_rkv": weight_rows(i["rwkv_w_rkv_2"][0]),
         "w_w1": weight_tiles(i["rwkv_w1_2"][0], 64), "w_a1": weight_tiles(i["rwkv_a1_2"][0], 64),
         "w_g1": weight_tiles(i["rwkv_g1_2"][0], 80), "w_w2": i["rwkv_w2_2"][0], "w_a2": i["rwkv_a2_2"][0],
         "w_g2": i["rwkv_g2_2"][0], "w_o": weight_rows(i["rwkv_w_o_2"][0]),
         "d_in": weight_tiles(np.concatenate([d_in[:, :384], d_in[:, 384:448], d_in[:, 384:448]], axis=1)),
         "d_widx": weight_tiles(d_in[:, 448:456], 8),
         "d_uq": weight_tiles(i["dsa_w_uq_2"][0]), "d_uk": i["dsa_w_uk_2"][0].reshape(H // 2, P, P).transpose(1, 0, 2).reshape(P, -1),
         "d_uv": i["dsa_w_uv_2"][0].transpose(1, 0, 2).reshape(P, -1), "d_qidx": weight_tiles(i["dsa_w_qidx_2"][0]),
         "d_wo": weight_rows(i["dsa_w_o_2"][0]), "rel_bias": i["rel_bias_2"]}
    a["of_heads"], a["to_heads"] = head_selectors()
    for l in range(2):
        a[f"up{l}"] = weight_tiles(i["ffn_w_up_2"][l])
        a[f"down{l}"] = weight_rows(i["ffn_w_down_2"][l])
    return {n: np.ascontiguousarray(v) for n, v in a.items()}


def kernel(**inputs):
    import concourse.bacc as bacc
    from concourse.bass_utils import run_bass_kernel_spmd

    arrays = lay_out({n: np.asarray(v) for n, v in inputs.items()})
    nc = bacc.Bacc("TRN2", target_bir_lowering=False, num_devices=1)
    dram = {n: nc.dram_tensor("in_" + n, a.shape, mybir.dt.float32, kind="ExternalInput").ap() for n, a in arrays.items()}
    out = nc.dram_tensor("out", (P, KT, T), mybir.dt.float32, kind="ExternalOutput").ap()
    program(nc, dram, out)
    r = run_bass_kernel_spmd(nc, [{"in_" + n: a for n, a in arrays.items()}], core_ids=[0])
    got = r.results[0]["out"]
    return np.ascontiguousarray(got.transpose(1, 0, 2).reshape(D, T).T).reshape(1, T, D)
```
